# Optimizing a Trainium2 kernel written in Bass

```python
import jax, jax.numpy as jnp
from jax import lax
import numpy as np

D_MODEL = 1024
BATCH = 1
SEQ = 256
DEPTH = 2

CHUNK = 64
N_A_LAYERS = DEPTH // 2
N_B_LAYERS = DEPTH - N_A_LAYERS

M_HEADS = 4
M_QK_DIM = D_MODEL // (2 * M_HEADS)
M_V_DIM = D_MODEL // M_HEADS
M_QK_WIDTH = M_HEADS * M_QK_DIM
M_V_WIDTH = M_HEADS * M_V_DIM
M_IN_WIDTH = 2 * M_QK_WIDTH + 2 * M_V_WIDTH + 2 * M_HEADS
GATE_SOFTCAP = 15.0
MH_NORM_EPS = 1e-6

A_HEADS = 16
A_KV_HEADS = 4
A_HEAD_DIM = D_MODEL // A_HEADS
A_GROUP = A_HEADS // A_KV_HEADS
A_KV_WIDTH = A_KV_HEADS * A_HEAD_DIM
WINDOW = 128
WINDOW_CHUNKS = WINDOW // CHUNK
ROPE_THETA = 10000.0

N_EXPERTS = 16
N_GROUPS = 4
EXPERTS_PER_GROUP = N_EXPERTS // N_GROUPS
TOP_K = 2
D_FF_EXPERT = D_MODEL // 2

DN_ALPHA = (2.0 * DEPTH) ** 0.25
DN_BETA = (8.0 * DEPTH) ** -0.25
LN_EPS = 1e-5

kernel_name = 'yoco_mlstm_swa_sink_grouped_moe_deepnorm'

def _layer_norm(x, g, b):
    xf = x.astype(jnp.float32)
    mu = xf.mean(-1, keepdims=True)
    var = jnp.square(xf - mu).mean(-1, keepdims=True)
    y = (xf - mu) * lax.rsqrt(var + LN_EPS) * g.astype(jnp.float32) + b.astype(jnp.float32)
    return y.astype(x.dtype)

def _rope_tables(seq_len):
    inv_freq = ROPE_THETA ** (-jnp.arange(0, A_HEAD_DIM, 2, dtype=jnp.float32) / A_HEAD_DIM)
    ang = jnp.arange(seq_len, dtype=jnp.float32)[:, None] * inv_freq[None, :]
    return jnp.cos(ang), jnp.sin(ang)

def _rope(x, cos, sin):
    x1, x2 = jnp.split(x, 2, axis=-1)
    c = cos[None, :, None, :].astype(x.dtype)
    s = sin[None, :, None, :].astype(x.dtype)
    return jnp.concatenate([x1 * c - x2 * s, x2 * c + x1 * s], axis=-1)

def _mlstm_chunk_step(carry, inp):
    C, n, m = carry
    q, k, v, logi, logf = inp
    L = q.shape[-2]
    tri = jnp.tril(jnp.ones((L, L), dtype=bool))
    b = jnp.cumsum(logf, axis=-1)
    d = jnp.where(tri, b[..., :, None] - b[..., None, :] + logi[..., None, :], -jnp.inf)
    m_inter = b + m[..., None]
    m_t = jnp.maximum(m_inter, d.max(-1))
    s = jnp.einsum('bhjd,bhsd->bhjs', q, k) * jnp.exp(d - m_t[..., None])
    w_inter = jnp.exp(m_inter - m_t)
    num = jnp.einsum('bhjs,bhsv->bhjv', s, v) + w_inter[..., None] * jnp.einsum('bhvd,bhjd->bhjv', C, q)
    den = s.sum(-1) + w_inter * jnp.einsum('bhd,bhjd->bhj', n, q)
    h = num / jnp.maximum(jnp.abs(den), jnp.exp(-m_t))[..., None]
    b_last = b[..., -1]
    g = b_last[..., None] - b + logi
    m_new = jnp.maximum(b_last + m, g.max(-1))
    wk = jnp.exp(g - m_new[..., None])
    decay = jnp.exp(b_last + m - m_new)
    C_new = decay[..., None, None] * C + jnp.einsum('bhsv,bhsd->bhvd', v * wk[..., None], k)
    n_new = decay[..., None] * n + jnp.einsum('bhs,bhsd->bhd', wk, k)
    return (C_new, n_new, m_new), h

def _mlstm_mixer(x, w_in, b_gates, mh_norm_g, w_out):
    B, S, _ = x.shape
    nc = S // CHUNK
    proj = x @ w_in
    q, k, v, o, gates = jnp.split(
        proj, [M_QK_WIDTH, 2 * M_QK_WIDTH, 2 * M_QK_WIDTH + M_V_WIDTH, 2 * M_QK_WIDTH + 2 * M_V_WIDTH], axis=-1)
    gates = gates.astype(jnp.float32) + b_gates.astype(jnp.float32)
    gates = GATE_SOFTCAP * jnp.tanh(gates / GATE_SOFTCAP)
    logi = gates[..., :M_HEADS]
    logf = jax.nn.log_sigmoid(gates[..., M_HEADS:])

    def to_chunks(t, hd):
        return t.astype(jnp.float32).reshape(B, nc, CHUNK, M_HEADS, hd).transpose(1, 0, 3, 2, 4)

    def gate_chunks(t):
        return t.reshape(B, nc, CHUNK, M_HEADS).transpose(1, 0, 3, 2)

    qc = to_chunks(q, M_QK_DIM)
    kc = to_chunks(k, M_QK_DIM) * (M_QK_DIM ** -0.5)
    vc = to_chunks(v, M_V_DIM)
    init = (jnp.zeros((B, M_HEADS, M_V_DIM, M_QK_DIM), jnp.float32),
            jnp.zeros((B, M_HEADS, M_QK_DIM), jnp.float32),
            jnp.zeros((B, M_HEADS), jnp.float32))
    _, h = lax.scan(_mlstm_chunk_step, init, (qc, kc, vc, gate_chunks(logi), gate_chunks(logf)))
    h = h.transpose(1, 0, 3, 2, 4).reshape(B, S, M_HEADS, M_V_DIM)
    h = h * lax.rsqrt(jnp.mean(jnp.square(h), -1, keepdims=True) + MH_NORM_EPS)
    h = h.reshape(B, S, M_V_WIDTH) * mh_norm_g.astype(jnp.float32)
    h = (h * jax.nn.sigmoid(o.astype(jnp.float32))).astype(x.dtype)
    return h @ w_out

def _shared_kv(x, w_kv, cos, sin):
    B, S, _ = x.shape
    k, v = jnp.split(x @ w_kv, 2, axis=-1)
    k = _rope(k.reshape(B, S, A_KV_HEADS, A_HEAD_DIM), cos, sin)
    v = v.reshape(B, S, A_KV_HEADS, A_HEAD_DIM)
    return k, v

def _shift_chunks(t, w):
    if w == 0:
        return t
    pad = [(0, 0)] * t.ndim
    pad[1] = (w, 0)
    return jnp.pad(t, pad)[:, :-w]

def _swa_sink_mixer(x, k_sh, v_sh, w_q, sinks, w_out, cos, sin):
    B, S, _ = x.shape
    nc = S // CHUNK
    q = _rope((x @ w_q).reshape(B, S, A_HEADS, A_HEAD_DIM), cos, sin)
    qc = q.reshape(B, nc, CHUNK, A_KV_HEADS, A_GROUP, A_HEAD_DIM)
    kc = k_sh.reshape(B, nc, CHUNK, A_KV_HEADS, A_HEAD_DIM)
    vc = v_sh.reshape(B, nc, CHUNK, A_KV_HEADS, A_HEAD_DIM)
    offsets = list(range(WINDOW_CHUNKS - 1, -1, -1))
    kb = jnp.concatenate([_shift_chunks(kc, w) for w in offsets], axis=2)
    vb = jnp.concatenate([_shift_chunks(vc, w) for w in offsets], axis=2)
    key_off = jnp.repeat(jnp.array(offsets, dtype=jnp.int32), CHUNK)
    valid = (jnp.arange(nc, dtype=jnp.int32)[:, None] - key_off[None, :]) >= 0
    s = jnp.einsum('bcqhgd,bckhd->bchgqk', qc, kb).astype(jnp.float32) * (A_HEAD_DIM ** -0.5)
    s = jnp.where(valid[None, :, None, None, None, :], s, -jnp.inf)
    sink = sinks.astype(jnp.float32).reshape(1, 1, A_KV_HEADS, A_GROUP, 1, 1)
    mx = jnp.maximum(s.max(-1, keepdims=True), sink)
    p = jnp.exp(s - mx)
    p = p / (p.sum(-1, keepdims=True) + jnp.exp(sink - mx))
    out = jnp.einsum('bchgqk,bckhd->bcqhgd', p.astype(vb.dtype), vb).reshape(B, S, D_MODEL)
    return out @ w_out

def _grouped_moe(x, w_router, b_router, w_gu, w_down):
    B, S, D = x.shape
    t = x.reshape(B * S, D)
    probs = jax.nn.softmax((t @ w_router).astype(jnp.float32), axis=-1)
    sel = (probs + b_router.astype(jnp.float32)).reshape(-1, N_GROUPS, EXPERTS_PER_GROUP)
    group_score = lax.top_k(sel, TOP_K)[0].sum(-1)
    best_group = jnp.argmax(group_score, axis=-1)
    in_group = jnp.take_along_axis(sel, best_group[:, None, None], axis=1)[:, 0]
    _, local = lax.top_k(in_group, TOP_K)
    idx = best_group[:, None] * EXPERTS_PER_GROUP + local
    w = jnp.take_along_axis(probs, idx, axis=-1)
    w = w / w.sum(-1, keepdims=True)
    gate = (jax.nn.one_hot(idx, N_EXPERTS, dtype=jnp.float32) * w[..., None]).sum(1)
    out = jnp.zeros_like(t)
    for e in range(N_EXPERTS):
        g, u = jnp.split(t @ w_gu[e], 2, axis=-1)
        y = (jax.nn.silu(g) * u) @ w_down[e]
        out = out + gate[:, e:e + 1].astype(y.dtype) * y
    return out.reshape(B, S, D)

def setup_inputs(seed: int = 0) -> dict:
    key = jax.random.key(seed)
    ks = jax.random.split(key, 20)
    f32 = jnp.float32
    sd = D_MODEL ** -0.5
    x = jax.random.normal(ks[0], (BATCH, SEQ, D_MODEL), f32)
    w_in_a = jnp.concatenate([
        jax.random.normal(ks[1], (N_A_LAYERS, D_MODEL, 2 * M_QK_WIDTH), f32) * sd,
        jax.random.normal(ks[2], (N_A_LAYERS, D_MODEL, M_V_WIDTH), f32) * sd * DN_BETA,
        jax.random.normal(ks[3], (N_A_LAYERS, D_MODEL, M_V_WIDTH), f32) * sd,
        jax.random.normal(ks[4], (N_A_LAYERS, D_MODEL, 2 * M_HEADS), f32) * sd * 0.5,
    ], axis=-1)
    b_i = 0.1 * jax.random.normal(ks[5], (N_A_LAYERS, M_HEADS), f32)
    b_f = jnp.linspace(3.0, 6.0, M_HEADS, dtype=f32)[None, :] + 0.1 * jax.random.normal(ks[6], (N_A_LAYERS, M_HEADS), f32)
    b_gates_a = jnp.concatenate([b_i, b_f], axis=-1)
    mh_norm_a = 1.0 + 0.02 * jax.random.normal(ks[7], (N_A_LAYERS, M_V_WIDTH), f32)
    w_out_a = jax.random.normal(ks[8], (N_A_LAYERS, M_V_WIDTH, D_MODEL), f32) * (M_V_WIDTH ** -0.5) * DN_BETA
    w_kv_shared = jnp.concatenate([
        jax.random.normal(ks[9], (D_MODEL, A_KV_WIDTH), f32) * sd,
        jax.random.normal(ks[10], (D_MODEL, A_KV_WIDTH), f32) * sd * DN_BETA,
    ], axis=-1)
    w_q_b = jax.random.normal(ks[11], (N_B_LAYERS, D_MODEL, D_MODEL), f32) * sd
    sinks_b = 0.5 * jax.random.normal(ks[12], (N_B_LAYERS, A_HEADS), f32)
    w_out_b = jax.random.normal(ks[13], (N_B_LAYERS, D_MODEL, D_MODEL), f32) * sd * DN_BETA
    w_router = jax.random.normal(ks[14], (D_MODEL, N_EXPERTS), f32) * sd
    b_router = 0.01 * jax.random.normal(ks[15], (N_EXPERTS,), f32)
    w_gu = jax.random.normal(ks[16], (DEPTH, N_EXPERTS, D_MODEL, 2 * D_FF_EXPERT), f32) * sd
    w_down = jax.random.normal(ks[17], (DEPTH, N_EXPERTS, D_FF_EXPERT, D_MODEL), f32) * (D_FF_EXPERT ** -0.5) * DN_BETA
    ln_g = 1.0 + 0.02 * jax.random.normal(ks[18], (DEPTH, 2, D_MODEL), f32)
    ln_b = 0.02 * jax.random.normal(ks[19], (DEPTH, 2, D_MODEL), f32)
    return {'x': x, 'w_in_a': w_in_a, 'b_gates_a': b_gates_a, 'mh_norm_a': mh_norm_a, 'w_out_a': w_out_a,
            'w_kv_shared': w_kv_shared, 'w_q_b': w_q_b, 'sinks_b': sinks_b, 'w_out_b': w_out_b,
            'w_router': w_router, 'b_router': b_router, 'w_gu': w_gu, 'w_down': w_down,
            'ln_g': ln_g, 'ln_b': ln_b}

def reference(x, w_in_a, b_gates_a, mh_norm_a, w_out_a, w_kv_shared, w_q_b, sinks_b, w_out_b,
              w_router, b_router, w_gu, w_down, ln_g, ln_b):
    cos, sin = _rope_tables(x.shape[1])
    h = x
    k_sh = v_sh = None
    for layer in range(DEPTH):
        if layer < N_A_LAYERS:
            mix = _mlstm_mixer(h, w_in_a[layer], b_gates_a[layer], mh_norm_a[layer], w_out_a[layer])
        else:
            if layer == N_A_LAYERS:
                k_sh, v_sh = _shared_kv(h, w_kv_shared, cos, sin)
            j = layer - N_A_LAYERS
            mix = _swa_sink_mixer(h, k_sh, v_sh, w_q_b[j], sinks_b[j], w_out_b[j], cos, sin)
        h = _layer_norm(DN_ALPHA * h + mix, ln_g[layer, 0], ln_b[layer, 0])
        ffn = _grouped_moe(h, w_router, b_router, w_gu[layer], w_down[layer])
        h = _layer_norm(DN_ALPHA * h + ffn, ln_g[layer, 1], ln_b[layer, 1])
    return h


_drawn_inputs = setup_inputs


def setup_inputs(seed=0):
    import zlib

    import numpy as np

    out = dict(_drawn_inputs(seed))
    spreads = {}
    factors = {'mh_norm_a': 3.959, 'sinks_b': 62.136}
    for name, (base, spread) in spreads.items():
        noise = np.random.default_rng([zlib.crc32(name.encode()), seed]).standard_normal(out[name].shape)
        drawn = base * np.exp(spread * noise) if base else spread * noise
        out[name] = __import__('jax').numpy.asarray(drawn.astype(out[name].dtype))
    for name, factor in factors.items():
        out[name] = (out[name] * factor).astype(out[name].dtype)
    return out
```

```python
import concourse.bass as bass
from concourse import mybir
from contextlib import ExitStack

F32 = mybir.dt.float32
I32 = mybir.dt.int32
ACT = mybir.ActivationFunctionType
ALU = mybir.AluOpType
AX_X = mybir.AxisListType.X

SEQ, D = 256, 1024
P = 128
NT = SEQ // P
KC = D // P
HALF = 512
M_HEADS, M_V = 4, 256
M_QK = 128
QK_W, V_W = M_HEADS * M_QK, M_HEADS * M_V
A_HEADS, A_KV, DH, CHUNK = 16, 4, 64, 64
PAIRS = A_HEADS // 2
KV_W = A_KV * DH
EXPERTS, GROUPS, FF = 16, 4, 512
PER_GROUP = EXPERTS // GROUPS
FC = FF // P
SLOTS = 64
USED = 64
START = 1
U = 4
TURNS = EXPERTS // U
ALPHA = 4.0 ** 0.25
CAP = 15.0
LN_EPS, MH_EPS = 1e-5, 1e-6
LOW = -1.0e30
NG, ND = 4, 2
G_MIX = [0, 20]
G_EXP = [4, 22]
D_EXP = [0, 17]
D_KV = 16


def build(nc, x, w_in_a, b_gates_a, mh_norm_a, w_out_a, w_kv_shared, w_q_b, sinks_b, w_out_b,
          w_router, b_router, w_gu, w_down, ln_g, ln_b, rope, out):
    ctx = ExitStack()
    with ctx:
        def sb(name, shape, dt=F32):
            return ctx.enter_context(nc.sbuf_tensor(name, shape, dt))

        def sem(name):
            return ctx.enter_context(nc.semaphore(name))

        big = [sb(f"big{n}", [P, KC, D]) for n in range(NG)]
        small = [sb(f"small{n}", [P, FC, D]) for n in range(ND)]
        ident = sb("ident", [P, P])
        tri = sb("tri", [P, P])
        ones = sb("ones", [P, 1])
        zero = sb("zero", [P, 1])
        slot_no = sb("slot_no", [P, SLOTS])
        rank16 = sb("rank16", [P, EXPERTS])
        rank4 = rank16[:, EXPERTS - GROUPS:EXPERTS]
        rows = sb("rows", [9, D])
        h = sb("h", [P, NT, D])
        hT = sb("hT", [P, KC, SEQ])
        bufA = sb("bufA", [P, 2048])
        bufB = sb("bufB", [P, 2048])
        bufC = sb("bufC", [P, 1536])
        v_shift = sb("v_shift", [P, NT, KV_W])
        w_gate = sb("w_gate", [P, KC, 2 * M_HEADS])
        w_rt = sb("w_rt", [P, KC, EXPERTS])
        b_rt = sb("b_rt", [P, EXPERTS])
        sink = sb("sink", [P, A_HEADS])
        b_gate = sb("b_gate", [M_HEADS, 2])
        cs = sb("cs", [P, NT, DH])
        st = sb("st", [P, 160])

        qkT = bufA[:, :].rearrange("p (g n) -> p g n", g=8)
        gate_o = bufA[:, :].rearrange("p (t n) -> p t n", t=NT)
        val = bufB[:, :].rearrange("p (t n) -> p t n", t=NT)
        wts = bufC[:, :].rearrange("p (h n) -> p h n", h=M_HEADS)
        lane = [bufC[0:M_HEADS, n * SEQ:(n + 1) * SEQ] for n in range(6)]
        kdup = bufB[:, 0:1024].rearrange("p (t g d n) -> p t g d n", t=NT, g=A_KV, d=2)
        q_rot = gate_o
        qT = bufB[:, :].rearrange("p (j n) -> p j n", j=PAIRS)
        kT = bufC[:, 0:1024].rearrange("p (g n) -> p g n", g=A_KV)
        v_tok = bufC[:, 1024:1536].rearrange("p (t n) -> p t n", t=NT)
        prob = [bufA[:, n * 512:(n + 1) * 512] for n in range(2)]
        probT = [bufA[:, 1024 + n * 512:1024 + (n + 1) * 512] for n in range(2)]
        res = gate_o
        xe = [bufB[:, n * 512:(n + 1) * 512].rearrange("p (k s) -> p k s", k=KC) for n in range(2)]
        ye = [bufB[:, 1024 + n * 512:1024 + (n + 1) * 512] for n in range(2)]
        pick = [bufC[:, n * 128:(n + 1) * 128].rearrange("p (t s) -> p t s", t=NT) for n in range(2)]
        pickg = [bufC[:, 256 + n * 256:256 + (n + 1) * 256].rearrange("p (t d s) -> p t d s", t=NT, d=2)
                 for n in range(2)]
        act_g = [bufC[:, 768 + n * 256:768 + (n + 1) * 256] for n in range(2)]
        back = [v_shift[:, n, :] for n in range(2)]
        heT = bufC[:, 1280:1536]
        spill_w = hT[:, 0:4, :].rearrange("p k n -> p (k n)")

        r_logit = st[:, 0:32]
        r_prob = st[:, 32:64].rearrange("p (t e) -> p t e", t=NT)
        r_sel = st[:, 64:96].rearrange("p (t e) -> p t e", t=NT)
        r_a = st[:, 96:128].rearrange("p (t e) -> p t e", t=NT)
        r_s = st[:, 128:160]
        ro = bufC[:, 1280:1376].rearrange("p (a n) -> p a n", a=3)
        oh1 = ro[:, 0, :].rearrange("p (t e) -> p t e", t=NT)
        oh2 = ro[:, 1, :].rearrange("p (t e) -> p t e", t=NT)
        oh = ro[:, 2, :].rearrange("p (t e) -> p t e", t=NT)
        pos = sb("pos", [P, EXPERTS, NT])
        gate = sb("gate", [P, EXPERTS, NT])
        extra_f = sb("extra_f", [P, 4])
        extra = sb("extra", [P, 1], I32)
        ln = st[:, 0:40].rearrange("p (t n) -> p t n", t=NT)

        pb = [ctx.enter_context(nc.psum_tensor(f"pb{n}", [P, HALF], F32)) for n in range(8)]

        big_in = [[sem(f"big_in{n}_{q}") for q in range(4)] for n in range(NG)]
        small_in = [[sem(f"small_in{n}_{q}") for q in range(2)] for n in range(ND)]
        big_used, small_used = sem("big_used"), sem("small_used")
        x_in, gates_w_in, params_in = sem("x_in"), sem("gates_w_in"), sem("params_in")
        consts = sem("consts")
        turned = sem("turned")
        hT_dve, hT_act = sem("hT_dve"), sem("hT_act")
        qk_done, qk_sb = sem("qk_done"), sem("qk_sb")
        gates_done, gates_read = sem("gates_done"), sem("gates_read")
        v_done, v_sb = sem("v_done"), sem("v_sb")
        lanes_ready = sem("lanes_ready")
        small_T, small_sb = sem("small_T"), sem("small_sb")
        m_bcast, s_done = sem("m_bcast"), sem("s_done")
        w_arg, w_exp, w_masked, p_ready = sem("w_arg"), sem("w_exp"), sem("w_masked"), sem("p_ready")
        o_done, o_sb, mh_bcast = sem("o_done"), sem("o_sb"), sem("mh_bcast")
        den_done, den_inv = sem("den_done"), sem("den_inv")
        num_done, sq_done, hn_ready = sem("num_done"), sem("sq_done"), sem("hn_ready")
        a2d, d2a = sem("a2d"), sem("d2a")
        mix_done = sem("mix_done")
        ln_rows, ln_std_in, ln_std, ln_scale, ln_norm, ln_ready = (
            sem("ln_rows"), sem("ln_std_in"), sem("ln_std"), sem("ln_scale"), sem("ln_norm"), sem("ln_ready"))
        logits, rt_exp_in, rt_exp, chosen, placed, lists = (
            sem("logits"), sem("rt_exp_in"), sem("rt_exp"), sem("chosen"), sem("placed"), sem("lists"))
        pick_ready, pickg_ready = sem("pick_ready"), sem("pickg_ready")
        x_got, x_sb = sem("x_got"), sem("x_sb")
        gu_done, silu_done, he_ready = sem("gu_done"), sem("silu_done"), sem("he_ready")
        heT_done, heT_sb, back_sb = sem("heT_done"), sem("heT_sb"), sem("back_sb")
        y_done, y_sb, sent = sem("y_done"), sem("y_sb"), sem("sent")
        ov = [{n: sem(f"ov{l}_{n}") for n in ("w_in", "w_used", "pick", "x", "xs", "gu", "silu", "he", "t",
                                               "ts", "y", "ys", "z", "zs", "dve")} for l in range(2)]
        res_ready = sem("res_ready")
        kv_done, v_split, k_rot, q_done, q_rotd, kT_done, kT_sb, qT_done, qT_sb, q_moved = (
            sem("kv_done"), sem("v_split"), sem("k_rot"), sem("q_done"), sem("q_rotd"), sem("kT_done"),
            sem("kT_sb"), sem("qT_done"), sem("qT_sb"), sem("q_moved"))
        sc_done, mx_ready, e_done, es_done, pn_ready, pT_done, pT_sb, pv_done, outT_sb = (
            sem("sc_done"), sem("mx_ready"), sem("e_done"), sem("es_done"), sem("pn_ready"), sem("pT_done"),
            sem("pT_sb"), sem("pv_done"), sem("outT_sb"))
        shift_zero = sem("shift_zero")
        dch, ach = sem("dch"), sem("ach")
        stored = sem("stored")

        block = ctx.enter_context(nc.Block())

        def big_at(n):
            return big[n % NG], big_in[n % NG], n // NG + 1

        def small_at(n):
            return small[n % ND], small_in[n % ND], n // ND + 1

        SCB = [[[2, 3], [4, 5]], [[0, 1], [6, 7]]]
        SC_ORDER = [(t, par, jj) for t in range(NT) for jj in range(2) for par in range(2)]

        @block.sync
        def _(sp):
            def load_big(n, src, wait=None):
                buf, sems, _ = big_at(n)
                sp.wait_ge(big_used, n + 1 if wait is None else wait)
                v = src.rearrange("(k p) n -> p k n", p=P)
                for q in range(4):
                    sp.dma_start(buf[:, 2 * q:2 * q + 2, :], v[:, 2 * q:2 * q + 2, :]).then_inc(sems[q], 16)

            def load_small(n, src, wait=None):
                buf, sems, _ = small_at(n)
                sp.wait_ge(small_used, n + 1 if wait is None else wait)
                v = src.rearrange("(k p) n -> p k n", p=P)
                for q in range(2):
                    sp.dma_start(buf[:, 2 * q:2 * q + 2, :], v[:, 2 * q:2 * q + 2, :]).then_inc(sems[q], 16)

            w_in = w_in_a[0]
            for q in range(4):
                sp.dma_start(big[0][:, :, q * 256:(q + 1) * 256],
                             w_in[:, q * 256:(q + 1) * 256].rearrange("(k p) n -> p k n", p=P)
                             ).then_inc(big_in[0][q], 16)
            load_big(1, w_in[:, 1024:2048])
            load_big(2, w_in[:, 2048:3072])
            load_big(3, w_out_a[0])
            for l in range(2):
                G0, D0 = G_EXP[l], D_EXP[l]
                if l == 1:
                    sp.wait_ge(small_used, D_KV + 1)
                    v = w_kv_shared.rearrange("(k p) n -> p k n", p=P)
                    buf, sems, _ = small_at(D_KV)
                    bv = buf[:, :, :].rearrange("p a (b n) -> p (a b) n", b=2)
                    for q in range(2):
                        sp.dma_start(bv[:, 4 * q:4 * q + 4, :], v[:, 4 * q:4 * q + 4, :]).then_inc(sems[q], 16)
                    load_big(G_MIX[1] + 1, w_out_b[0])
                for e in range(2):
                    load_big(G0 + e, w_gu[l, e])
                with sp.Fori(0, TURNS - 1) as i:
                    for u in range(U):
                        n = D0 + u
                        load_small(n, w_down[l, bass.ds(i * U + u, 1)].rearrange("a k n -> (a k) n"), i * U + (n + 1))
                        m = G0 + u + 2
                        load_big(m, w_gu[l, bass.ds(i * U + (u + 2), 1)].rearrange("a k n -> (a k) n"),
                                 i * U + (m + 1))
                for e in range(EXPERTS - U, EXPERTS):
                    load_small(D0 + e, w_down[l, e])
                    m = e + 2
                    if m < EXPERTS:
                        load_big(G0 + m, w_gu[l, m])
                    elif m == EXPERTS and l == 0:
                        load_big(G_MIX[1], w_q_b[0])
                s = ov[l]
                sp.wait_ge(lists, l + 1)
                sp.wait_ge(res_ready, 4 * (l + 1))
                rounds = sp.value_load(extra[0:1, 0:1], min_val=0, max_val=3)
                with sp.If(rounds > 0):
                    with sp.Fori(0, rounds) as j:
                        with sp.Fori(0, EXPERTS) as e:
                            n0 = (j * EXPERTS + e) * (KC + FC)
                            for k in range(KC + FC):
                                sp.wait_ge(s["w_used"], n0 + (k + START))
                                src = (w_gu[l, bass.ds(e, 1), k * P:(k + 1) * P, :] if k < KC else
                                       w_down[l, bass.ds(e, 1), (k - KC) * P:(k - KC + 1) * P, :])
                                sp.dma_start(spill_w, src.rearrange("a p n -> (a p) n")).then_inc(s["w_in"], 16)
            for t in range(NT):
                sp.wait_ge(ln_ready, 3 * NT + t + 1)
                sp.dma_start(out[0, t * P:(t + 1) * P, :], h[:, t, :]).then_inc(stored, 16)
            sp.wait_ge(stored, 16 * NT)

        @block.gpsimd
        def _(pool):
            nc.gpsimd.memset(ones[:, :], 1.0).then_inc(consts, 1)
            nc.gpsimd.memset(ident[:, :], 0.0).then_inc(consts, 1)
            nc.gpsimd.memset(zero[:, :], 0.0).then_inc(consts, 1)
            pool.wait_ge(consts, 3)
            nc.gpsimd.affine_select(out=ident[:, :], in_=ident[:, :], compare_op=ALU.not_equal, fill=1.0, base=0,
                                    pattern=[[-1, P]], channel_multiplier=1).then_inc(consts, 1)
            nc.gpsimd.affine_select(out=tri[:, :], in_=ones[:, 0:1].to_broadcast([P, P]), compare_op=ALU.is_ge, fill=0.0, base=0,
                                    pattern=[[1, P]], channel_multiplier=-1).then_inc(consts, 1)
            nc.gpsimd.iota(slot_no[:, :], pattern=[[1, SLOTS]], base=0, channel_multiplier=0,
                           allow_small_or_imprecise_dtypes=True).then_inc(consts, 1)
            nc.gpsimd.iota(rank16[:, :], pattern=[[-1, EXPERTS]], base=EXPERTS, channel_multiplier=0,
                           allow_small_or_imprecise_dtypes=True).then_inc(consts, 1)
            if USED < SLOTS:
                pool.wait_ge(consts, 7)
                nc.gpsimd.memset(slot_no[:, USED:SLOTS], -1.0e6).then_inc(consts, 1)
            for hd in range(M_HEADS):
                pool.wait_ge(w_exp, hd + 1)
                for blk in range(2):
                    d = wts[:, hd, 256 * blk:256 * blk + P]
                    nc.gpsimd.tensor_tensor(d, d, tri[:, :], ALU.mult).then_inc(w_masked, 1)

        NCONST = 7 + (USED < SLOTS)

        @block.tensor
        def _(pe):
            mm = nc.tensor.matmul

            def wait_big(n, q, i=0):
                _, sems, fill = big_at(n)
                pe.wait_ge(sems[q], i * 16 + 16 * fill)

            def turn(src, n):
                if n:
                    pe.wait_ge(hT_dve, 2 * n)
                    pe.wait_ge(hT_act, 2 * n)
                for b in range(4):
                    for kk in range(2):
                        for t in range(NT):
                            c = (2 * kk + t) * P
                            k = 2 * b + kk
                            last = nc.tensor.transpose(pb[4 + b][:, c:c + P], src[:, t, k * P:(k + 1) * P], ident[:, :])
                    last.then_inc(turned, 1)

            def wait_hT(n):
                pe.wait_ge(hT_dve, 2 * n)
                pe.wait_ge(hT_act, 2 * n)

            def project(n, lhs, bank_of, done, wait_bank=None):
                w = big_at(n)[0]
                for t in range(NT):
                    for c in range(2):
                        if wait_bank:
                            wait_bank(t, c)
                        for k in range(KC):
                            if t == 0 and c == 0 and k % 2 == 0:
                                wait_big(n, k // 2)
                            last = mm(pb[bank_of(t, c)][:, :], lhs[:, k, t * P:(t + 1) * P],
                                      w[:, k, c * HALF:(c + 1) * HALF], start=k == 0, stop=k == KC - 1)
                        last.then_inc(done, 1)
                return last

            def bcast_row(bank, row, c):
                return mm(pb[bank][:, :], ident[0:9, row:row + 1].to_broadcast([9, P]),
                          rows[:, c * HALF:(c + 1) * HALF], start=True, stop=True)

            def ln_bcast(l, which, g0, b0):
                r = 2 * l + which
                for c in range(2):
                    bcast_row(g0 + c, r, c)
                    last = bcast_row(b0 + c, 4 + r, c)
                last.then_inc(ln_rows, 1)

            pe.sem_inc(big_used, NG)
            pe.sem_inc(small_used, ND)
            for first in (x_got, gu_done, heT_done, y_done, sent, ov[0]["w_used"], ov[1]["w_used"]):
                pe.sem_inc(first, START)

            pe.wait_ge(x_in, 16)
            pe.wait_ge(consts, NCONST)
            turn(h, 0)
            wait_hT(1)
            for g in range(8):
                if g % 2 == 0:
                    wait_big(0, g // 2)
                for k in range(KC):
                    last = mm(pb[g // 2][:, (g % 2) * SEQ:(g % 2 + 1) * SEQ], big[0][:, k, g * P:(g + 1) * P],
                              hT[:, k, :], start=k == 0, stop=k == KC - 1)
                last.then_inc(qk_done, 1)
            pe.wait_ge(gates_w_in, 16)
            for g in range(2):
                for k in range(KC):
                    last = mm(pb[4][0:M_HEADS, g * SEQ:(g + 1) * SEQ], w_gate[:, k, g * M_HEADS:(g + 1) * M_HEADS],
                              hT[:, k, :], start=k == 0, stop=k == KC - 1)
            last.then_inc(gates_done, 1)
            pe.wait_ge(qk_done, 8)
            pe.sem_inc(big_used, 1)

            vb = [5, 6, 7, 4]

            def v_bank_free(t, c):
                if (t, c) == (1, 1):
                    pe.wait_ge(gates_read, 2)
            project(1, hT, lambda t, c: vb[2 * t + c], v_done, v_bank_free)
            pe.wait_ge(v_done, 4)
            pe.sem_inc(big_used, 1)
            pe.wait_ge(lanes_ready, 1)
            pe.wait_ge(v_sb, 4)
            for n, ln_no in enumerate((3, 5)):
                for t in range(NT):
                    c = (2 * n + t) * M_HEADS
                    last = nc.tensor.transpose(pb[4][:, c:c + M_HEADS], lane[ln_no][:, t * P:(t + 1) * P],
                                               ident[0:M_HEADS, 0:M_HEADS])
            last.then_inc(small_T, 1)
            for hd in range(M_HEADS):
                mm(pb[5 + hd // 2][:, (hd % 2) * SEQ:(hd % 2 + 1) * SEQ],
                   ident[0:M_HEADS, hd:hd + 1].to_broadcast([M_HEADS, P]), lane[4], start=True, stop=True
                   ).then_inc(m_bcast, 1)
            pe.wait_ge(qk_sb, 8)
            for hd in range(M_HEADS):
                mm(pb[hd][:, 0:SEQ], qkT[:, 4 + hd, 0:P], qkT[:, hd, :], start=True, stop=True)
                mm(pb[hd][:, SEQ:SEQ + P], qkT[:, 4 + hd, P:SEQ], qkT[:, hd, P:SEQ], start=True, stop=True
                   ).then_inc(s_done, 1)
            ob = [7, 4, 5, 6]

            def o_bank_free(t, c):
                n = 2 * t + c
                if n == 1:
                    pe.wait_ge(small_sb, 1)
                if n >= 2:
                    pe.wait_ge(w_arg, 4 * (n - 1))
            project(2, hT, lambda t, c: ob[2 * t + c], o_done, o_bank_free)
            pe.wait_ge(o_done, 4)
            pe.sem_inc(big_used, 1)
            pe.wait_ge(o_sb, 1)
            pe.wait_ge(p_ready, M_HEADS)
            for t in range(NT):
                for hd in range(M_HEADS):
                    c = t * M_HEADS + hd
                    for s in range(t + 1):
                        lo = (s + t) * P
                        last = mm(pb[7][:, c:c + 1], wts[:, hd, lo:lo + P], ones[:, 0:1], start=s == 0, stop=s == t)
            last.then_inc(den_done, 1)
            for hd in range(M_HEADS):
                for t in range(NT):
                    for s in range(t + 1):
                        lo = (s + t) * P
                        last = mm(pb[hd][:, t * M_V:(t + 1) * M_V], wts[:, hd, lo:lo + P],
                                  val[:, s, hd * M_V:(hd + 1) * M_V], start=s == 0, stop=s == t)
                last.then_inc(num_done, 1)
            pe.wait_ge(params_in, 16 * 8)
            pe.wait_ge(o_sb, 4)
            for c in range(2):
                last = bcast_row(4 + c, 8, c)
            last.then_inc(mh_bcast, 1)
            pe.wait_ge(hn_ready, NT * M_HEADS)
            turn(val, 1)
            wait_hT(2)
            project(3, hT, lambda t, c: 2 * t + c, mix_done)
            pe.wait_ge(mix_done, 4)
            pe.sem_inc(big_used, 1)
            ln_bcast(0, 0, 4, 6)

            def moe(l):
                pe.wait_ge(ln_ready, 2 * NT * l + NT)
                turn(h, 2 + 2 * l + 0 if l == 0 else 4)
                wait_hT(3 if l == 0 else 5)
                for t in range(NT):
                    for k in range(KC):
                        last = mm(pb[0][:, t * EXPERTS:(t + 1) * EXPERTS], hT[:, k, t * P:(t + 1) * P],
                                  w_rt[:, k, :], start=k == 0, stop=k == KC - 1)
                last.then_inc(logits, 1)
                for b in range(4):
                    mm(pb[4 + b][:, :], zero[:, 0:1].to_broadcast([P, P]), big_zero(b), start=True, stop=False,
                       skip_group_check=True)
                pe.wait_ge(chosen, l + 1)
                mm(pb[1][:, 0:16], tri[:, :], oh[:, 0, :], start=True, stop=True)
                mm(pb[1][:, 16:32], ones[:, 0:1].to_broadcast([P, P]), oh[:, 0, :], start=True, stop=False)
                mm(pb[1][:, 16:32], tri[:, :], oh[:, 1, :], start=False, stop=True)
                mm(pb[1][:, 32:48], ones[:, 0:1].to_broadcast([P, P]), oh[:, 0, :], start=True, stop=False)
                mm(pb[1][:, 32:48], ones[:, 0:1].to_broadcast([P, P]), oh[:, 1, :], start=False, stop=True).then_inc(placed, 1)
                with pe.Fori(0, TURNS) as i:
                    E0 = EXPERTS * l + i * U + START

                    def gather(u):
                        pe.wait_ge(pick_ready, E0 + (u + 1))
                        pe.wait_ge(x_sb, E0 + u)
                        for k in range(KC):
                            for t in range(NT):
                                last = mm(pb[1][:, k * SLOTS:(k + 1) * SLOTS], h[:, t, k * P:(k + 1) * P],
                                          pick[u % 2][:, t, :], start=t == 0, stop=t == NT - 1)
                        last.then_inc(x_got, 1)

                    def gate_up(u):
                        n = G_EXP[l] + u
                        w = big_at(n)[0]
                        pe.wait_ge(x_sb, E0 + (u + 1))
                        pe.wait_ge(he_ready, E0 + u)
                        for k in range(KC):
                            if k % 2 == 0:
                                wait_big(n, k // 2, i)
                            for c in range(2):
                                last = mm(pb[0][c * 64:(c + 1) * 64, :].rearrange("p (a n) -> p a n", a=2),
                                          xe[u % 2][:, k, :],
                                          w[:, k, :].rearrange("p (a c n) -> p c a n", a=2, c=2)[:, c],
                                          start=k == 0, stop=k == KC - 1)
                        last.then_inc(gu_done, 1)

                    def scatter(u):
                        pe.wait_ge(y_sb, E0 + (u + 1))
                        pe.wait_ge(back_sb, E0 + (u + 1))
                        for t in range(NT):
                            for c in range(2):
                                last = mm(pb[4 + 2 * t + c][:, :], back[u % 2][c * 64:(c + 1) * 64, t * P:(t + 1) * P],
                                          ye[u % 2][c * 64:(c + 1) * 64, :], start=False, stop=False,
                                          skip_group_check=True)
                        last.then_inc(sent, 1)

                    def down(u):
                        pe.wait_ge(he_ready, E0 + (u + 1))
                        pe.wait_ge(pickg_ready, E0 + (u + 1))
                        pe.wait_ge(back_sb, E0 + u)
                        for j in range(2):
                            last = nc.tensor.transpose(pb[3][:, j * P:(j + 1) * P], act_g[u % 2][:, j * P:(j + 1) * P],
                                                       ident[:, :])
                        for t in range(NT):
                            last = nc.tensor.transpose(
                                pb[3][:, (2 + t) * P:(3 + t) * P],
                                pickg[u % 2][:, t, :, :].rearrange("p d s -> p (d s)"), ident[:, :])
                        last.then_inc(heT_done, 1)
                        pe.wait_ge(heT_sb, E0 + (u + 1))
                        n = D_EXP[l] + u
                        w, sems, fill = small_at(n)
                        pe.wait_ge(y_sb, E0 + u)
                        for j in range(2):
                            for hf in range(2):
                                kk = 2 * hf + j
                                if j == 0:
                                    pe.wait_ge(sems[hf], i * 32 + 16 * fill)
                                for c in range(2):
                                    last = mm(pb[2][c * 64:(c + 1) * 64, :],
                                              heT[:, j * P + hf * 64:j * P + (hf + 1) * 64],
                                              w[:, kk, c * HALF:(c + 1) * HALF],
                                              start=(j, hf) == (0, 0), stop=(j, hf) == (1, 1))
                        last.then_inc(y_done, 1)

                    gather(0)
                    for u in range(U):
                        gate_up(u)
                        if u:
                            scatter(u - 1)
                        pe.wait_ge(gu_done, E0 + (u + 1))
                        pe.sem_inc(big_used, 1)
                        if u < U - 1:
                            gather(u + 1)
                        down(u)
                        pe.wait_ge(y_done, E0 + (u + 1))
                        pe.sem_inc(small_used, 1)
                    scatter(U - 1)
                for b in range(4):
                    last = mm(pb[4 + b][:, :], zero[:, 0:1].to_broadcast([P, P]), big_zero(b), start=False,
                              stop=True, skip_group_check=True)
                last.then_inc(mix_done, 4)
                pe.wait_ge(gu_done, EXPERTS * (l + 1) + START)
                overflow(l)
                pe.wait_ge(he_ready, EXPERTS * (l + 1) + START)
                ln_bcast(l, 1, 0, 2)

            def overflow(l):
                s = ov[l]
                rounds = pe.value_load(extra[0:1, 0:1], min_val=0, max_val=3)
                with pe.If(rounds > 0):
                    with pe.Fori(0, rounds) as j:
                        with pe.Fori(0, EXPERTS) as e:
                            n = j * EXPERTS + e
                            pe.wait_ge(s["pick"], n + 1)
                            pe.wait_ge(res_ready, 4 * (l + 1))
                            for k in range(KC):
                                for t in range(NT):
                                    last = mm(pb[1][:, k * SLOTS:(k + 1) * SLOTS], h[:, t, k * P:(k + 1) * P],
                                              pick[0][:, t, :], start=t == 0, stop=t == NT - 1)
                            last.then_inc(s["x"], 1)
                            pe.wait_ge(s["xs"], n + 1)
                            for k in range(KC):
                                pe.wait_ge(s["w_in"], (n * (KC + FC) + (k + 1)) * 16)
                                for c in range(2):
                                    last = mm(pb[0][c * 64:(c + 1) * 64, :].rearrange("p (a n) -> p a n", a=2),
                                              xe[0][:, k, :],
                                              spill_w.rearrange("p (a c n) -> p c a n", a=2, c=2)[:, c],
                                              start=k == 0, stop=k == KC - 1)
                                last.then_inc(s["w_used"], 1)
                            pe.wait_ge(s["he"], n + 1)
                            for jj in range(2):
                                nc.tensor.transpose(pb[3][:, jj * P:(jj + 1) * P], act_g[0][:, jj * P:(jj + 1) * P],
                                                    ident[:, :])
                            for t in range(NT):
                                last = nc.tensor.transpose(
                                    pb[3][:, (2 + t) * P:(3 + t) * P],
                                    pickg[0][:, t, :, :].rearrange("p d s -> p (d s)"), ident[:, :])
                            last.then_inc(s["t"], 1)
                            pe.wait_ge(s["ts"], n + 1)
                            for kk in range(FC):
                                pe.wait_ge(s["w_in"], (n * (KC + FC) + (KC + kk + 1)) * 16)
                                hf, jj = kk // 2, kk % 2
                                for c in range(2):
                                    last = mm(pb[2][c * 64:(c + 1) * 64, :],
                                              heT[:, jj * P + hf * 64:jj * P + (hf + 1) * 64],
                                              spill_w[:, c * HALF:(c + 1) * HALF], start=kk == 0, stop=kk == FC - 1)
                                last.then_inc(s["w_used"], 1)
                            pe.wait_ge(s["ys"], n + 1)
                            for t in range(NT):
                                for c in range(2):
                                    last = mm(pb[4 + 2 * t + c][:, :], back[0][c * 64:(c + 1) * 64, t * P:(t + 1) * P],
                                              ye[0][c * 64:(c + 1) * 64, :], start=True, stop=True)
                            last.then_inc(s["z"], 1)
                            pe.wait_ge(s["zs"], n * 4 + (4 + START))

            def big_zero(b):
                return zero[:, 0:1].to_broadcast([P, HALF])

            moe(0)

            pe.wait_ge(ln_ready, 2 * NT)
            turn(h, 3)
            wait_hT(4)
            kvw, kvs, kvf = small_at(D_KV)
            kvw = kvw[:, :, :].rearrange("p a (b n) -> p (a b) n", b=2)
            for t in range(NT):
                for k in range(KC):
                    if t == 0 and k % 4 == 0:
                        pe.wait_ge(kvs[k // 4], 16 * kvf)
                    last = mm(pb[t][:, :], hT[:, k, t * P:(t + 1) * P], kvw[:, k, :], start=k == 0, stop=k == KC - 1)
                last.then_inc(kv_done, 1)
            pe.wait_ge(kv_done, NT)
            pe.sem_inc(small_used, 1)
            project(G_MIX[1], hT, lambda t, c: 2 + 2 * t + c, q_done)
            pe.wait_ge(q_done, 4)
            pe.sem_inc(big_used, 1)
            pe.wait_ge(k_rot, NT)
            for g in range(A_KV):
                for t in range(NT):
                    c = (g % 2) * SEQ + t * P
                    last = nc.tensor.transpose(pb[6 + g // 2][:, c:c + P],
                                               kdup[:, t, g, :, :].rearrange("p d n -> p (d n)"), ident[:, :])
                if g % 2:
                    last.then_inc(kT_done, 1)
            pe.wait_ge(v_split, NT)
            for t in range(NT):
                pe.wait_ge(q_rotd, 2 * t + 2)
                if t:
                    pe.wait_ge(kT_sb, 2)
                for jj in range(2):
                    b = jj if t == 0 else 6 + jj
                    for n in range(4):
                        j = 4 * jj + n
                        last = nc.tensor.transpose(pb[b][:, n * P:(n + 1) * P], q_rot[:, t, j * P:(j + 1) * P], ident[:, :])
                    last.then_inc(qT_done, 1)
            pe.wait_ge(kT_sb, 2)

            def score(t):
                pe.wait_ge(qT_sb, 2 * t + 2)
                for (tt, par, jj) in SC_ORDER:
                    if tt != t:
                        continue
                    b = SCB[t][par][jj]
                    for n in range(4):
                        j = 4 * jj + n
                        for ci in range(2):
                            c = 2 * t + ci
                            lo = max(0, c - 1) * CHUNK
                            hi = (c + 1) * CHUNK
                            last = mm(pb[b][ci * 64:(ci + 1) * 64, (n + 1) * P - (hi - lo):(n + 1) * P],
                                      qT[par * 64:(par + 1) * 64, j, c * CHUNK:(c + 1) * CHUNK],
                                      kT[par * 64:(par + 1) * 64, j // 2, lo:hi], start=True, stop=True)
                    last.then_inc(sc_done, 1)
            score(0)
            score(1)
            for n, (t, par, jj) in enumerate(SC_ORDER):
                b = SCB[t][par][jj]
                pe.wait_ge(pn_ready, n + 1)
                for s in range(4):
                    last = nc.tensor.transpose(pb[b][:, s * P:(s + 1) * P], prob[n % 2][:, s * P:(s + 1) * P], ident[:, :])
                last.then_inc(pT_done, 1)
                pe.wait_ge(pT_sb, n + 1)
                ob_ = SCB[t][0][jj]
                pv = probT[n % 2].rearrange("p (s q) -> p s q", s=4)
                for gg in range(2):
                    g = 2 * jj + gg
                    for ci in range(2):
                        vw = v_tok if ci else v_shift
                        o = pb[ob_][par * 64:(par + 1) * 64, :].rearrange("p (s q) -> p s q", s=4)
                        last = mm(o[:, 2 * gg:2 * gg + 2, ci * 64:(ci + 1) * 64], vw[:, t, g * DH:(g + 1) * DH],
                                  pv[:, 2 * gg:2 * gg + 2, ci * 64:(ci + 1) * 64], start=True, stop=True)
                last.then_inc(pv_done, 1)
            pe.wait_ge(outT_sb, 4)
            project(G_MIX[1] + 1, hT, lambda t, c: 2 * t + c, mix_done)
            pe.wait_ge(mix_done, 12)
            pe.sem_inc(big_used, 1)
            ln_bcast(1, 0, 4, 6)
            moe(1)

        @block.scalar
        def _(act):
            A = nc.scalar.activation
            n_ach = [0]

            def link(ins):
                n_ach[0] += 1
                ins.then_inc(ach, 1)
                act.wait_ge(ach, n_ach[0])

            act.dma_start(h[:, :, :], x[0].rearrange("(t p) n -> p t n", p=P)).then_inc(x_in, 16)
            act.dma_start(w_gate[:, :, :], w_in_a[0, :, 3072:3080].rearrange("(k p) n -> p k n", p=P)).then_inc(gates_w_in, 16)
            act.dma_start(b_gate[:, :], b_gates_a[0].rearrange("(g h) -> h g", g=2),
                          allow_slow_non_contiguous=True).then_inc(gates_w_in, 16)
            act.dma_start(rows[0:4, :], ln_g.rearrange("l w n -> (l w) n")).then_inc(params_in, 16)
            act.dma_start(rows[4:8, :], ln_b.rearrange("l w n -> (l w) n")).then_inc(params_in, 16)
            act.dma_start(rows[8:9, :], mh_norm_a).then_inc(params_in, 16)
            act.dma_start(w_rt[:, :, :], w_router.rearrange("(k p) n -> p k n", p=P)).then_inc(params_in, 16)
            act.dma_start(b_rt[:, :], b_router.rearrange("(a n) -> a n", a=1).to_broadcast([P, EXPERTS])).then_inc(params_in, 16)
            act.dma_start(sink[:, :], sinks_b.to_broadcast([P, A_HEADS])).then_inc(params_in, 16)
            for a in range(2):
                act.dma_start(cs[:, :, a * 32:(a + 1) * 32], rope[a].rearrange("(t p) n -> p t n", p=P)).then_inc(params_in, 16)

            def take_hT(n):
                for b in range(2, 4):
                    act.wait_ge(turned, 4 * n + b + 1)
                    A(hT[:, 2 * b:2 * b + 2, :].rearrange("p k n -> p (k n)"), pb[4 + b][:, :], ACT.Copy).then_inc(hT_act, 1)

            def ln_norm_part(n):
                src = h if n % 2 == 0 else res
                for t in range(NT):
                    act.wait_ge(ln_std_in, NT * n + t + 1)
                    A(ln[:, t, 15:16], ln[:, t, 14:15], ACT.Sqrt).then_inc(ln_std, 1)
                for t in range(NT):
                    act.wait_ge(ln_scale, NT * n + t + 1)
                    A(src[:, t, :], src[:, t, :], ACT.Identity, bias=ln[:, t, 17:18], scale=ln[:, t, 16:17]).then_inc(ln_norm, 1)

            for first in (x_sb, silu_done):
                act.sem_inc(first, START)

            take_hT(0)
            for g in range(8):
                act.wait_ge(qk_done, 2 * (g // 2) + 2)
                A(qkT[:, g, :], pb[g // 2][:, (g % 2) * SEQ:(g % 2 + 1) * SEQ], ACT.Copy,
                  scale=1.0 if g < 4 else float(M_QK) ** -0.5).then_inc(qk_sb, 1)
            act.wait_ge(gates_done, 1)
            act.wait_ge(d2a, 1)
            for g in range(2):
                A(lane[g], pb[4][0:M_HEADS, g * SEQ:(g + 1) * SEQ], ACT.Tanh, bias=b_gate[:, g:g + 1],
                  scale=1.0 / CAP).then_inc(gates_read, 1)
            act.wait_ge(gates_read, 2)
            link(A(lane[2], lane[1], ACT.Exp, scale=-CAP))
            A(lane[2], lane[2], ACT.Ln, bias=ones[0:M_HEADS, 0:1]).then_inc(a2d, 1)
            vb = [5, 6, 7, 4]
            for n in range(4):
                act.wait_ge(v_done, n + 1)
                A(val[:, n // 2, (n % 2) * HALF:(n % 2 + 1) * HALF], pb[vb[n]][:, :], ACT.Copy).then_inc(v_sb, 1)
            act.wait_ge(d2a, 2)
            A(st[:, 8:16], st[:, 8:16], ACT.Exp).then_inc(a2d, 1)
            for hd in range(M_HEADS):
                act.wait_ge(w_arg, 2 * hd + 2)
                A(wts[:, hd, :], wts[:, hd, :], ACT.Exp).then_inc(w_exp, 1)
            ob = [7, 4, 5, 6]
            act.wait_ge(s_done, M_HEADS)
            for n in range(4):
                act.wait_ge(o_done, n + 1)
                A(gate_o[:, n // 2, (n % 2) * HALF:(n % 2 + 1) * HALF], pb[ob[n]][:, :], ACT.Sigmoid).then_inc(o_sb, 1)
            act.wait_ge(den_inv, 1)
            for hd in range(M_HEADS):
                act.wait_ge(num_done, hd + 1)
                for t in range(NT):
                    c = t * M_HEADS + hd
                    A(wts[:, hd, 0:M_V] if t == 0 else wts[:, hd, P:P + M_V], pb[hd][:, t * M_V:(t + 1) * M_V], ACT.Square, scale=st[:, 16 + c:17 + c],
                      accum_out=st[:, 24 + c:25 + c]).then_inc(sq_done, 1)
                    act.wait_ge(sq_done, hd * 2 + t + 1)
            act.wait_ge(d2a, 3)
            A(st[:, 32:40], st[:, 32:40], ACT.Sqrt).then_inc(a2d, 1)
            take_hT(1)
            ln_norm_part(0)

            def moe(l):
                take_hT(2 if l == 0 else 4)
                act.wait_ge(rt_exp_in, l + 1)
                A(r_logit, r_logit, ACT.Exp).then_inc(rt_exp, 1)
                with act.Fori(0, TURNS) as i:
                    E0 = EXPERTS * l + i * U + START

                    def take_x(u):
                        act.wait_ge(x_got, E0 + (u + 1))
                        act.wait_ge(gu_done, E0 + max(u - 1, 0))
                        A(xe[u % 2].rearrange("p k s -> p (k s)"), pb[1][:, :], ACT.Copy).then_inc(x_sb, 1)

                    take_x(0)
                    for u in range(U):
                        act.wait_ge(gu_done, E0 + (u + 1))
                        act.wait_ge(heT_done, E0 + max(u - 1, 0))
                        A(act_g[u % 2], pb[0][:, 0:256], ACT.Silu).then_inc(silu_done, 1)
                        if u < U - 1:
                            take_x(u + 1)
                s = ov[l]
                rounds = act.value_load(extra[0:1, 0:1], min_val=0, max_val=3)
                with act.If(rounds > 0):
                    with act.Fori(0, rounds) as j:
                        with act.Fori(0, EXPERTS) as e:
                            n = j * EXPERTS + e
                            act.wait_ge(s["x"], n + 1)
                            A(xe[0].rearrange("p k s -> p (k s)"), pb[1][:, :], ACT.Copy).then_inc(s["xs"], 1)
                            act.wait_ge(s["w_used"], n * (KC + FC) + (KC + START))
                            A(act_g[0], pb[0][:, 0:256], ACT.Silu).then_inc(s["silu"], 1)
                ln_norm_part(2 * l + 1)

            moe(0)

            take_hT(3)
            act.wait_ge(shift_zero, 1)
            for t in range(NT):
                act.wait_ge(kv_done, t + 1)
                A(v_tok[:, t, :], pb[t][:, KV_W:2 * KV_W], ACT.Copy)
                if t == 0:
                    A(v_shift[0:64, 1, :], pb[0][64:128, KV_W:2 * KV_W], ACT.Copy)
                A(v_shift[64:128, t, :], pb[t][0:64, KV_W:2 * KV_W], ACT.Copy).then_inc(v_split, 1)
            for b in range(2):
                act.wait_ge(kT_done, b + 1)
                A(kT[:, 2 * b:2 * b + 2, :].rearrange("p g n -> p (g n)"), pb[6 + b][:, :], ACT.Copy).then_inc(kT_sb, 1)
            for t in range(NT):
                for jj in range(2):
                    act.wait_ge(qT_done, 2 * t + jj + 1)
                    b = jj if t == 0 else 6 + jj
                    A(qT[:, 4 * jj:4 * jj + 4, t * P:(t + 1) * P], pb[b][:, :].rearrange("p (j n) -> p j n", j=4),
                      ACT.Copy).then_inc(qT_sb, 1)
            act.wait_ge(qT_done, 4)
            for n, (t, par, jj) in enumerate(SC_ORDER):
                b = SCB[t][par][jj]
                act.wait_ge(mx_ready, n + 1)
                if n >= 2:
                    act.wait_ge(pT_done, n - 1)
                o = 64 * (n % 2)
                for s in range(4):
                    A(prob[n % 2][:, s * P:(s + 1) * P], pb[b][:, s * P:(s + 1) * P], ACT.Exp,
                      bias=st[:, o + 4 + s:o + 5 + s], scale=float(DH) ** -0.5, accum_out=st[:, o + 12 + s:o + 13 + s]
                      ).then_inc(e_done, 1)
                A(st[:, o + 8:o + 12], st[:, o + 8:o + 12], ACT.Exp).then_inc(e_done, 1)
                if par == 1:
                    act.wait_ge(pv_done, n + 1)
                    ob_ = SCB[t][0][jj]
                    A(hT[:, 4 * jj:4 * jj + 4, t * P:(t + 1) * P], pb[ob_][:, :].rearrange("p (j n) -> p j n", j=4),
                      ACT.Copy).then_inc(outT_sb, 1)
            ln_norm_part(2)
            moe(1)

        @block.vector
        def _(dve):
            V = nc.vector
            n_dch = [0]

            def link(ins):
                n_dch[0] += 1
                ins.then_inc(dch, 1)
                dve.wait_ge(dch, n_dch[0])

            def take_hT(n):
                for b in range(2):
                    dve.wait_ge(turned, 4 * n + b + 1)
                    V.tensor_copy(hT[:, 2 * b:2 * b + 2, :].rearrange("p k n -> p (k n)"), pb[4 + b][:, :]).then_inc(hT_dve, 1)

            def layer_norm(n, src, bank0, g0, b0):
                for t in range(NT):
                    for c in range(2):
                        dve.wait_ge(mix_done, 4 * n + (2 * t + c + 1 if n % 2 == 0 else 4))
                        cc = slice(c * HALF, (c + 1) * HALF)
                        ins = V.scalar_tensor_tensor(out=src[:, t, cc], in0=h[:, t, cc], scalar=ALPHA,
                                                     in1=pb[bank0 + 2 * t + c][:, :], op0=ALU.mult, op1=ALU.add)
                        link(ins)
                        if n % 2:
                            dve.sem_inc(res_ready, 1)
                if n % 2:
                    overflow(n // 2)
                for t in range(NT):
                    for c in range(2):
                        link(V.bn_stats(ln[:, t, 6 * c:6 * c + 6], src[:, t, c * HALF:(c + 1) * HALF]))
                    link(V.bn_aggr(ln[:, t, 12:14], ln[:, t, 0:12]))
                    V.tensor_scalar(ln[:, t, 14:15], ln[:, t, 13:14], LN_EPS, None, ALU.add).then_inc(ln_std_in, 1)
                for t in range(NT):
                    dve.wait_ge(ln_std, NT * n + t + 1)
                    link(V.reciprocal(ln[:, t, 16:17], ln[:, t, 15:16]))
                    V.scalar_tensor_tensor(out=ln[:, t, 17:18], in0=ln[:, t, 12:13], scalar=-1.0,
                                           in1=ln[:, t, 16:17], op0=ALU.mult, op1=ALU.mult).then_inc(ln_scale, 1)
                dve.wait_ge(ln_rows, n + 1)
                for t in range(NT):
                    dve.wait_ge(ln_norm, NT * n + t + 1)
                    for c in range(2):
                        cc = slice(c * HALF, (c + 1) * HALF)
                        ins = V.tensor_tensor(src[:, t, cc], src[:, t, cc], pb[g0 + c][:, :], ALU.mult)
                        if c:
                            link(ins)
                    for c in range(2):
                        cc = slice(c * HALF, (c + 1) * HALF)
                        ins = V.tensor_tensor(h[:, t, cc], src[:, t, cc], pb[b0 + c][:, :], ALU.add)
                    ins.then_inc(ln_ready, 1)

            for first in (pick_ready, pickg_ready, he_ready, heT_sb, back_sb, y_sb, ov[0]["zs"], ov[1]["zs"]):
                dve.sem_inc(first, START)

            dve.wait_ge(gates_w_in, 32)
            V.tensor_scalar(b_gate[:, :], b_gate[:, :], 1.0 / CAP, None, ALU.mult).then_inc(d2a, 1)
            take_hT(0)
            dve.wait_ge(a2d, 1)
            link(V.tensor_tensor_scan(out=lane[1], data0=ones[0:M_HEADS, 0:1].to_broadcast([M_HEADS, SEQ]),
                                      data1=lane[2], initial=0.0, op0=ALU.mult, op1=ALU.add))
            link(V.scalar_tensor_tensor(out=lane[3], in0=lane[0], scalar=CAP, in1=lane[1], op0=ALU.mult, op1=ALU.add))
            link(V.tensor_tensor_scan(out=lane[2], data0=lane[3], data1=lane[3], initial=0.0, op0=ALU.max, op1=ALU.max))
            V.tensor_scalar(lane[4], lane[2], -1.0, None, ALU.mult)
            V.tensor_tensor(lane[5], lane[1], lane[2], ALU.subtract).then_inc(lanes_ready, 1)
            dve.wait_ge(small_T, 1)
            link(V.tensor_copy(st[:, 0:8], pb[4][:, 0:8]))
            V.tensor_scalar(st[:, 8:16], pb[4][:, 8:16], 88.0, None, ALU.min).then_inc(d2a, 1)
            dve.wait_ge(d2a, 2)
            dve.sem_inc(small_sb, 1)
            dve.wait_ge(m_bcast, M_HEADS)
            for hd in range(M_HEADS):
                mb = pb[5 + hd // 2][:, (hd % 2) * SEQ:(hd % 2 + 1) * SEQ]
                V.tensor_scalar(wts[:, hd, 0:SEQ], mb, st[:, hd:hd + 1], 0.0, ALU.add, ALU.min).then_inc(w_arg, 1)
                V.tensor_scalar(wts[:, hd, SEQ:SEQ + P], mb[:, P:SEQ], st[:, 4 + hd:5 + hd], 0.0, ALU.add, ALU.min
                                ).then_inc(w_arg, 1)
            for hd in range(M_HEADS):
                dve.wait_ge(s_done, hd + 1)
                dve.wait_ge(w_masked, 2 * hd + 2)
                V.tensor_tensor(wts[:, hd, :], wts[:, hd, :], pb[hd][:, 0:SEQ + P], ALU.mult).then_inc(p_ready, 1)
            dve.wait_ge(den_done, 1)
            dve.wait_ge(a2d, 2)
            link(V.tensor_copy(st[:, 32:40], pb[7][:, 0:8]))
            link(V.scalar_tensor_tensor(out=st[:, 40:48], in0=st[:, 32:40], scalar=-1.0, in1=st[:, 32:40],
                                        op0=ALU.mult, op1=ALU.max))
            link(V.tensor_tensor(st[:, 40:48], st[:, 40:48], st[:, 8:16], ALU.max))
            V.reciprocal(st[:, 16:24], st[:, 40:48]).then_inc(den_inv, 1)
            dve.wait_ge(mh_bcast, 1)
            for t in range(NT):
                for c in range(2):
                    cc = slice(c * HALF, (c + 1) * HALF)
                    ins = V.tensor_tensor(gate_o[:, t, cc], gate_o[:, t, cc], pb[4 + c][:, :], ALU.mult)
            link(ins)
            dve.wait_ge(sq_done, 8)
            V.tensor_scalar(st[:, 32:40], st[:, 24:32], 1.0 / M_V, MH_EPS, ALU.mult, ALU.add).then_inc(d2a, 1)
            dve.wait_ge(a2d, 3)
            link(V.reciprocal(st[:, 40:48], st[:, 32:40]))
            link(V.tensor_tensor(st[:, 40:48], st[:, 40:48], st[:, 16:24], ALU.mult))
            for hd in range(M_HEADS):
                for t in range(NT):
                    cc = slice(hd * M_V, (hd + 1) * M_V)
                    c = 40 + t * M_HEADS + hd
                    V.scalar_tensor_tensor(out=val[:, t, cc], in0=pb[hd][:, t * M_V:(t + 1) * M_V],
                                           scalar=st[:, c:c + 1], in1=gate_o[:, t, cc], op0=ALU.mult, op1=ALU.mult
                                           ).then_inc(hn_ready, 1)
            take_hT(1)
            layer_norm(0, h, 0, 4, 6)

            def route(l):
                def b3(ap, n):
                    return ap.rearrange("p (t o) -> p t o", o=1).to_broadcast([P, NT, n])
                lg = r_logit.rearrange("p (t e) -> p t e", t=NT)
                dve.wait_ge(logits, l + 1)
                dve.wait_ge(params_in, 16 * 8)
                link(V.reduce_max(r_s[:, 0:2], pb[0][:, 0:32].rearrange("p (t e) -> p t e", t=NT), AX_X))
                V.tensor_tensor(lg, pb[0][:, 0:32].rearrange("p (t e) -> p t e", t=NT), b3(r_s[:, 0:2], 16),
                                ALU.subtract).then_inc(rt_exp_in, 1)
                dve.wait_ge(rt_exp, l + 1)
                link(V.reduce_sum(r_s[:, 2:4], lg, AX_X))
                link(V.reciprocal(r_s[:, 4:6], r_s[:, 2:4]))
                link(V.tensor_tensor(r_prob, lg, b3(r_s[:, 4:6], 16), ALU.mult))
                link(V.tensor_tensor(r_sel, r_prob, b_rt[:, :].rearrange("p (o e) -> p o e", o=1).to_broadcast([P, NT, 16]), ALU.add))
                s4 = st[:, 64:96].rearrange("p (q a b) -> p q a b", a=2, b=2)
                hi = r_logit[:, 0:16].rearrange("p (q a) -> p q a", a=2)
                lo = r_logit[:, 16:32].rearrange("p (q a) -> p q a", a=2)
                V.tensor_tensor(hi, s4[:, :, :, 0], s4[:, :, :, 1], ALU.max)
                link(V.tensor_tensor(lo, s4[:, :, :, 0], s4[:, :, :, 1], ALU.min))
                V.tensor_tensor(r_s[:, 0:8], hi[:, :, 0], hi[:, :, 1], ALU.max)
                V.tensor_tensor(r_s[:, 8:16], hi[:, :, 0], hi[:, :, 1], ALU.min)
                link(V.tensor_tensor(r_s[:, 16:24], lo[:, :, 0], lo[:, :, 1], ALU.max))
                link(V.tensor_tensor(r_s[:, 8:16], r_s[:, 8:16], r_s[:, 16:24], ALU.max))
                link(V.tensor_tensor(r_s[:, 0:8], r_s[:, 0:8], r_s[:, 8:16], ALU.add))
                gs = r_s[:, 0:8].rearrange("p (t g) -> p t g", t=NT)

                def first_best(vals, n, rank, key, m, res_):
                    link(V.reduce_max(m, vals, AX_X))
                    link(V.tensor_tensor(key, vals, b3(m, n), ALU.is_equal))
                    link(V.tensor_tensor(key, key, rank[:, :].rearrange("p (o e) -> p o e", o=1).to_broadcast([P, NT, n]), ALU.mult))
                    link(V.reduce_max(m, key, AX_X))
                    link(V.tensor_tensor(res_, key, b3(m, n), ALU.is_equal))
                gm = r_s[:, 8:16].rearrange("p (t g) -> p t g", t=NT)
                first_best(gs, 4, rank4, r_s[:, 16:24].rearrange("p (t g) -> p t g", t=NT), r_s[:, 24:26], gm)
                link(V.tensor_scalar(r_s[:, 16:24], r_s[:, 8:16], 1.0, -LOW, ALU.subtract, ALU.mult))
                q4 = lambda ap: ap.rearrange("p (q a) -> p q a", a=4)
                b4 = lambda ap: ap.rearrange("p (q o) -> p q o", o=1).to_broadcast([P, 8, 4])
                link(V.tensor_tensor(q4(r_logit), q4(st[:, 64:96]), b4(r_s[:, 8:16]), ALU.mult))
                link(V.tensor_tensor(q4(r_logit), q4(r_logit), b4(r_s[:, 16:24]), ALU.add))
                first_best(lg, 16, rank16, r_a, r_s[:, 24:26], oh1)
                link(V.scalar_tensor_tensor(out=r_logit, in0=ro[:, 0, :], scalar=3.0 * LOW, in1=r_logit, op0=ALU.mult, op1=ALU.add))
                first_best(lg, 16, rank16, r_a, r_s[:, 24:26], oh2)
                V.tensor_tensor(oh, oh1, oh2, ALU.add).then_inc(chosen, 1)
                dve.wait_ge(chosen, l + 1)
                link(V.tensor_tensor(r_a, oh, r_prob, ALU.mult))
                link(V.reduce_sum(r_s[:, 0:2], r_a, AX_X))
                link(V.reciprocal(r_s[:, 2:4], r_s[:, 0:2]))
                link(V.tensor_tensor(gate[:, :, :].rearrange("p e t -> p t e"), r_a, b3(r_s[:, 2:4], 16), ALU.mult))
                dve.wait_ge(placed, l + 1)
                pt = pos[:, :, :].rearrange("p e t -> p t e")
                link(V.tensor_tensor(r_a, pb[1][:, 0:32].rearrange("p (t e) -> p t e", t=NT), oh, ALU.mult))
                link(V.tensor_scalar(pt, r_a, 1.0, None, ALU.subtract))
                link(V.reduce_max(extra_f[:, 0:1], pb[1][:, 32:48], AX_X))
                link(V.tensor_scalar(extra_f[:, 1:2], extra_f[:, 0:1], float(USED), None, ALU.is_gt))
                for r in range(2, SEQ // USED if USED == 64 else 4):
                    link(V.tensor_scalar(extra_f[:, 2:3], extra_f[:, 0:1], float(r * USED), None, ALU.is_gt))
                    link(V.tensor_tensor(extra_f[:, 1:2], extra_f[:, 1:2], extra_f[:, 2:3], ALU.add))
                V.tensor_copy(extra[:, :], extra_f[:, 1:2]).then_inc(lists, 1)

            def make_pick(dst, dstg, e, chain):
                chain(V.tensor_tensor(dst, slot_no[:, :].rearrange("p (o s) -> p o s", o=1).to_broadcast([P, NT, SLOTS]),
                                      pos[:, bass.ds(e, 1), :].rearrange("p o t -> p t o").to_broadcast([P, NT, SLOTS]),
                                      ALU.is_equal))
                for t in range(NT):
                    for d in range(2):
                        ins = V.tensor_tensor(dstg[:, t, d, :], dst[:, t, :],
                                              gate[:, bass.ds(e, 1), t:t + 1].rearrange("p o t -> p (o t)").to_broadcast([P, SLOTS]),
                                              ALU.mult)
                return ins

            def experts(l):
                dve.wait_ge(lists, l + 1)
                with dve.Fori(0, TURNS) as i:
                    E0 = EXPERTS * l + i * U + START

                    def picks(u):
                        dve.wait_ge(x_got, E0 + max(u - 1, 0))
                        dve.wait_ge(heT_done, E0 + max(u - 1, 0))

                        def ready(ins):
                            ins.then_inc(pick_ready, 1)
                            dve.wait_ge(pick_ready, E0 + (u + 1))
                        make_pick(pick[u % 2], pickg[u % 2], i * U + u, ready).then_inc(pickg_ready, 1)

                    picks(0)
                    picks(1)
                    for u in range(U):
                        dve.wait_ge(silu_done, E0 + (u + 1))
                        V.tensor_tensor(act_g[u % 2], act_g[u % 2], pb[0][:, 256:512], ALU.mult).then_inc(he_ready, 1)
                        dve.wait_ge(heT_done, E0 + (u + 1))
                        V.tensor_copy(heT, pb[3][:, 0:2 * P]).then_inc(heT_sb, 1)
                        dve.wait_ge(sent, E0 + max(u - 1, 0))
                        V.tensor_copy(back[u % 2], pb[3][:, 2 * P:4 * P]).then_inc(back_sb, 1)
                        if u + 2 < U:
                            picks(u + 2)
                        dve.wait_ge(y_done, E0 + (u + 1))
                        dve.wait_ge(sent, E0 + max(u - 1, 0))
                        V.tensor_copy(ye[u % 2], pb[2][:, :]).then_inc(y_sb, 1)

            def overflow(l):
                s = ov[l]
                rounds = dve.value_load(extra[0:1, 0:1], min_val=0, max_val=3)
                with dve.If(rounds > 0):
                    with dve.Fori(0, rounds) as j:
                        V.tensor_scalar(pos[:, :, :], pos[:, :, :], float(USED), None, ALU.subtract).then_inc(s["dve"], 1)
                        with dve.Fori(0, EXPERTS) as e:
                            n = j * EXPERTS + e

                            def ready(ins):
                                ins.then_inc(s["dve"], 1)
                                dve.wait_ge(s["dve"], n + j + 2)
                            dve.wait_ge(s["dve"], n + j + 1)
                            make_pick(pick[0], pickg[0], e, ready).then_inc(s["pick"], 1)
                            dve.wait_ge(s["silu"], n + 1)
                            V.tensor_tensor(act_g[0], act_g[0], pb[0][:, 256:512], ALU.mult).then_inc(s["he"], 1)
                            dve.wait_ge(s["t"], n + 1)
                            V.tensor_copy(heT, pb[3][:, 0:2 * P])
                            V.tensor_copy(back[0], pb[3][:, 2 * P:4 * P]).then_inc(s["ts"], 1)
                            dve.wait_ge(s["w_used"], n * (KC + FC) + (KC + FC + START))
                            V.tensor_copy(ye[0], pb[2][:, :]).then_inc(s["ys"], 1)
                            dve.wait_ge(s["z"], n + 1)
                            dve.wait_ge(s["zs"], n * 4 + START)
                            for t in range(NT):
                                for c in range(2):
                                    cc = slice(c * HALF, (c + 1) * HALF)
                                    V.tensor_tensor(res[:, t, cc], res[:, t, cc], pb[4 + 2 * t + c][:, :], ALU.add
                                                    ).then_inc(s["zs"], 1)
                    dve.wait_ge(s["zs"], rounds * (EXPERTS * 4) + START)
                    V.tensor_copy(extra_f[:, 3:4], extra_f[:, 1:2])

            take_hT(2)
            route(0)
            experts(0)
            layer_norm(1, res, 4, 0, 2)

            take_hT(3)

            def rotate(dst1, dst2, src, t, nh):
                c = cs[:, t, 0:32].rearrange("p (o n) -> p o n", o=1).to_broadcast([P, nh, 32])
                s = cs[:, t, 32:64].rearrange("p (o n) -> p o n", o=1).to_broadcast([P, nh, 32])
                x1, x2 = src[:, :, 0:32], src[:, :, 32:64]
                V.tensor_tensor(dst1, x1, c, ALU.mult)
                link(V.tensor_tensor(dst2, x2, c, ALU.mult))
                V.tensor_tensor(x1, x1, s, ALU.mult)
                link(V.tensor_tensor(x2, x2, s, ALU.mult))
                V.tensor_tensor(dst1, dst1, x2, ALU.subtract)
                return V.tensor_tensor(dst2, dst2, x1, ALU.add)

            V.memset(v_shift[:, :, :], 0.0).then_inc(shift_zero, 1)
            for t in range(NT):
                dve.wait_ge(v_split, t + 1)
                link(rotate(kdup[:, t, :, 0, 0:32], kdup[:, t, :, 0, 32:64],
                            pb[t][:, 0:KV_W].rearrange("p (g n) -> p g n", g=A_KV), t, A_KV))
                V.tensor_copy(kdup[:, t, :, 1, :], kdup[:, t, :, 0, :]).then_inc(k_rot, 1)
            for t in range(NT):
                for c in range(2):
                    dve.wait_ge(q_done, 2 * t + c + 1)
                    qd = q_rot[:, t, c * HALF:(c + 1) * HALF].rearrange("p (h n) -> p h n", n=DH)
                    link(rotate(qd[:, :, 0:32], qd[:, :, 32:64],
                                pb[2 + 2 * t + c][:, :].rearrange("p (h n) -> p h n", n=DH), t, 8))
                    dve.sem_inc(q_rotd, 1)
            inv = float(DH) ** -0.5

            def soft_in(n):
                t, par, jj = SC_ORDER[n]
                b = SCB[t][par][jj]
                o = 64 * (n % 2)
                sk = sink[:, 8 * jj + par:8 * jj + 8:2]
                dve.wait_ge(sc_done, n + 1)
                pr = pb[b][:, :].rearrange("p (s k) -> p s k", s=4)
                if t == 0:
                    link(V.memset(pr[0:64, :, 0:64], LOW))
                if n >= 2:
                    dve.wait_ge(e_done, 5 * (n - 1))
                link(V.reduce_max(st[:, o:o + 4], pr, AX_X))
                link(V.scalar_tensor_tensor(out=st[:, o:o + 4], in0=st[:, o:o + 4], scalar=inv, in1=sk, op0=ALU.mult, op1=ALU.max))
                V.tensor_scalar(st[:, o + 4:o + 8], st[:, o:o + 4], -1.0, None, ALU.mult)
                V.tensor_tensor(st[:, o + 8:o + 12], sk, st[:, o:o + 4], ALU.subtract).then_inc(mx_ready, 1)

            def soft_out(n):
                o = 64 * (n % 2)
                dve.wait_ge(e_done, 5 * (n + 1))
                link(V.tensor_tensor(st[:, o:o + 4], st[:, o + 8:o + 12], st[:, o + 12:o + 16], ALU.add))
                link(V.reciprocal(st[:, o + 16:o + 20], st[:, o:o + 4]))
                p3 = prob[n % 2].rearrange("p (s k) -> p s k", s=4)
                V.tensor_tensor(p3, p3, st[:, o + 16:o + 20].rearrange("p (s o) -> p s o", o=1).to_broadcast([P, 4, P]),
                                ALU.mult).then_inc(pn_ready, 1)

            def soft_T(n):
                t, par, jj = SC_ORDER[n]
                dve.wait_ge(pT_done, n + 1)
                if n >= 2:
                    dve.wait_ge(pv_done, n - 1)
                V.tensor_copy(probT[n % 2], pb[SCB[t][par][jj]][:, :]).then_inc(pT_sb, 1)

            soft_in(0)
            for n in range(8):
                if n < 7:
                    soft_in(n + 1)
                soft_out(n)
                soft_T(n)
            layer_norm(2, h, 0, 4, 6)
            take_hT(4)
            route(1)
            experts(1)
            layer_norm(3, res, 4, 0, 2)


_INS = ['x', 'w_in_a', 'b_gates_a', 'mh_norm_a', 'w_out_a', 'w_kv_shared', 'w_q_b', 'sinks_b', 'w_out_b',
        'w_router', 'b_router', 'w_gu', 'w_down', 'ln_g', 'ln_b']


def kernel(**inputs):
    import numpy as _np
    import concourse.bacc as _bacc
    from concourse import mybir as _mybir
    from concourse.bass_utils import run_bass_kernel_spmd as _run

    nc = _bacc.Bacc("TRN2", target_bir_lowering=False, num_devices=1)
    arrays, args = {}, []
    for name in _INS:
        a = _np.ascontiguousarray(inputs[name])
        arrays[f"in_{name}"] = a
        args.append(nc.dram_tensor(f"in_{name}", a.shape, _mybir.dt.from_np(a.dtype), kind="ExternalInput").ap())
    freq = _np.float32(10000.0) ** (-_np.arange(0, DH, 2, dtype=_np.float32) / _np.float32(DH))
    ang = _np.arange(SEQ, dtype=_np.float32)[:, None] * freq[None, :]
    table = _np.stack([_np.cos(ang), _np.sin(ang)]).astype(_np.float32)
    arrays["rope"] = table
    args.append(nc.dram_tensor("rope", table.shape, F32, kind="ExternalInput").ap())
    args.append(nc.dram_tensor("out_0", (1, SEQ, D), F32, kind="ExternalOutput").ap())
    build(nc, *args)
    r = _run(nc, [arrays], core_ids=[0])
    return r.results[0]["out_0"]
```

```python
import concourse.bass as bass
from concourse import mybir
from contextlib import ExitStack

F32 = mybir.dt.float32
I32 = mybir.dt.int32
ACT = mybir.ActivationFunctionType
ALU = mybir.AluOpType
AX_X = mybir.AxisListType.X

SEQ, D = 256, 1024
P = 128
NT = SEQ // P
KC = D // P
HALF = 512
M_HEADS, M_V = 4, 256
M_QK = 128
QK_W, V_W = M_HEADS * M_QK, M_HEADS * M_V
A_HEADS, A_KV, DH, CHUNK = 16, 4, 64, 64
PAIRS = A_HEADS // 2
KV_W = A_KV * DH
EXPERTS, GROUPS, FF = 16, 4, 512
PER_GROUP = EXPERTS // GROUPS
FC = FF // P
SLOTS = 64
USED = 64
GW = 32 + M_HEADS
START = 2
U = 4
TURNS = EXPERTS // U
ALPHA = 4.0 ** 0.25
CAP = 15.0
LN_EPS, MH_EPS = 1e-5, 1e-6
LOW = -1.0e30
NG, ND = 4, 2
G_MIX = [0, 20]
G_EXP = [4, 22]
D_EXP = [0, 17]
D_KV = 16


def build(nc, x, w_in_a, b_gates_a, mh_norm_a, w_out_a, w_kv_shared, w_q_b, sinks_b, w_out_b,
          w_router, b_router, w_gu, w_down, ln_g, ln_b, rope, out):
    ctx = ExitStack()
    with ctx:
        def sb(name, shape, dt=F32):
            return ctx.enter_context(nc.sbuf_tensor(name, shape, dt))

        def sem(name):
            return ctx.enter_context(nc.semaphore(name))

        big = [sb(f"big{n}", [P, KC, D]) for n in range(NG)]
        small = [sb(f"small{n}", [P, FC, D]) for n in range(ND)]
        ident = sb("ident", [P, P])
        tri = sb("tri", [P, P])
        ones = sb("ones", [P, 1])
        zero = sb("zero", [P, 1])
        slot_no = sb("slot_no", [P, SLOTS])
        rank16 = sb("rank16", [P, EXPERTS])
        rank4 = rank16[:, EXPERTS - GROUPS:EXPERTS]
        rows = sb("rows", [9, D])
        h = sb("h", [P, NT, D])
        hT = sb("hT", [P, KC, SEQ])
        bufA = sb("bufA", [P, 2048])
        bufB = sb("bufB", [P, 2048])
        bufC = sb("bufC", [P, 1536])
        v_shift = sb("v_shift", [P, NT, KV_W])
        w_rt = sb("w_rt", [P, KC, EXPERTS])
        b_rt = sb("b_rt", [P, EXPERTS])
        sink = sb("sink", [P, A_HEADS])
        b_gate = sb("b_gate", [GW, 1])
        cs = sb("cs", [P, NT, DH])
        st = sb("st", [P, 160])

        w_gate = v_shift[:, :, :].rearrange("p t n -> p (t n)")[:, 0:KC * GW].rearrange("p (k n) -> p k n", k=KC)
        qkT = bufA[:, :].rearrange("p (g n) -> p g n", g=8)
        gate_o = bufA[:, :].rearrange("p (t n) -> p t n", t=NT)
        val = bufB[:, :].rearrange("p (t n) -> p t n", t=NT)
        wts = bufC[:, :].rearrange("p (h n) -> p h n", h=M_HEADS)
        lane = [bufC[0:M_HEADS, n * SEQ:(n + 1) * SEQ] for n in range(6)]
        tanh_rows = bufC[0:GW, 0:SEQ]
        kdup = bufB[:, 0:1024].rearrange("p (t g d n) -> p t g d n", t=NT, g=A_KV, d=2)
        q_rot = [bufA[:, 0:1024], small[D_KV % ND][:, 0, :]]
        qT = bufB[:, :].rearrange("p (j n) -> p j n", j=PAIRS)
        kT = bufC[:, 0:1024].rearrange("p (g n) -> p g n", g=A_KV)
        v_tok = bufC[:, 1024:1536].rearrange("p (t n) -> p t n", t=NT)
        prob = [bufA[:, n * 512:(n + 1) * 512] for n in range(2)]
        probT = [bufA[:, 1024 + n * 512:1024 + (n + 1) * 512] for n in range(2)]
        res = gate_o
        xe = [bufB[:, 0:1024].rearrange("p (k s) -> p k s", k=KC),
              hT[:, 4:8, :].rearrange("p k n -> p (k n)").rearrange("p (k s) -> p k s", k=KC)]
        ye = bufB[:, 1024:2048]
        pick = [bufC[:, n * 256:(n + 1) * 256].rearrange("p (t e s) -> p t e s", t=NT, e=2) for n in range(2)]
        pickg = bufC[:, 512:768].rearrange("p (t e s) -> p t e s", t=NT, e=2)
        act_g = [bufC[:, 768 + n * 256:768 + (n + 1) * 256] for n in range(2)]
        back = v_shift[:, 0, :]
        heT = bufC[:, 1280:1536]
        spill_w = hT[:, 0:4, :].rearrange("p k n -> p (k n)")

        r_logit = st[:, 0:32]
        r_prob = st[:, 32:64].rearrange("p (t e) -> p t e", t=NT)
        r_sel = st[:, 64:96].rearrange("p (t e) -> p t e", t=NT)
        r_a = st[:, 96:128].rearrange("p (t e) -> p t e", t=NT)
        r_s = st[:, 128:160]
        ro = bufC[:, 1280:1376].rearrange("p (a n) -> p a n", a=3)
        oh1 = ro[:, 0, :].rearrange("p (t e) -> p t e", t=NT)
        oh2 = ro[:, 1, :].rearrange("p (t e) -> p t e", t=NT)
        oh = ro[:, 2, :].rearrange("p (t e) -> p t e", t=NT)
        pos = sb("pos", [P, EXPERTS, NT])
        gate = sb("gate", [P, EXPERTS, NT])
        extra_f = sb("extra_f", [P, 4])
        extra = sb("extra", [P, 1], I32)
        ln = st[:, 0:40].rearrange("p (t n) -> p t n", t=NT)

        pb = [ctx.enter_context(nc.psum_tensor(f"pb{n}", [P, HALF], F32)) for n in range(8)]

        big_in = [[sem(f"big_in{n}_{q}") for q in range(4)] for n in range(NG)]
        small_in = [[sem(f"small_in{n}_{q}") for q in range(2)] for n in range(ND)]
        x_in = [sem(f"x_in{t}") for t in range(NT)]
        gates_w_in, params_in = sem("gates_w_in"), sem("params_in")
        gate_zero = sem("gate_zero")
        consts = sem("consts")
        turned = sem("turned")
        hT_dve, hT_act = sem("hT_dve"), sem("hT_act")
        qk_done, qk_sb = sem("qk_done"), sem("qk_sb")
        gates_done, gates_read = sem("gates_done"), sem("gates_read")
        v_done, v_sb = sem("v_done"), sem("v_sb")
        lanes_ready = sem("lanes_ready")
        small_T, small_sb = sem("small_T"), sem("small_sb")
        m_bcast, s_done = sem("m_bcast"), sem("s_done")
        w_arg, w_exp, w_masked, p_ready = sem("w_arg"), sem("w_exp"), sem("w_masked"), sem("p_ready")
        o_done, o_sb, mh_bcast = sem("o_done"), sem("o_sb"), sem("mh_bcast")
        den_done, den_inv = sem("den_done"), sem("den_inv")
        num_done, sq_done, hn_ready = sem("num_done"), sem("sq_done"), sem("hn_ready")
        a2d, d2a = sem("a2d"), sem("d2a")
        mix_done = sem("mix_done")
        ln_rows, ln_std_in, ln_std, ln_ready = sem("ln_rows"), sem("ln_std_in"), sem("ln_std"), sem("ln_ready")
        logits, rt_exp_in, rt_exp, chosen, placed, lists = (
            sem("logits"), sem("rt_exp_in"), sem("rt_exp"), sem("chosen"), sem("placed"), sem("lists"))
        pick_ready, pickg_ready = sem("pick_ready"), sem("pickg_ready")
        x_got, x_sb = sem("x_got"), sem("x_sb")
        gu_done, silu_done, he_ready = sem("gu_done"), sem("silu_done"), sem("he_ready")
        heT_done, heT_sb, back_sb = sem("heT_done"), sem("heT_sb"), sem("back_sb")
        mh_used, num_sb, std_ready, rms_in, rms_std, gated = (
            sem("mh_used"), sem("num_sb"), sem("std_ready"), sem("rms_in"), sem("rms_std"), sem("gated"))
        inv_ready = sem("inv_ready")
        y_done, y_sb = sem("y_done"), sem("y_sb")
        ov = [{n: sem(f"ov{l}_{n}") for n in ("w_in", "w_used", "pick", "x", "xs", "gu", "silu", "he", "t",
                                               "ts", "y", "ys", "z", "zs", "dve")} for l in range(2)]
        res_ready, mix_res = sem("res_ready"), sem("mix_res")
        kv_done, v_split, k_rot, q_done, q_rotd, kT_done, kT_sb, qT_done, qT_sb, q_moved = (
            sem("kv_done"), sem("v_split"), sem("k_rot"), sem("q_done"), sem("q_rotd"), sem("kT_done"),
            sem("kT_sb"), sem("qT_done"), sem("qT_sb"), sem("q_moved"))
        sc_done, mx_ready, e_done, es_done, pn_ready, pT_done, pT_sb, pv_done, outT_sb = (
            sem("sc_done"), sem("mx_ready"), sem("e_done"), sem("es_done"), sem("pn_ready"), sem("pT_done"),
            sem("pT_sb"), sem("pv_done"), sem("outT_sb"))
        shift_zero = sem("shift_zero")
        dch, ach = sem("dch"), sem("ach")
        stored = sem("stored")

        block = ctx.enter_context(nc.Block())

        def big_at(n):
            return big[n % NG], big_in[n % NG], n // NG + 1

        def small_at(n):
            return small[n % ND], small_in[n % ND], n // ND + 1

        SCB = [[[0, 1], [4, 5]], [[2, 3], [6, 7]]]
        SC_ORDER = [(t, par, jj) for t in range(NT) for jj in range(2) for par in range(2)]

        @block.sync
        def _(sp):
            def load_big(n, src):
                buf, sems, _ = big_at(n)
                v = src.rearrange("(k p) n -> p k n", p=P)
                for q in range(4):
                    sp.dma_start(buf[:, 2 * q:2 * q + 2, :], v[:, 2 * q:2 * q + 2, :]).then_inc(sems[q], 16)

            def load_small(n, src):
                buf, sems, _ = small_at(n)
                v = src.rearrange("(k p) n -> p k n", p=P)
                for q in range(2):
                    sp.dma_start(buf[:, 2 * q:2 * q + 2, :], v[:, 2 * q:2 * q + 2, :]).then_inc(sems[q], 16)

            for t in range(NT):
                sp.dma_start(h[:, t, :], x[0, t * P:(t + 1) * P, :]).then_inc(x_in[t], 16)
            w_in = w_in_a[0]
            for q in range(4):
                sp.dma_start(big[0][:, :, q * 256:(q + 1) * 256],
                             w_in[:, q * 256:(q + 1) * 256].rearrange("(k p) n -> p k n", p=P)
                             ).then_inc(big_in[0][q], 16)
            load_big(1, w_in[:, 1024:2048])
            load_big(2, w_in[:, 2048:3072])
            load_big(3, w_out_a[0])
            for l in range(2):
                G0, D0 = G_EXP[l], D_EXP[l]
                DONE = START + EXPERTS * l
                if l == 1:
                    sp.wait_ge(y_done, DONE - 1)
                    v = w_kv_shared.rearrange("(k p) n -> p k n", p=P)
                    buf, sems, _ = small_at(D_KV)
                    bv = buf[:, :, :].rearrange("p a (b n) -> p (a b) n", b=2)
                    for q in range(2):
                        sp.dma_start(bv[:, 4 * q:4 * q + 4, :], v[:, 4 * q:4 * q + 4, :]).then_inc(sems[q], 16)
                    load_big(G_MIX[1] + 1, w_out_b[0])
                if l == 0:
                    sp.wait_ge(qk_done, 8)
                else:
                    sp.wait_ge(gu_done, DONE - 1)
                load_big(G0, w_gu[l, 0])
                if l == 0:
                    sp.wait_ge(v_done, 4)
                else:
                    sp.wait_ge(gu_done, DONE)
                load_big(G0 + 1, w_gu[l, 1])
                if l == 1:
                    sp.wait_ge(y_done, DONE)
                with sp.Fori(0, TURNS - 1) as i:
                    for u in range(U):
                        if l == 1 and u == 1:
                            sp.wait_ge(qT_done, 4)
                        sp.wait_ge(y_done, i * U + (DONE + u - 1))
                        load_small(D0 + u, w_down[l, bass.ds(i * U + u, 1)].rearrange("a k n -> (a k) n"))
                        if u == 0:
                            sp.wait_ge(q_done if l else o_done, 4)
                        if u == 1:
                            sp.wait_ge(mix_done, 4 + 8 * l)
                        sp.wait_ge(gu_done, i * U + (DONE + u - 1))
                        load_big(G0 + u + 2, w_gu[l, bass.ds(i * U + (u + 2), 1)].rearrange("a k n -> (a k) n"))
                for e in range(EXPERTS - U, EXPERTS):
                    sp.wait_ge(y_done, DONE + e - 1)
                    load_small(D0 + e, w_down[l, e])
                    if e + 2 < EXPERTS:
                        sp.wait_ge(gu_done, DONE + e - 1)
                        load_big(G0 + e + 2, w_gu[l, e + 2])
                    elif e + 2 == EXPERTS and l == 0:
                        sp.wait_ge(gu_done, DONE + e - 1)
                        load_big(G_MIX[1], w_q_b[0])
                s = ov[l]
                sp.wait_ge(lists, l + 1)
                rounds = sp.value_load(extra[0:1, 0:1], min_val=0, max_val=3)
                with sp.If(rounds > 0):
                    sp.wait_ge(res_ready, 4 * (l + 1))
                    with sp.Fori(0, rounds) as j:
                        with sp.Fori(0, EXPERTS) as e:
                            n0 = (j * EXPERTS + e) * (KC + FC)
                            for k in range(KC + FC):
                                sp.wait_ge(s["w_used"], n0 + (k + START))
                                src = (w_gu[l, bass.ds(e, 1), k * P:(k + 1) * P, :] if k < KC else
                                       w_down[l, bass.ds(e, 1), (k - KC) * P:(k - KC + 1) * P, :])
                                sp.dma_start(spill_w, src.rearrange("a p n -> (a p) n")).then_inc(s["w_in"], 16)
            for t in range(NT):
                sp.wait_ge(ln_ready, 3 * NT + t + 1)
                sp.dma_start(out[0, t * P:(t + 1) * P, :], h[:, t, :]).then_inc(stored, 16)
            sp.wait_ge(stored, 16 * NT)

        @block.gpsimd
        def _(pool):
            nc.gpsimd.memset(ones[:, :], 1.0).then_inc(consts, 1)
            nc.gpsimd.memset(ident[:, :], 0.0).then_inc(consts, 1)
            nc.gpsimd.memset(zero[:, :], 0.0).then_inc(consts, 1)
            pool.wait_ge(consts, 3)
            nc.gpsimd.affine_select(out=ident[:, :], in_=ident[:, :], compare_op=ALU.not_equal, fill=1.0, base=0,
                                    pattern=[[-1, P]], channel_multiplier=1).then_inc(consts, 1)
            nc.gpsimd.affine_select(out=tri[:, :], in_=ones[:, 0:1].to_broadcast([P, P]), compare_op=ALU.is_ge, fill=0.0, base=0,
                                    pattern=[[1, P]], channel_multiplier=-1).then_inc(consts, 1)
            nc.gpsimd.iota(slot_no[:, :], pattern=[[1, SLOTS]], base=0, channel_multiplier=0,
                           allow_small_or_imprecise_dtypes=True).then_inc(consts, 1)
            nc.gpsimd.iota(rank16[:, :], pattern=[[-1, EXPERTS]], base=EXPERTS, channel_multiplier=0,
                           allow_small_or_imprecise_dtypes=True).then_inc(consts, 1)
            if USED < SLOTS:
                pool.wait_ge(consts, 7)
                nc.gpsimd.memset(slot_no[:, USED:SLOTS], -1.0e6).then_inc(consts, 1)
            nc.gpsimd.memset(w_gate, 0.0).then_inc(gate_zero, 1)
            nc.gpsimd.memset(b_gate[:, :], 0.0).then_inc(gate_zero, 1)
            for hd in range(M_HEADS):
                pool.wait_ge(w_exp, hd + 1)
                for blk in range(2):
                    d = wts[:, hd, 256 * blk:256 * blk + P]
                    nc.gpsimd.tensor_tensor(d, d, tri[:, :], ALU.mult).then_inc(w_masked, 1)
            for n in range(8):
                pool.wait_ge(inv_ready, n + 1)
                o = 20 * (n % 4)
                p3 = prob[n % 2].rearrange("p (s k) -> p s k", s=4)
                nc.gpsimd.tensor_tensor(p3, p3, st[:, o + 16:o + 20].rearrange("p (s o) -> p s o", o=1).to_broadcast([P, 4, P]),
                                        ALU.mult).then_inc(pn_ready, 1)

        NCONST = 7 + (USED < SLOTS)

        @block.tensor
        def _(pe):
            mm = nc.tensor.matmul

            def wait_big(n, q, i=0):
                _, sems, fill = big_at(n)
                pe.wait_ge(sems[q], i * 16 + 16 * fill)

            def turn(src, n, t, j, bank0):
                for kk in range(4):
                    k = 4 * j + kk
                    last = nc.tensor.transpose(pb[bank0 + 2 * t + j][:, kk * P:(kk + 1) * P],
                                               src[:, t, k * P:(k + 1) * P], ident[:, :])
                last.then_inc(turned, 1)

            def wait_hT(n, t):
                pe.wait_ge(hT_dve, 2 * n + t + 1)
                pe.wait_ge(hT_act, 2 * n + t + 1)

            def project(n, t, c, bank, done):
                w = big_at(n)[0]
                for k in range(KC):
                    if t == 0 and c == 0 and k % 2 == 0:
                        wait_big(n, k // 2)
                    last = mm(pb[bank][:, :], hT[:, k, t * P:(t + 1) * P], w[:, k, c * HALF:(c + 1) * HALF],
                              start=k == 0, stop=k == KC - 1)
                last.then_inc(done, 1)

            def bcast_row(bank, row, c):
                return mm(pb[bank][:, :], ident[0:9, row:row + 1].to_broadcast([9, P]),
                          rows[:, c * HALF:(c + 1) * HALF], start=True, stop=True)

            def ln_bcast(l, which, g0, b0):
                r = 2 * l + which
                for c in range(2):
                    bcast_row(g0 + c, r, c)
                    last = bcast_row(b0 + c, 4 + r, c)
                last.then_inc(ln_rows, 1)

            for first in (x_got, gu_done, heT_done, y_done, ov[0]["w_used"], ov[1]["w_used"]):
                pe.sem_inc(first, START)

            pe.wait_ge(consts, NCONST)
            for t in range(NT):
                pe.wait_ge(x_in[t], 16)
                for j in range(2):
                    turn(h, 0, t, j, 4)
            wait_hT(0, 1)
            for g in range(8):
                if g % 2 == 0:
                    wait_big(0, g // 2)
                for k in range(KC):
                    last = mm(pb[g // 2][:, (g % 2) * SEQ:(g % 2 + 1) * SEQ], big[0][:, k, g * P:(g + 1) * P],
                              hT[:, k, :], start=k == 0, stop=k == KC - 1)
                last.then_inc(qk_done, 1)
            pe.wait_ge(gates_w_in, 64)
            for k in range(KC):
                last = mm(pb[4][0:GW, 0:SEQ], w_gate[:, k, :], hT[:, k, :], start=k == 0, stop=k == KC - 1)
            last.then_inc(gates_done, 1)
            for t, c, bank in ((0, 0, 5), (0, 1, 6), (1, 0, 7), (1, 1, 4)):
                if bank == 4:
                    pe.wait_ge(gates_read, 1)
                project(1, t, c, bank, v_done)
            pe.wait_ge(lanes_ready, 1)
            pe.wait_ge(v_sb, 4)
            for n, ln_no in enumerate((3, 5)):
                for t in range(NT):
                    c = (2 * n + t) * M_HEADS
                    last = nc.tensor.transpose(pb[4][:, c:c + M_HEADS], lane[ln_no][:, t * P:(t + 1) * P],
                                               ident[0:M_HEADS, 0:M_HEADS])
            last.then_inc(small_T, 1)
            for hd in range(M_HEADS):
                mm(pb[5 + hd // 2][:, (hd % 2) * SEQ:(hd % 2 + 1) * SEQ],
                   ident[0:M_HEADS, hd:hd + 1].to_broadcast([M_HEADS, P]), lane[4], start=True, stop=True
                   ).then_inc(m_bcast, 1)
            pe.wait_ge(qk_sb, 8)
            for hd in range(M_HEADS):
                mm(pb[hd][:, 0:SEQ], qkT[:, 4 + hd, 0:P], qkT[:, hd, :], start=True, stop=True)
                mm(pb[hd][:, SEQ:SEQ + P], qkT[:, 4 + hd, P:SEQ], qkT[:, hd, P:SEQ], start=True, stop=True
                   ).then_inc(s_done, 1)
            project(2, 0, 0, 7, o_done)
            pe.wait_ge(small_sb, 1)
            project(2, 0, 1, 4, o_done)
            pe.wait_ge(o_sb, 1)
            pe.wait_ge(p_ready, M_HEADS)
            for t in range(NT):
                for hd in range(M_HEADS):
                    c = t * M_HEADS + hd
                    for s in range(t + 1):
                        lo = (s + t) * P
                        last = mm(pb[7][:, c:c + 1], wts[:, hd, lo:lo + P], ones[:, 0:1], start=s == 0, stop=s == t)
            last.then_inc(den_done, 1)
            for hd in range(M_HEADS):
                for t in range(NT):
                    for s in range(t + 1):
                        lo = (s + t) * P
                        last = mm(pb[hd][:, t * M_V:(t + 1) * M_V], wts[:, hd, lo:lo + P],
                                  val[:, s, hd * M_V:(hd + 1) * M_V], start=s == 0, stop=s == t)
                last.then_inc(num_done, 1)
            pe.wait_ge(params_in, 16 * 8)
            pe.wait_ge(o_sb, 2)
            pe.wait_ge(den_inv, 1)
            for c, bank in ((0, 7), (1, 4)):
                last = bcast_row(bank, 8, c)
            last.then_inc(mh_bcast, 1)
            pe.wait_ge(w_arg, 2 * M_HEADS)
            project(2, 1, 0, 5, o_done)
            pe.wait_ge(num_sb, NT * M_HEADS)
            pe.wait_ge(gated, 1)
            for j in range(2):
                turn(val, 1, 0, j, 0)
            project(2, 1, 1, 6, o_done)
            wait_hT(1, 0)
            for c in range(2):
                project(3, 0, c, c, mix_done)
            pe.wait_ge(gated, 2)
            for j in range(2):
                turn(val, 1, 1, j, 0)
            ln_bcast(0, 0, 4, 6)
            wait_hT(1, 1)
            for c in range(2):
                project(3, 1, c, 2 + c, mix_done)

            PAIRS_E = EXPERTS // 2

            def moe(l):
                for t in range(NT):
                    pe.wait_ge(ln_ready, 2 * NT * l + t + 1)
                    for j in range(2):
                        turn(h, 2 + 2 * l, t, j, 0)
                for t in range(NT):
                    wait_hT(2 + 2 * l, t)
                    for k in range(KC):
                        last = mm(pb[0][:, t * EXPERTS:(t + 1) * EXPERTS], hT[:, k, t * P:(t + 1) * P],
                                  w_rt[:, k, :], start=k == 0, stop=k == KC - 1)
                last.then_inc(logits, 1)
                for b in range(4):
                    mm(pb[4 + b][:, :], zero[:, 0:1].to_broadcast([P, P]), big_zero(b), start=True, stop=False,
                       skip_group_check=True)
                pe.wait_ge(chosen, l + 1)
                mm(pb[1][:, 0:16], tri[:, :], oh[:, 0, :], start=True, stop=True)
                mm(pb[1][:, 16:32], ones[:, 0:1].to_broadcast([P, P]), oh[:, 0, :], start=True, stop=False)
                mm(pb[1][:, 16:32], tri[:, :], oh[:, 1, :], start=False, stop=True)
                mm(pb[1][:, 32:48], ones[:, 0:1].to_broadcast([P, P]), oh[:, 0, :], start=True, stop=False)
                mm(pb[1][:, 32:48], ones[:, 0:1].to_broadcast([P, P]), oh[:, 1, :], start=False, stop=True).then_inc(placed, 1)

                def gather(m, P0, ks):
                    for k in ks:
                        if k == 0:
                            pe.wait_ge(pick_ready, P0 + (m + 1))
                        if k % 4 == 0:
                            pe.wait_ge(x_sb, (P0 + m) * 2 + (k // 4 - START))
                        for t in range(NT):
                            last = mm(pb[1][:, (k % 4) * P:(k % 4 + 1) * P], h[:, t, k * P:(k + 1) * P],
                                      pick[m % 2][:, t, :, :].rearrange("p e s -> p (e s)"),
                                      start=t == 0, stop=t == NT - 1)
                        if k % 4 == 3:
                            last.then_inc(x_got, 1)

                def gate_up(u, i, E0, P0):
                    n = G_EXP[l] + u
                    w = big_at(n)[0]
                    if u % 2 == 0:
                        pe.wait_ge(x_sb, (P0 + u // 2) * 2 + (2 - START))
                    pe.wait_ge(he_ready, E0 + u)
                    for k in range(KC):
                        if k % 2 == 0:
                            wait_big(n, k // 2, i)
                        for c in range(2):
                            last = mm(pb[0][c * 64:(c + 1) * 64, :].rearrange("p (a n) -> p a n", a=2),
                                      xe[u // 2][:, k, (u % 2) * SLOTS:(u % 2 + 1) * SLOTS],
                                      w[:, k, :].rearrange("p (a c n) -> p c a n", a=2, c=2)[:, c],
                                      start=k == 0, stop=k == KC - 1)
                    last.then_inc(gu_done, 1)

                def inner_T(u, E0, P0):
                    pe.wait_ge(he_ready, E0 + (u + 1))
                    pe.wait_ge(heT_sb, E0 + u)
                    if u % 2:
                        pe.wait_ge(pickg_ready, P0 + (u // 2 + 1))
                    else:
                        pe.wait_ge(back_sb, P0 + u // 2)
                    for j in range(2):
                        last = nc.tensor.transpose(pb[3][:, j * P:(j + 1) * P], act_g[u % 2][:, j * P:(j + 1) * P],
                                                   ident[:, :])
                    if u % 2:
                        for t in range(NT):
                            last = nc.tensor.transpose(pb[3][:, (2 + t) * P:(3 + t) * P],
                                                       pickg[:, t, :, :].rearrange("p e s -> p (e s)"), ident[:, :])
                    last.then_inc(heT_done, 1)

                def down(u, i, E0):
                    pe.wait_ge(heT_sb, E0 + (u + 1))
                    n = D_EXP[l] + u
                    w, sems, fill = small_at(n)
                    pe.wait_ge(y_sb, (E0 + u) * 2 - START)
                    for j in range(2):
                        for hf in range(2):
                            kk = 2 * hf + j
                            if j == 0:
                                pe.wait_ge(sems[hf], i * 32 + 16 * fill)
                            for c in range(2):
                                last = mm(pb[2][c * 64:(c + 1) * 64, :],
                                          heT[:, j * P + hf * 64:j * P + (hf + 1) * 64],
                                          w[:, kk, c * HALF:(c + 1) * HALF],
                                          start=(j, hf) == (0, 0), stop=(j, hf) == (1, 1))
                    last.then_inc(y_done, 1)

                def scatter(m, E0, P0, last_one):
                    pe.wait_ge(y_sb, (E0 + 2 * m) * 2 + (4 - START))
                    pe.wait_ge(back_sb, P0 + (m + 1))
                    for t in range(NT):
                        for c in range(2):
                            ins = mm(pb[4 + 2 * t + c][:, :], back[:, t * P:(t + 1) * P],
                                     ye[:, c * HALF:(c + 1) * HALF], start=False, stop=last_one,
                                     skip_group_check=True)
                            if last_one:
                                ins.then_inc(mix_done, 1)

                def one_turn(i, final):
                    E0 = EXPERTS * l + i * U + START
                    P0 = PAIRS_E * l + i * 2 + START
                    for m in range(2):
                        a, b = 2 * m, 2 * m + 1
                        over = final and m == 1
                        gate_up(a, i, E0, P0)
                        if not over:
                            gather(m + 1, P0, (0, 1))
                        inner_T(a, E0, P0)
                        if not over:
                            gather(m + 1, P0, (2, 3))
                        down(a, i, E0)
                        gate_up(b, i, E0, P0)
                        if over:
                            bcast_row(1, 2 * l + 1, 0)
                        else:
                            gather(m + 1, P0, (4, 5))
                        inner_T(b, E0, P0)
                        if over:
                            bcast_row(0, 2 * l + 1, 1)
                        else:
                            gather(m + 1, P0, (6,))
                        down(b, i, E0)
                        if over:
                            pe.wait_ge(back_sb, P0 + (m + 1))
                            bcast_row(3, 4 + 2 * l + 1, 0)
                        else:
                            gather(m + 1, P0, (7,))
                        scatter(m, E0, P0, over)

                gather(0, PAIRS_E * l + START, range(KC))
                with pe.Fori(0, TURNS - 1) as i:
                    one_turn(i, False)
                one_turn(TURNS - 1, True)
                overflow(l)
                bcast_row(2, 4 + 2 * l + 1, 1).then_inc(ln_rows, 1)

            def overflow(l):
                s = ov[l]
                rounds = pe.value_load(extra[0:1, 0:1], min_val=0, max_val=3)
                with pe.If(rounds > 0):
                    pe.wait_ge(res_ready, 4 * (l + 1))
                    with pe.Fori(0, rounds) as j:
                        with pe.Fori(0, EXPERTS) as e:
                            n = j * EXPERTS + e
                            pe.wait_ge(s["pick"], n + 1)
                            for half in range(2):
                                if half:
                                    pe.wait_ge(s["xs"], n * 2 + 1)
                                for k in range(4 * half, 4 * half + 4):
                                    for t in range(NT):
                                        last = mm(pb[1][:, (k % 4) * P:(k % 4 + 1) * P], h[:, t, k * P:(k + 1) * P],
                                                  pick[0][:, t, :, :].rearrange("p e s -> p (e s)"),
                                                  start=t == 0, stop=t == NT - 1)
                                last.then_inc(s["x"], 1)
                            pe.wait_ge(s["xs"], n * 2 + 2)
                            for k in range(KC):
                                pe.wait_ge(s["w_in"], (n * (KC + FC) + (k + 1)) * 16)
                                for c in range(2):
                                    last = mm(pb[0][c * 64:(c + 1) * 64, :].rearrange("p (a n) -> p a n", a=2),
                                              xe[0][:, k, 0:SLOTS],
                                              spill_w.rearrange("p (a c n) -> p c a n", a=2, c=2)[:, c],
                                              start=k == 0, stop=k == KC - 1)
                                last.then_inc(s["w_used"], 1)
                            pe.wait_ge(s["he"], n + 1)
                            for jj in range(2):
                                nc.tensor.transpose(pb[3][:, jj * P:(jj + 1) * P], act_g[0][:, jj * P:(jj + 1) * P],
                                                    ident[:, :])
                            for t in range(NT):
                                last = nc.tensor.transpose(pb[3][:, (2 + t) * P:(3 + t) * P],
                                                           pickg[:, t, :, :].rearrange("p e s -> p (e s)"), ident[:, :])
                            last.then_inc(s["t"], 1)
                            pe.wait_ge(s["ts"], n + 1)
                            for kk in range(FC):
                                pe.wait_ge(s["w_in"], (n * (KC + FC) + (KC + kk + 1)) * 16)
                                hf, jj = kk // 2, kk % 2
                                for c in range(2):
                                    last = mm(pb[2][c * 64:(c + 1) * 64, :],
                                              heT[:, jj * P + hf * 64:jj * P + (hf + 1) * 64],
                                              spill_w[:, c * HALF:(c + 1) * HALF], start=kk == 0, stop=kk == FC - 1)
                                last.then_inc(s["w_used"], 1)
                            pe.wait_ge(s["ys"], n + 1)
                            for t in range(NT):
                                for c in range(2):
                                    last = mm(pb[4 + 2 * t + c][:, :], back[0:SLOTS, t * P:(t + 1) * P],
                                              ye[0:SLOTS, c * HALF:(c + 1) * HALF], start=True, stop=True)
                            last.then_inc(s["z"], 1)
                            pe.wait_ge(s["zs"], n * 4 + (4 + START))
                    bcast_row(1, 2 * l + 1, 0)
                    bcast_row(0, 2 * l + 1, 1)
                    bcast_row(3, 4 + 2 * l + 1, 0)

            def big_zero(b):
                return zero[:, 0:1].to_broadcast([P, HALF])

            moe(0)

            for t in range(NT):
                pe.wait_ge(ln_ready, NT + t + 1)
                for j in range(2):
                    turn(h, 3, t, j, 4)
            kvw, kvs, kvf = small_at(D_KV)
            kvw = kvw[:, :, :].rearrange("p a (b n) -> p (a b) n", b=2)
            for t in range(NT):
                wait_hT(3, t)
                for k in range(KC):
                    if t == 0 and k % 4 == 0:
                        pe.wait_ge(kvs[k // 4], 16 * kvf)
                    last = mm(pb[t][:, :], hT[:, k, t * P:(t + 1) * P], kvw[:, k, :], start=k == 0, stop=k == KC - 1)
                last.then_inc(kv_done, 1)
            for c in range(2):
                project(G_MIX[1], 0, c, 2 + c, q_done)
            pe.wait_ge(k_rot, NT)
            for g in range(A_KV):
                for t in range(NT):
                    c = (g % 2) * SEQ + t * P
                    last = nc.tensor.transpose(pb[4 + g // 2][:, c:c + P],
                                               kdup[:, t, g, :, :].rearrange("p d n -> p (d n)"), ident[:, :])
                if g % 2:
                    last.then_inc(kT_done, 1)

            def turn_q(t):
                for jj in range(2):
                    pe.wait_ge(q_rotd, 2 * t + jj + 1)
                    if t:
                        pe.wait_ge(qT_sb, 2)
                    for n in range(4):
                        j = 4 * jj + n
                        last = nc.tensor.transpose(pb[6 + jj][:, n * P:(n + 1) * P], q_rot[t][:, j * P:(j + 1) * P],
                                                   ident[:, :])
                    last.then_inc(qT_done, 1)

            def score(t):
                pe.wait_ge(qT_sb, 2 * t + 2)
                for (tt, par, jj) in SC_ORDER:
                    if tt != t:
                        continue
                    b = SCB[t][par][jj]
                    for n in range(4):
                        j = 4 * jj + n
                        for ci in range(2):
                            c = 2 * t + ci
                            lo = max(0, c - 1) * CHUNK
                            hi = (c + 1) * CHUNK
                            last = mm(pb[b][ci * 64:(ci + 1) * 64, (n + 1) * P - (hi - lo):(n + 1) * P],
                                      qT[par * 64:(par + 1) * 64, j, c * CHUNK:(c + 1) * CHUNK],
                                      kT[par * 64:(par + 1) * 64, j // 2, lo:hi], start=True, stop=True)
                    last.then_inc(sc_done, 1)

            def attend(n0):
                for n in (n0, n0 + 1):
                    t, par, jj = SC_ORDER[n]
                    pe.wait_ge(pn_ready, n + 1)
                    for s in range(4):
                        last = nc.tensor.transpose(pb[SCB[t][par][jj]][:, s * P:(s + 1) * P],
                                                   prob[n % 2][:, s * P:(s + 1) * P], ident[:, :])
                    last.then_inc(pT_done, 1)
                for n in (n0, n0 + 1):
                    t, par, jj = SC_ORDER[n]
                    pe.wait_ge(pT_sb, n + 1)
                    pv = probT[n % 2].rearrange("p (s q) -> p s q", s=4)
                    o = pb[SCB[t][0][jj]][par * 64:(par + 1) * 64, :].rearrange("p (s q) -> p s q", s=4)
                    for gg in range(2):
                        g = 2 * jj + gg
                        for ci in range(2):
                            vw = v_tok if ci else v_shift
                            last = mm(o[:, 2 * gg:2 * gg + 2, ci * 64:(ci + 1) * 64], vw[:, t, g * DH:(g + 1) * DH],
                                      pv[:, 2 * gg:2 * gg + 2, ci * 64:(ci + 1) * 64], start=True, stop=True)
                    last.then_inc(pv_done, 1)

            turn_q(0)
            pe.wait_ge(kT_sb, 2)
            score(0)
            project(G_MIX[1], 1, 0, 2, q_done)
            attend(0)
            project(G_MIX[1], 1, 1, 3, q_done)
            attend(2)
            turn_q(1)
            score(1)
            wo = G_MIX[1] + 1
            pe.wait_ge(outT_sb, 2)
            project(wo, 0, 0, 0, mix_done)
            attend(4)
            project(wo, 0, 1, 1, mix_done)
            attend(6)
            ln_bcast(1, 0, 4, 6)
            pe.wait_ge(outT_sb, 4)
            for c in range(2):
                project(wo, 1, c, 2 + c, mix_done)
            moe(1)

        @block.scalar
        def _(act):
            A = nc.scalar.activation
            n_ach = [0]

            def link(ins):
                n_ach[0] += 1
                ins.then_inc(ach, 1)
                act.wait_ge(ach, n_ach[0])

            for first in (x_sb, silu_done):
                act.sem_inc(first, START)

            act.wait_ge(gate_zero, 2)
            for g in range(2):
                w4 = w_in_a[0, :, 3072 + g * M_HEADS:3072 + (g + 1) * M_HEADS]
                act.dma_start(w_gate[:, :, 32 * g:32 * g + M_HEADS], w4.rearrange("(k p) n -> p k n", p=P)).then_inc(gates_w_in, 16)
                act.dma_start(b_gate[32 * g:32 * g + M_HEADS, :],
                              b_gates_a[0, g * M_HEADS:(g + 1) * M_HEADS].rearrange("(h o) -> h o", o=1)).then_inc(gates_w_in, 16)
            act.dma_start(rows[0:4, :], ln_g.rearrange("l w n -> (l w) n")).then_inc(params_in, 16)
            act.dma_start(rows[4:8, :], ln_b.rearrange("l w n -> (l w) n")).then_inc(params_in, 16)
            act.dma_start(rows[8:9, :], mh_norm_a).then_inc(params_in, 16)
            act.dma_start(w_rt[:, :, :], w_router.rearrange("(k p) n -> p k n", p=P)).then_inc(params_in, 16)
            act.dma_start(b_rt[:, :], b_router.rearrange("(a n) -> a n", a=1).to_broadcast([P, EXPERTS])).then_inc(params_in, 16)
            act.dma_start(sink[:, :], sinks_b.to_broadcast([P, A_HEADS])).then_inc(params_in, 16)
            for a in range(2):
                act.dma_start(cs[:, :, a * 32:(a + 1) * 32], rope[a].rearrange("(t p) n -> p t n", p=P)).then_inc(params_in, 16)

            def take_hT(n, t, bank0):
                act.wait_ge(turned, 4 * n + 2 * t + 2)
                A(hT[:, 4:8, t * P:(t + 1) * P], pb[bank0 + 2 * t + 1][:, :].rearrange("p (k n) -> p k n", k=4),
                  ACT.Copy).then_inc(hT_act, 1)

            def ln_std_part(n, t):
                act.wait_ge(ln_std_in, NT * n + t + 1)
                A(ln[:, t, 15:16], ln[:, t, 14:15], ACT.Sqrt).then_inc(ln_std, 1)

            for t in range(NT):
                take_hT(0, t, 4)
            for g in range(8):
                act.wait_ge(qk_done, 2 * (g // 2) + 2)
                A(qkT[:, g, :], pb[g // 2][:, (g % 2) * SEQ:(g % 2 + 1) * SEQ], ACT.Copy,
                  scale=1.0 if g < 4 else float(M_QK) ** -0.5).then_inc(qk_sb, 1)
            act.wait_ge(gates_done, 1)
            act.wait_ge(d2a, 1)
            A(tanh_rows, pb[4][0:GW, 0:SEQ], ACT.Tanh, bias=b_gate[:, 0:1], scale=1.0 / CAP).then_inc(gates_read, 1)
            act.wait_ge(gates_read, 1)
            link(A(lane[2], tanh_rows[32:GW, :], ACT.Exp, scale=-CAP))
            A(lane[2], lane[2], ACT.Ln, bias=ones[0:M_HEADS, 0:1]).then_inc(a2d, 1)
            for n, bank in enumerate((5, 6, 7, 4)):
                act.wait_ge(v_done, n + 1)
                A(val[:, n // 2, (n % 2) * HALF:(n % 2 + 1) * HALF], pb[bank][:, :], ACT.Copy).then_inc(v_sb, 1)
            act.wait_ge(d2a, 2)
            A(st[:, 8:16], st[:, 8:16], ACT.Exp).then_inc(a2d, 1)
            for hd in range(M_HEADS):
                act.wait_ge(w_arg, 2 * hd + 2)
                A(wts[:, hd, :], wts[:, hd, :], ACT.Exp).then_inc(w_exp, 1)

            def o_gate(n, bank):
                act.wait_ge(o_done, n + 1)
                A(gate_o[:, n // 2, (n % 2) * HALF:(n % 2 + 1) * HALF], pb[bank][:, :], ACT.Sigmoid).then_inc(o_sb, 1)
            act.wait_ge(s_done, M_HEADS)
            o_gate(0, 7)
            o_gate(1, 4)
            act.wait_ge(den_inv, 1)
            for hd in range(M_HEADS):
                act.wait_ge(num_done, hd + 1)
                for t in range(NT):
                    c = t * M_HEADS + hd
                    A(wts[:, hd, t * P:t * P + M_V], pb[hd][:, t * M_V:(t + 1) * M_V], ACT.Square,
                      scale=st[:, 16 + c:17 + c], accum_out=st[:, 24 + c:25 + c]).then_inc(sq_done, 1)
                    act.wait_ge(sq_done, hd * 2 + t + 1)
            act.wait_ge(rms_in, 1)
            A(st[:, 32:40], st[:, 32:40], ACT.Sqrt).then_inc(rms_std, 1)
            act.wait_ge(std_ready, 1)
            for t in range(NT):
                for hd in range(M_HEADS):
                    c = 40 + t * M_HEADS + hd
                    A(val[:, t, hd * M_V:(hd + 1) * M_V], pb[hd][:, t * M_V:(t + 1) * M_V], ACT.Copy,
                      scale=st[:, c:c + 1]).then_inc(num_sb, 1)
            o_gate(2, 5)
            take_hT(1, 0, 0)
            o_gate(3, 6)
            take_hT(1, 1, 0)
            for t in range(NT):
                ln_std_part(0, t)

            def moe(l):
                for t in range(NT):
                    take_hT(2 + 2 * l, t, 0)
                act.wait_ge(rt_exp_in, l + 1)
                A(r_logit, r_logit, ACT.Exp).then_inc(rt_exp, 1)

                def take_x(m, P0, half):
                    act.wait_ge(x_got, (P0 + m) * 2 + (half + 1 - START))
                    A(xe[m % 2][:, 4 * half:4 * half + 4, :].rearrange("p k s -> p (k s)"), pb[1][:, :], ACT.Copy
                      ).then_inc(x_sb, 1)

                def take_y(u, E0):
                    p = (u % 2) * 64
                    act.wait_ge(y_done, E0 + (u + 1))
                    A(ye[p:p + 64, HALF:2 * HALF], pb[2][64:128, :], ACT.Copy).then_inc(y_sb, 1)

                def silu(u, E0):
                    act.wait_ge(gu_done, E0 + (u + 1))
                    A(act_g[u % 2], pb[0][:, 0:256], ACT.Silu).then_inc(silu_done, 1)

                def one_turn(i, final):
                    E0 = EXPERTS * l + i * U + START
                    P0 = EXPERTS // 2 * l + i * 2 + START
                    for m in range(2):
                        over = final and m == 1
                        silu(2 * m, E0)
                        if not over:
                            take_x(m + 1, P0, 0)
                        take_y(2 * m, E0)
                        silu(2 * m + 1, E0)
                        take_y(2 * m + 1, E0)
                        if not over:
                            take_x(m + 1, P0, 1)

                for half in range(2):
                    take_x(0, EXPERTS // 2 * l + START, half)
                with act.Fori(0, TURNS - 1) as i:
                    one_turn(i, False)
                one_turn(TURNS - 1, True)
                s = ov[l]
                rounds = act.value_load(extra[0:1, 0:1], min_val=0, max_val=3)
                with act.If(rounds > 0):
                    with act.Fori(0, rounds) as j:
                        with act.Fori(0, EXPERTS) as e:
                            n = j * EXPERTS + e
                            for half in range(2):
                                act.wait_ge(s["x"], n * 2 + (half + 1))
                                A(xe[0][:, 4 * half:4 * half + 4, :].rearrange("p k s -> p (k s)"), pb[1][:, :], ACT.Copy
                                  ).then_inc(s["xs"], 1)
                            act.wait_ge(s["w_used"], n * (KC + FC) + (KC + START))
                            A(act_g[0], pb[0][:, 0:256], ACT.Silu).then_inc(s["silu"], 1)
                for t in range(NT):
                    ln_std_part(2 * l + 1, t)

            moe(0)

            for t in range(NT):
                take_hT(3, t, 4)
            act.wait_ge(shift_zero, 1)
            for t in range(NT):
                act.wait_ge(kv_done, t + 1)
                A(v_tok[:, t, :], pb[t][:, KV_W:2 * KV_W], ACT.Copy)
                if t == 0:
                    A(v_shift[0:64, 1, :], pb[0][64:128, KV_W:2 * KV_W], ACT.Copy)
                A(v_shift[64:128, t, :], pb[t][0:64, KV_W:2 * KV_W], ACT.Copy).then_inc(v_split, 1)
            for b in range(2):
                act.wait_ge(kT_done, b + 1)
                A(kT[:, 2 * b:2 * b + 2, :].rearrange("p g n -> p (g n)"), pb[4 + b][:, :], ACT.Copy).then_inc(kT_sb, 1)

            def take_qT(t):
                for jj in range(2):
                    act.wait_ge(qT_done, 2 * t + jj + 1)
                    A(qT[:, 4 * jj:4 * jj + 4, t * P:(t + 1) * P], pb[6 + jj][:, :].rearrange("p (j n) -> p j n", j=4),
                      ACT.Copy).then_inc(qT_sb, 1)

            def exps(n):
                t, par, jj = SC_ORDER[n]
                b = SCB[t][par][jj]
                act.wait_ge(mx_ready, n + 1)
                if n >= 2:
                    act.wait_ge(pT_done, n - 1)
                o = 20 * (n % 4)
                for s in range(4):
                    A(prob[n % 2][:, s * P:(s + 1) * P], pb[b][:, s * P:(s + 1) * P], ACT.Exp,
                      bias=st[:, o + 4 + s:o + 5 + s], scale=float(DH) ** -0.5, accum_out=st[:, o + 12 + s:o + 13 + s]
                      ).then_inc(e_done, 1)
                A(st[:, o + 8:o + 12], st[:, o + 8:o + 12], ACT.Exp).then_inc(e_done, 1)

            take_qT(0)
            for n in range(4):
                exps(n)
            take_qT(1)
            for n in range(4, 8):
                exps(n)
            for t in range(NT):
                ln_std_part(2, t)
            moe(1)

        @block.vector
        def _(dve):
            V = nc.vector
            n_dch = [0]

            def link(ins):
                n_dch[0] += 1
                ins.then_inc(dch, 1)
                dve.wait_ge(dch, n_dch[0])

            def take_hT(n, t, bank0):
                dve.wait_ge(turned, 4 * n + 2 * t + 1)
                V.tensor_copy(hT[:, 0:4, t * P:(t + 1) * P], pb[bank0 + 2 * t][:, :].rearrange("p (k n) -> p k n", k=4)
                              ).then_inc(hT_dve, 1)

            def ln_sum(n, t, src, bank0):
                for c in range(2):
                    dve.wait_ge(mix_done, 4 * n + 2 * t + c + 1)
                    cc = slice(c * HALF, (c + 1) * HALF)
                    V.scalar_tensor_tensor(out=src[:, t, cc], in0=h[:, t, cc], scalar=ALPHA,
                                           in1=pb[bank0 + 2 * t + c][:, :], op0=ALU.mult, op1=ALU.add
                                           ).then_inc(res_ready if n % 2 else mix_res, 1)

            def ln_tile(n, t, src, g_banks, b_banks):
                dve.wait_ge(res_ready if n % 2 else mix_res, 4 * (n // 2) + 2 * t + 2)
                for c in range(2):
                    link(V.bn_stats(ln[:, t, 6 * c:6 * c + 6], src[:, t, c * HALF:(c + 1) * HALF]))
                link(V.bn_aggr(ln[:, t, 12:14], ln[:, t, 0:12]))
                V.tensor_scalar(ln[:, t, 14:15], ln[:, t, 13:14], LN_EPS, None, ALU.add).then_inc(ln_std_in, 1)
                dve.wait_ge(ln_rows, n + 1)
                for c in range(2):
                    cc = slice(c * HALF, (c + 1) * HALF)
                    V.scalar_tensor_tensor(out=src[:, t, cc], in0=src[:, t, cc], scalar=ln[:, t, 12:13],
                                           in1=pb[g_banks[c]][:, :], op0=ALU.subtract, op1=ALU.mult)
                dve.wait_ge(ln_std, NT * n + t + 1)
                link(V.reciprocal(ln[:, t, 16:17], ln[:, t, 15:16]))
                for c in range(2):
                    cc = slice(c * HALF, (c + 1) * HALF)
                    ins = V.scalar_tensor_tensor(out=h[:, t, cc], in0=src[:, t, cc], scalar=ln[:, t, 16:17],
                                                 in1=pb[b_banks[c]][:, :], op0=ALU.mult, op1=ALU.add)
                ins.then_inc(ln_ready, 1)

            for first in (pick_ready, pickg_ready, he_ready, heT_sb, back_sb, y_sb, ov[0]["zs"], ov[1]["zs"]):
                dve.sem_inc(first, START)

            dve.wait_ge(gates_w_in, 64)
            V.tensor_scalar(b_gate[:, :], b_gate[:, :], 1.0 / CAP, None, ALU.mult).then_inc(d2a, 1)
            for t in range(NT):
                take_hT(0, t, 4)
            dve.wait_ge(a2d, 1)
            link(V.tensor_tensor_scan(out=lane[1], data0=ones[0:M_HEADS, 0:1].to_broadcast([M_HEADS, SEQ]),
                                      data1=lane[2], initial=0.0, op0=ALU.mult, op1=ALU.add))
            link(V.scalar_tensor_tensor(out=lane[3], in0=lane[0], scalar=CAP, in1=lane[1], op0=ALU.mult, op1=ALU.add))
            link(V.tensor_tensor_scan(out=lane[2], data0=lane[3], data1=lane[3], initial=0.0, op0=ALU.max, op1=ALU.max))
            V.tensor_scalar(lane[4], lane[2], -1.0, None, ALU.mult)
            V.tensor_tensor(lane[5], lane[1], lane[2], ALU.subtract).then_inc(lanes_ready, 1)
            dve.wait_ge(small_T, 1)
            link(V.tensor_copy(st[:, 0:8], pb[4][:, 0:8]))
            V.tensor_scalar(st[:, 8:16], pb[4][:, 8:16], 88.0, None, ALU.min).then_inc(d2a, 1)
            dve.wait_ge(d2a, 2)
            dve.sem_inc(small_sb, 1)
            dve.wait_ge(m_bcast, M_HEADS)
            for hd in range(M_HEADS):
                mb = pb[5 + hd // 2][:, (hd % 2) * SEQ:(hd % 2 + 1) * SEQ]
                V.tensor_scalar(wts[:, hd, 0:SEQ], mb, st[:, hd:hd + 1], 0.0, ALU.add, ALU.min).then_inc(w_arg, 1)
                V.tensor_scalar(wts[:, hd, SEQ:SEQ + P], mb[:, P:SEQ], st[:, 4 + hd:5 + hd], 0.0, ALU.add, ALU.min
                                ).then_inc(w_arg, 1)
            for hd in range(M_HEADS):
                dve.wait_ge(s_done, hd + 1)
                dve.wait_ge(w_masked, 2 * hd + 2)
                V.tensor_tensor(wts[:, hd, :], wts[:, hd, :], pb[hd][:, 0:SEQ + P], ALU.mult).then_inc(p_ready, 1)
            dve.wait_ge(den_done, 1)
            dve.wait_ge(a2d, 2)
            link(V.tensor_copy(st[:, 32:40], pb[7][:, 0:8]))
            link(V.scalar_tensor_tensor(out=st[:, 40:48], in0=st[:, 32:40], scalar=-1.0, in1=st[:, 32:40],
                                        op0=ALU.mult, op1=ALU.max))
            link(V.tensor_tensor(st[:, 40:48], st[:, 40:48], st[:, 8:16], ALU.max))
            V.reciprocal(st[:, 16:24], st[:, 40:48]).then_inc(den_inv, 1)
            dve.wait_ge(sq_done, 8)
            V.tensor_scalar(st[:, 32:40], st[:, 24:32], 1.0 / M_V, MH_EPS, ALU.mult, ALU.add).then_inc(rms_in, 1)
            dve.wait_ge(rms_std, 1)
            link(V.reciprocal(st[:, 40:48], st[:, 32:40]))
            V.tensor_tensor(st[:, 40:48], st[:, 40:48], st[:, 16:24], ALU.mult).then_inc(std_ready, 1)
            dve.wait_ge(mh_bcast, 1)
            for t in range(NT):
                for c, bank in ((0, 7), (1, 4)):
                    cc = slice(c * HALF, (c + 1) * HALF)
                    dve.wait_ge(o_sb, 2 * t + c + 1)
                    dve.wait_ge(num_sb, M_HEADS * (t + 1))
                    link(V.tensor_tensor(gate_o[:, t, cc], gate_o[:, t, cc], pb[bank][:, :], ALU.mult))
                    ins = V.tensor_tensor(val[:, t, cc], val[:, t, cc], gate_o[:, t, cc], ALU.mult)
                ins.then_inc(gated, 1)
                take_hT(1, t, 0)
            for t in range(NT):
                ln_sum(0, t, h, 0)
                ln_tile(0, t, h, (4, 5), (6, 7))

            def route(l):
                def b3(ap, n):
                    return ap.rearrange("p (t o) -> p t o", o=1).to_broadcast([P, NT, n])
                lg = r_logit.rearrange("p (t e) -> p t e", t=NT)
                dve.wait_ge(logits, l + 1)
                dve.wait_ge(params_in, 16 * 8)
                link(V.reduce_max(r_s[:, 0:2], pb[0][:, 0:32].rearrange("p (t e) -> p t e", t=NT), AX_X))
                V.tensor_tensor(lg, pb[0][:, 0:32].rearrange("p (t e) -> p t e", t=NT), b3(r_s[:, 0:2], 16),
                                ALU.subtract).then_inc(rt_exp_in, 1)
                dve.wait_ge(rt_exp, l + 1)
                link(V.reduce_sum(r_s[:, 2:4], lg, AX_X))
                link(V.reciprocal(r_s[:, 4:6], r_s[:, 2:4]))
                link(V.tensor_tensor(r_prob, lg, b3(r_s[:, 4:6], 16), ALU.mult))
                link(V.tensor_tensor(r_sel, r_prob, b_rt[:, :].rearrange("p (o e) -> p o e", o=1).to_broadcast([P, NT, 16]), ALU.add))
                s4 = st[:, 64:96].rearrange("p (q a b) -> p q a b", a=2, b=2)
                hi = r_logit[:, 0:16].rearrange("p (q a) -> p q a", a=2)
                lo = r_logit[:, 16:32].rearrange("p (q a) -> p q a", a=2)
                V.tensor_tensor(hi, s4[:, :, :, 0], s4[:, :, :, 1], ALU.max)
                link(V.tensor_tensor(lo, s4[:, :, :, 0], s4[:, :, :, 1], ALU.min))
                V.tensor_tensor(r_s[:, 0:8], hi[:, :, 0], hi[:, :, 1], ALU.max)
                V.tensor_tensor(r_s[:, 8:16], hi[:, :, 0], hi[:, :, 1], ALU.min)
                link(V.tensor_tensor(r_s[:, 16:24], lo[:, :, 0], lo[:, :, 1], ALU.max))
                link(V.tensor_tensor(r_s[:, 8:16], r_s[:, 8:16], r_s[:, 16:24], ALU.max))
                link(V.tensor_tensor(r_s[:, 0:8], r_s[:, 0:8], r_s[:, 8:16], ALU.add))
                gs = r_s[:, 0:8].rearrange("p (t g) -> p t g", t=NT)

                def first_best(vals, n, rank, key, m, res_):
                    link(V.reduce_max(m, vals, AX_X))
                    link(V.tensor_tensor(key, vals, b3(m, n), ALU.is_equal))
                    link(V.tensor_tensor(key, key, rank[:, :].rearrange("p (o e) -> p o e", o=1).to_broadcast([P, NT, n]), ALU.mult))
                    link(V.reduce_max(m, key, AX_X))
                    link(V.tensor_tensor(res_, key, b3(m, n), ALU.is_equal))
                gm = r_s[:, 8:16].rearrange("p (t g) -> p t g", t=NT)
                first_best(gs, 4, rank4, r_s[:, 16:24].rearrange("p (t g) -> p t g", t=NT), r_s[:, 24:26], gm)
                link(V.tensor_scalar(r_s[:, 16:24], r_s[:, 8:16], 1.0, -LOW, ALU.subtract, ALU.mult))
                q4 = lambda ap: ap.rearrange("p (q a) -> p q a", a=4)
                b4 = lambda ap: ap.rearrange("p (q o) -> p q o", o=1).to_broadcast([P, 8, 4])
                link(V.tensor_tensor(q4(r_logit), q4(st[:, 64:96]), b4(r_s[:, 8:16]), ALU.mult))
                link(V.tensor_tensor(q4(r_logit), q4(r_logit), b4(r_s[:, 16:24]), ALU.add))
                first_best(lg, 16, rank16, r_a, r_s[:, 24:26], oh1)
                link(V.scalar_tensor_tensor(out=r_logit, in0=ro[:, 0, :], scalar=3.0 * LOW, in1=r_logit, op0=ALU.mult, op1=ALU.add))
                first_best(lg, 16, rank16, r_a, r_s[:, 24:26], oh2)
                V.tensor_tensor(oh, oh1, oh2, ALU.add).then_inc(chosen, 1)
                dve.wait_ge(chosen, l + 1)
                link(V.tensor_tensor(r_a, oh, r_prob, ALU.mult))
                link(V.reduce_sum(r_s[:, 0:2], r_a, AX_X))
                link(V.reciprocal(r_s[:, 2:4], r_s[:, 0:2]))
                link(V.tensor_tensor(gate[:, :, :].rearrange("p e t -> p t e"), r_a, b3(r_s[:, 2:4], 16), ALU.mult))
                dve.wait_ge(placed, l + 1)
                pt = pos[:, :, :].rearrange("p e t -> p t e")
                link(V.tensor_tensor(r_a, pb[1][:, 0:32].rearrange("p (t e) -> p t e", t=NT), oh, ALU.mult))
                V.reduce_max(extra_f[:, 0:1], pb[1][:, 32:48], AX_X)
                link(V.tensor_scalar(pt, r_a, 1.0, None, ALU.subtract))

            def count_rounds(l):
                link(V.tensor_scalar(extra_f[:, 1:2], extra_f[:, 0:1], float(USED), None, ALU.is_gt))
                for r in range(2, SEQ // USED if USED == 64 else 4):
                    link(V.tensor_scalar(extra_f[:, 2:3], extra_f[:, 0:1], float(r * USED), None, ALU.is_gt))
                    link(V.tensor_tensor(extra_f[:, 1:2], extra_f[:, 1:2], extra_f[:, 2:3], ALU.add))
                V.tensor_copy(extra[:, :], extra_f[:, 1:2]).then_inc(lists, 1)

            def make_pick(dst, e):
                pt = pos[:, bass.ds(e, 2), :].rearrange("p e t -> p t e").rearrange("p t (e o) -> p t e o", o=1)
                return V.tensor_tensor(dst, slot_no[:, :].rearrange("p (t e s) -> p t e s", t=1, e=1).to_broadcast([P, NT, 2, SLOTS]),
                                       pt.to_broadcast([P, NT, 2, SLOTS]), ALU.is_equal)

            def make_pickg(src, e):
                gt = gate[:, bass.ds(e, 2), :].rearrange("p e t -> p t e").rearrange("p t (e o) -> p t e o", o=1)
                return V.tensor_tensor(pickg, src, gt.to_broadcast([P, NT, 2, SLOTS]), ALU.mult)

            def experts(l):
                def one_turn(i, final):
                    E0 = EXPERTS * l + i * U + START
                    P0 = EXPERTS // 2 * l + i * 2 + START

                    def inner(u):
                        dve.wait_ge(silu_done, E0 + (u + 1))
                        V.tensor_tensor(act_g[u % 2], act_g[u % 2], pb[0][:, 256:512], ALU.mult).then_inc(he_ready, 1)
                        dve.wait_ge(heT_done, E0 + (u + 1))
                        V.tensor_copy(heT, pb[3][:, 0:2 * P]).then_inc(heT_sb, 1)
                        if u % 2:
                            V.tensor_copy(back, pb[3][:, 2 * P:4 * P]).then_inc(back_sb, 1)
                        p = (u % 2) * 64
                        dve.wait_ge(y_done, E0 + (u + 1))
                        V.tensor_copy(ye[p:p + 64, 0:HALF], pb[2][0:64, :]).then_inc(y_sb, 1)

                    for m in range(2):
                        dve.wait_ge(pick_ready, P0 + (m + 1))
                        make_pickg(pick[m % 2], i * U + 2 * m).then_inc(pickg_ready, 1)
                        if not (final and m == 1):
                            dve.wait_ge(x_got, (P0 + m) * 2 - START)
                            make_pick(pick[(m + 1) % 2], i * U + (2 * m + 2)).then_inc(pick_ready, 1)
                        inner(2 * m)
                        inner(2 * m + 1)

                make_pick(pick[0], 0).then_inc(pick_ready, 1)
                count_rounds(l)
                with dve.Fori(0, TURNS - 1) as i:
                    one_turn(i, False)
                one_turn(TURNS - 1, True)

            def make_pick1(e):
                return V.tensor_tensor(pick[0], slot_no[:, :].rearrange("p (t e s) -> p t e s", t=1, e=1).to_broadcast([P, NT, 2, SLOTS]),
                                       pos[:, bass.ds(e, 1), :].rearrange("p e t -> p t e").rearrange("p t (e o) -> p t e o", o=1)
                                       .to_broadcast([P, NT, 2, SLOTS]), ALU.is_equal)

            def make_pickg1(e):
                return V.tensor_tensor(pickg, pick[0], gate[:, bass.ds(e, 1), :].rearrange("p e t -> p t e")
                                       .rearrange("p t (e o) -> p t e o", o=1).to_broadcast([P, NT, 2, SLOTS]), ALU.mult)

            def overflow(l):
                s = ov[l]
                rounds = dve.value_load(extra[0:1, 0:1], min_val=0, max_val=3)
                with dve.If(rounds > 0):
                    with dve.Fori(0, rounds) as j:
                        V.tensor_scalar(pos[:, :, :], pos[:, :, :], float(USED), None, ALU.subtract).then_inc(s["dve"], 1)
                        with dve.Fori(0, EXPERTS) as e:
                            n = j * EXPERTS + e

                            dve.wait_ge(s["dve"], n + j + 1)
                            make_pick1(e).then_inc(s["dve"], 1)
                            dve.wait_ge(s["dve"], n + j + 2)
                            make_pickg1(e).then_inc(s["pick"], 1)
                            dve.wait_ge(s["silu"], n + 1)
                            V.tensor_tensor(act_g[0], act_g[0], pb[0][:, 256:512], ALU.mult).then_inc(s["he"], 1)
                            dve.wait_ge(s["t"], n + 1)
                            V.tensor_copy(heT, pb[3][:, 0:2 * P])
                            V.tensor_copy(back, pb[3][:, 2 * P:4 * P]).then_inc(s["ts"], 1)
                            dve.wait_ge(s["w_used"], n * (KC + FC) + (KC + FC + START))
                            V.tensor_copy(ye[0:64, 0:HALF], pb[2][0:64, :])
                            V.tensor_copy(ye[0:64, HALF:2 * HALF], pb[2][64:128, :]).then_inc(s["ys"], 1)
                            dve.wait_ge(s["z"], n + 1)
                            dve.wait_ge(s["zs"], n * 4 + START)
                            for t in range(NT):
                                for c in range(2):
                                    cc = slice(c * HALF, (c + 1) * HALF)
                                    V.tensor_tensor(res[:, t, cc], res[:, t, cc], pb[4 + 2 * t + c][:, :], ALU.add
                                                    ).then_inc(s["zs"], 1)
                    dve.wait_ge(s["zs"], rounds * (EXPERTS * 4) + START)
                    V.tensor_copy(extra_f[:, 3:4], extra_f[:, 1:2])

            def moe(l):
                for t in range(NT):
                    take_hT(2 + 2 * l, t, 0)
                route(l)
                experts(l)
                for t in range(NT):
                    ln_sum(2 * l + 1, t, res, 4)
                overflow(l)
                for t in range(NT):
                    ln_tile(2 * l + 1, t, res, (1, 0), (3, 2))

            moe(0)

            for t in range(NT):
                take_hT(3, t, 4)

            def rotate(dst1, dst2, src, t, nh):
                c = cs[:, t, 0:32].rearrange("p (o n) -> p o n", o=1).to_broadcast([P, nh, 32])
                s = cs[:, t, 32:64].rearrange("p (o n) -> p o n", o=1).to_broadcast([P, nh, 32])
                x1, x2 = src[:, :, 0:32], src[:, :, 32:64]
                V.tensor_tensor(dst1, x1, c, ALU.mult)
                link(V.tensor_tensor(dst2, x2, c, ALU.mult))
                V.tensor_tensor(x1, x1, s, ALU.mult)
                link(V.tensor_tensor(x2, x2, s, ALU.mult))
                V.tensor_tensor(dst1, dst1, x2, ALU.subtract)
                return V.tensor_tensor(dst2, dst2, x1, ALU.add)

            V.memset(v_shift[:, :, :], 0.0).then_inc(shift_zero, 1)
            for t in range(NT):
                dve.wait_ge(v_split, t + 1)
                link(rotate(kdup[:, t, :, 0, 0:32], kdup[:, t, :, 0, 32:64],
                            pb[t][:, 0:KV_W].rearrange("p (g n) -> p g n", g=A_KV), t, A_KV))
                V.tensor_copy(kdup[:, t, :, 1, :], kdup[:, t, :, 0, :]).then_inc(k_rot, 1)

            def rotate_q(t, c):
                dve.wait_ge(q_done, 2 * t + c + 1)
                qd = q_rot[t][:, c * HALF:(c + 1) * HALF].rearrange("p (h n) -> p h n", n=DH)
                rotate(qd[:, :, 0:32], qd[:, :, 32:64], pb[2 + c][:, :].rearrange("p (h n) -> p h n", n=DH), t, 8
                       ).then_inc(q_rotd, 1)
            inv = float(DH) ** -0.5

            def soft_in(n):
                t, par, jj = SC_ORDER[n]
                b = SCB[t][par][jj]
                o = 20 * (n % 4)
                sk = sink[:, 8 * jj + par:8 * jj + 8:2]
                dve.wait_ge(sc_done, n + 1)
                pr = pb[b][:, :].rearrange("p (s k) -> p s k", s=4)
                if t == 0:
                    link(V.memset(pr[0:64, :, 0:64], LOW))
                link(V.reduce_max(st[:, o:o + 4], pr, AX_X))
                link(V.scalar_tensor_tensor(out=st[:, o:o + 4], in0=st[:, o:o + 4], scalar=inv, in1=sk, op0=ALU.mult, op1=ALU.max))
                V.tensor_scalar(st[:, o + 4:o + 8], st[:, o:o + 4], -1.0, None, ALU.mult)
                V.tensor_tensor(st[:, o + 8:o + 12], sk, st[:, o:o + 4], ALU.subtract).then_inc(mx_ready, 1)

            def soft_out(n):
                o = 20 * (n % 4)
                dve.wait_ge(e_done, 5 * (n + 1))
                link(V.tensor_tensor(st[:, o:o + 4], st[:, o + 8:o + 12], st[:, o + 12:o + 16], ALU.add))
                V.reciprocal(st[:, o + 16:o + 20], st[:, o:o + 4]).then_inc(inv_ready, 1)

            def soft_T(n):
                t, par, jj = SC_ORDER[n]
                dve.wait_ge(pT_done, n + 1)
                V.tensor_copy(probT[n % 2], pb[SCB[t][par][jj]][:, :]).then_inc(pT_sb, 1)

            def take_out(n):
                t, _, jj = SC_ORDER[n]
                dve.wait_ge(pv_done, n + 1)
                V.tensor_copy(hT[:, 4 * jj:4 * jj + 4, t * P:(t + 1) * P],
                              pb[SCB[t][0][jj]][:, :].rearrange("p (j n) -> p j n", j=4)).then_inc(outT_sb, 1)

            for c in range(2):
                rotate_q(0, c)
            for n0 in (0, 4):
                for n in range(n0, n0 + 4):
                    soft_in(n)
                for nn in (n0, n0 + 2):
                    soft_out(nn)
                    soft_out(nn + 1)
                    soft_T(nn)
                    soft_T(nn + 1)
                    if n0 == 0:
                        rotate_q(1, nn // 2)
                    take_out(nn + 1)
            for t in range(NT):
                ln_sum(2, t, h, 0)
                ln_tile(2, t, h, (4, 5), (6, 7))
            moe(1)


_INS = ['x', 'w_in_a', 'b_gates_a', 'mh_norm_a', 'w_out_a', 'w_kv_shared', 'w_q_b', 'sinks_b', 'w_out_b',
        'w_router', 'b_router', 'w_gu', 'w_down', 'ln_g', 'ln_b']


def kernel(**inputs):
    import numpy as _np
    import concourse.bacc as _bacc
    from concourse import mybir as _mybir
    from concourse.bass_utils import run_bass_kernel_spmd as _run

    nc = _bacc.Bacc("TRN2", target_bir_lowering=False, num_devices=1)
    arrays, args = {}, []
    for name in _INS:
        a = _np.ascontiguousarray(inputs[name])
        arrays[f"in_{name}"] = a
        args.append(nc.dram_tensor(f"in_{name}", a.shape, _mybir.dt.from_np(a.dtype), kind="ExternalInput").ap())
    freq = _np.float32(10000.0) ** (-_np.arange(0, DH, 2, dtype=_np.float32) / _np.float32(DH))
    ang = _np.arange(SEQ, dtype=_np.float32)[:, None] * freq[None, :]
    table = _np.stack([_np.cos(ang), _np.sin(ang)]).astype(_np.float32)
    arrays["rope"] = table
    args.append(nc.dram_tensor("rope", table.shape, F32, kind="ExternalInput").ap())
    args.append(nc.dram_tensor("out_0", (1, SEQ, D), F32, kind="ExternalOutput").ap())
    build(nc, *args)
    r = _run(nc, [arrays], core_ids=[0])
    return r.results[0]["out_0"]
```

```python
import concourse.bass as bass
from concourse import mybir
from contextlib import ExitStack

F32 = mybir.dt.float32
I32 = mybir.dt.int32
BF16 = mybir.dt.bfloat16
ACT = mybir.ActivationFunctionType
ALU = mybir.AluOpType
AX_X = mybir.AxisListType.X

SEQ, D = 256, 1024
P = 128
NT = SEQ // P
KC = D // P
HALF = 512
M_HEADS, M_V = 4, 256
M_QK = 128
A_HEADS, A_KV, DH, CHUNK = 16, 4, 64, 64
PAIRS = A_HEADS // 2
KV_W = A_KV * DH
EXPERTS, GROUPS, FF = 16, 4, 512
PER_GROUP = EXPERTS // GROUPS
FC = FF // P
SLOTS = 64
USED = 64
GW = 32 + M_HEADS
START = 2
U = 4
TURNS = EXPERTS // U
ALPHA = 4.0 ** 0.25
CAP = 15.0
LN_EPS, MH_EPS = 1e-5, 1e-6
LOW = -1.0e30
NG, ND = 4, 2
G_MIX = [0, 20]
G_EXP = [4, 22]
D_EXP = [0, 17]
D_KV = 16


def build(nc, x, w_in_a, b_gates_a, mh_norm_a, w_out_a, w_kv_shared, w_q_b, sinks_b, w_out_b,
          w_router, b_router, w_gu, w_down, ln_g, ln_b, rope, out):
    ctx = ExitStack()
    with ctx:
        def sb(name, shape, dt=F32):
            return ctx.enter_context(nc.sbuf_tensor(name, shape, dt))

        def sem(name):
            return ctx.enter_context(nc.semaphore(name))

        big = [sb(f"big{n}", [P, KC, D]) for n in range(NG)]
        small = [sb(f"small{n}", [P, FC, D]) for n in range(ND)]
        ident = sb("ident", [P, P])
        tri = sb("tri", [P, P])
        ones = sb("ones", [P, 1])
        slot_no = sb("slot_no", [P, SLOTS])
        rank16 = sb("rank16", [P, EXPERTS])
        rank4 = rank16[:, EXPERTS - GROUPS:EXPERTS]
        rows3 = sb("rows3", [64 + 9, D], BF16)
        row_pick = sb("row_pick", [64 + 9, 9], BF16)
        alpha_i = sb("alpha_i", [P, P])
        h = sb("h", [P, NT, D])
        hT = sb("hT", [P, KC, SEQ])
        bufA = sb("bufA", [P, 2048])
        bufB = sb("bufB", [P, 2048])
        bufC = sb("bufC", [P, 1536])
        v_shift = sb("v_shift", [P, NT, KV_W])
        w_rt = sb("w_rt", [P, KC, EXPERTS])
        b_rt = sb("b_rt", [P, EXPERTS])
        sink = sb("sink", [P, A_HEADS // 2])
        b_gate = sb("b_gate", [GW, 1])
        cs = sb("cs", [P, NT, DH])
        st = sb("st", [P, 160])

        rows = [bufB[32 * n:32 * n + 9, 0:D] for n in range(3)]
        w_gate = v_shift[:, :, :].rearrange("p t n -> p (t n)")[:, 0:KC * GW].rearrange("p (k n) -> p k n", k=KC)
        qkT = bufA[:, :].rearrange("p (g n) -> p g n", g=8)
        gate_o = bufA[:, :].rearrange("p (t n) -> p t n", t=NT)
        val = bufB[:, :].rearrange("p (t n) -> p t n", t=NT)
        wts = bufC[:, :].rearrange("p (h n) -> p h n", h=M_HEADS)
        lane = [bufC[0:M_HEADS, n * SEQ:(n + 1) * SEQ] for n in range(6)]
        tanh_rows = bufC[0:GW, 0:SEQ]
        kdup = bufB[:, 0:1024].rearrange("p (t g d n) -> p t g d n", t=NT, g=A_KV, d=2)
        q_rot = [bufA[:, 0:1024], small[D_KV % ND][:, 0, :]]
        qT = bufB[:, :].rearrange("p (g c r q) -> p g c r q", g=A_KV, c=SEQ // CHUNK, r=2)
        kT = bufC[:, 0:1024].rearrange("p (g n) -> p g n", g=A_KV)
        v_tok = bufC[:, 1024:1536].rearrange("p (t n) -> p t n", t=NT)
        prob = [bufA[:, n * 512:(n + 1) * 512] for n in range(2)]
        probT = [bufA[:, 1024 + n * 512:1024 + (n + 1) * 512] for n in range(2)]
        res = gate_o
        xe = [bufB[:, 0:1024].rearrange("p (k s) -> p k s", k=KC),
              hT[:, 4:8, :].rearrange("p k n -> p (k n)").rearrange("p (k s) -> p k s", k=KC)]
        ye = bufB[:, 1024:2048]
        pick = [bufC[:, n * 256:(n + 1) * 256].rearrange("p (t e s) -> p t e s", t=NT, e=2) for n in range(2)]
        pickg = bufC[:, 512:768].rearrange("p (t e s) -> p t e s", t=NT, e=2)
        act_g = [bufC[:, 768 + n * 256:768 + (n + 1) * 256] for n in range(2)]
        back = v_shift[:, 0, :]
        heT = bufC[:, 1280:1536]
        spill_w = hT[:, 0:4, :].rearrange("p k n -> p (k n)")

        r_logit = st[:, 0:32]
        r_prob = st[:, 32:64].rearrange("p (t e) -> p t e", t=NT)
        r_sel = st[:, 64:96].rearrange("p (t e) -> p t e", t=NT)
        r_a = st[:, 96:128].rearrange("p (t e) -> p t e", t=NT)
        r_s = st[:, 128:160]
        lgT = bufC[0:EXPERTS, 0:SEQ]
        ro = bufC[:, 1280:1376].rearrange("p (a n) -> p a n", a=3)
        oh1 = ro[:, 0, :].rearrange("p (t e) -> p t e", t=NT)
        oh2 = ro[:, 1, :].rearrange("p (t e) -> p t e", t=NT)
        oh = ro[:, 2, :].rearrange("p (t e) -> p t e", t=NT)
        pos = sb("pos", [P, EXPERTS, NT])
        gate = sb("gate", [P, EXPERTS, NT])
        extra_f = sb("extra_f", [P, 4])
        extra = sb("extra", [P, 1], I32)
        ln = st[:, 0:40].rearrange("p (t n) -> p t n", t=NT)

        pb = [ctx.enter_context(nc.psum_tensor(f"pb{n}", [P, HALF], F32)) for n in range(8)]

        big_in = [[sem(f"big_in{n}_{q}") for q in range(4)] for n in range(NG)]
        small_in = [[sem(f"small_in{n}_{q}") for q in range(2)] for n in range(ND)]
        x_in = [sem(f"x_in{t}") for t in range(NT)]
        gates_w_in, params_in = sem("gates_w_in"), sem("params_in")
        rows_in, rows_part, rows_ready = sem("rows_in"), sem("rows_part"), sem("rows_ready")
        gate_zero = sem("gate_zero")
        consts = sem("consts")
        turned = sem("turned")
        hT_dve, hT_act = sem("hT_dve"), sem("hT_act")
        qk_done, qk_sb = sem("qk_done"), sem("qk_sb")
        gates_done, gates_read = sem("gates_done"), sem("gates_read")
        v_done, v_sb = sem("v_done"), sem("v_sb")
        lanes_ready = sem("lanes_ready")
        small_T, small_sb = sem("small_T"), sem("small_sb")
        m_bcast, s_done = sem("m_bcast"), sem("s_done")
        w_arg, w_exp, w_masked, p_ready = sem("w_arg"), sem("w_exp"), sem("w_masked"), sem("p_ready")
        o_done, o_sb, mh_bcast = sem("o_done"), sem("o_sb"), sem("mh_bcast")
        den_done, den_inv = sem("den_done"), sem("den_inv")
        num_done, sq_done = sem("num_done"), sem("sq_done")
        a2d, d2a = sem("a2d"), sem("d2a")
        mix_done = sem("mix_done")
        ln_rows, ln_std_in, ln_std, ln_ready = sem("ln_rows"), sem("ln_std_in"), sem("ln_std"), sem("ln_ready")
        lgT_done, lgT_sb = sem("lgT_done"), sem("lgT_sb")
        logits, rt_exp_in, rt_exp, chosen, placed, lists = (
            sem("logits"), sem("rt_exp_in"), sem("rt_exp"), sem("chosen"), sem("placed"), sem("lists"))
        pick_ready, pickg_ready = sem("pick_ready"), sem("pickg_ready")
        x_got, x_sb = sem("x_got"), sem("x_sb")
        first_gu = sem("first_gu")
        gu_done, silu_done, he_ready = sem("gu_done"), sem("silu_done"), sem("he_ready")
        heT_done, heT_sb, back_sb = sem("heT_done"), sem("heT_sb"), sem("back_sb")
        num_sb, std_ready, rms_in, rms_std, gated = (
            sem("num_sb"), sem("std_ready"), sem("rms_in"), sem("rms_std"), sem("gated"))
        inv_ready = sem("inv_ready")
        res_in = sem("res_in")
        y_done, y_sb = sem("y_done"), sem("y_sb")
        ov = [{n: sem(f"ov{l}_{n}") for n in ("w_in", "w_used", "pick", "x", "xs", "silu", "he", "t",
                                               "ts", "ys", "z", "zs", "dve")} for l in range(2)]
        kv_done, v_split, k_rot, q_done, q_rotd, kT_done, kT_sb, qT_done, qT_sb = (
            sem("kv_done"), sem("v_split"), sem("k_rot"), sem("q_done"), sem("q_rotd"), sem("kT_done"),
            sem("kT_sb"), sem("qT_done"), sem("qT_sb"))
        sc_done, mx_ready, e_done, pn_ready, pT_done, pT_sb, pv_done, outT_sb = (
            sem("sc_done"), sem("mx_ready"), sem("e_done"), sem("pn_ready"), sem("pT_done"),
            sem("pT_sb"), sem("pv_done"), sem("outT_sb"))
        shift_zero = sem("shift_zero")
        dch, ach = sem("dch"), sem("ach")
        stored = sem("stored")

        block = ctx.enter_context(nc.Block())

        def big_at(n):
            return big[n % NG], big_in[n % NG], n // NG + 1

        def small_at(n):
            return small[n % ND], small_in[n % ND], n // ND + 1

        SCB = [[[0, 1], [4, 5]], [[2, 3], [6, 7]]]
        SC_ORDER = [(t, par, jj) for t in range(NT) for jj in range(2) for par in range(2)]

        @block.sync
        def _(sp):
            def load_big(n, src):
                buf, sems, _ = big_at(n)
                v = src.rearrange("(k p) n -> p k n", p=P)
                for q in range(4):
                    sp.dma_start(buf[:, 2 * q:2 * q + 2, :], v[:, 2 * q:2 * q + 2, :]).then_inc(sems[q], 16)

            def load_small(n, src):
                buf, sems, _ = small_at(n)
                v = src.rearrange("(k p) n -> p k n", p=P)
                for q in range(2):
                    sp.dma_start(buf[:, 2 * q:2 * q + 2, :], v[:, 2 * q:2 * q + 2, :]).then_inc(sems[q], 16)

            for t in range(NT):
                sp.dma_start(h[:, t, :], x[0, t * P:(t + 1) * P, :]).then_inc(x_in[t], 16)
            w_in = w_in_a[0]
            for q in range(4):
                sp.dma_start(big[0][:, :, q * 256:(q + 1) * 256],
                             w_in[:, q * 256:(q + 1) * 256].rearrange("(k p) n -> p k n", p=P)
                             ).then_inc(big_in[0][q], 16)
            load_big(1, w_in[:, 1024:2048])
            load_big(2, w_in[:, 2048:3072])
            load_big(3, w_out_a[0])
            for l in range(2):
                G0, D0 = G_EXP[l], D_EXP[l]
                DONE = START + EXPERTS * l

                def load_gu(e, ring=None):
                    load_big(G0 + (e if ring is None else ring), w_gu[l, bass.ds(e, 1)].rearrange("a k n -> (a k) n"))

                def load_dn(e, ring=None):
                    load_small(D0 + (e if ring is None else ring), w_down[l, bass.ds(e, 1)].rearrange("a k n -> (a k) n"))

                if l == 0:
                    load_dn(0)
                    load_dn(1)
                    sp.wait_ge(qk_done, 8)
                    load_gu(0)
                    sp.wait_ge(v_done, 4)
                    load_gu(1)
                    sp.wait_ge(o_done, 4)
                    load_gu(2)
                    sp.wait_ge(mix_done, 4)
                    load_gu(3)
                else:
                    sp.wait_ge(y_done, DONE - 1)
                    v = w_kv_shared.rearrange("(k p) n -> p k n", p=P)
                    buf, sems, _ = small_at(D_KV)
                    bv = buf[:, :, :].rearrange("p a (b n) -> p (a b) n", b=2)
                    for q in range(2):
                        sp.dma_start(bv[:, 4 * q:4 * q + 4, :], v[:, 4 * q:4 * q + 4, :]).then_inc(sems[q], 16)
                    sp.wait_ge(gu_done, DONE)
                    load_big(G_MIX[1], w_q_b[0])
                    load_big(G_MIX[1] + 1, w_out_b[0])
                    load_gu(0)
                    load_gu(1)
                    sp.wait_ge(y_done, DONE)
                    load_dn(0)
                    sp.wait_ge(q_done, 4)
                    load_gu(2)
                    sp.wait_ge(qT_done, 4)
                    load_dn(1)
                    sp.wait_ge(mix_done, 12)
                    load_gu(3)
                def next_gu(e, i=0):
                    sp.wait_ge(gu_done, i * U + (DONE + e - 3))
                    load_gu(i * U + e, e)

                def next_dn(e, i=0):
                    sp.wait_ge(y_done, i * U + (DONE + e - 1))
                    load_dn(i * U + e, e)

                for e in (4, 5):
                    buf, sems, _ = big_at(G0 + e)
                    for q in range(4):
                        if q < 3:
                            sp.wait_ge(first_gu, 3 * (2 * l + e - 4) + q + 1)
                        else:
                            sp.wait_ge(gu_done, DONE + e - 3)
                        sp.dma_start(buf[:, 2 * q:2 * q + 2, :],
                                     w_gu[l, e].rearrange("(k p) n -> p k n", p=P)[:, 2 * q:2 * q + 2, :]
                                     ).then_inc(sems[q], 16)
                next_dn(2)
                next_dn(3)
                with sp.Fori(0, TURNS - 2) as i:
                    for e in range(4, 4 + U):
                        next_gu(e + 2, i)
                        next_dn(e, i)
                for e in range(4 + U * (TURNS - 2), EXPERTS):
                    next_dn(e)
                    if e + 2 < EXPERTS:
                        next_gu(e + 2)
                s = ov[l]
                sp.wait_ge(lists, l + 1)
                rounds = sp.value_load(extra[0:1, 0:1], min_val=0, max_val=3)
                with sp.If(rounds > 0):
                    sp.wait_ge(s["dve"], 1)
                    with sp.Fori(0, rounds) as j:
                        with sp.Fori(0, EXPERTS) as e:
                            n0 = (j * EXPERTS + e) * (KC + FC)
                            for k in range(KC + FC):
                                sp.wait_ge(s["w_used"], n0 + (k + START))
                                src = (w_gu[l, bass.ds(e, 1), k * P:(k + 1) * P, :] if k < KC else
                                       w_down[l, bass.ds(e, 1), (k - KC) * P:(k - KC + 1) * P, :])
                                sp.dma_start(spill_w, src.rearrange("a p n -> (a p) n")).then_inc(s["w_in"], 16)
            for t in range(NT):
                for c in range(2):
                    sp.wait_ge(ln_ready, 2 * (3 * NT + t) + c + 1)
                    sp.dma_start(out[0, t * P:(t + 1) * P, c * HALF:(c + 1) * HALF],
                                 h[:, t, c * HALF:(c + 1) * HALF]).then_inc(stored, 16)
            sp.wait_ge(stored, 16 * 2 * NT)

        NCONST = 6 + (USED < SLOTS)

        @block.gpsimd
        def _(pool):
            nc.gpsimd.memset(ones[:, :], 1.0).then_inc(consts, 1)
            nc.gpsimd.memset(ident[:, :], 0.0).then_inc(consts, 1)
            pool.wait_ge(consts, 2)
            nc.gpsimd.affine_select(out=ident[:, :], in_=ident[:, :], compare_op=ALU.not_equal, fill=1.0, base=0,
                                    pattern=[[-1, P]], channel_multiplier=1).then_inc(consts, 1)
            nc.gpsimd.affine_select(out=tri[:, :], in_=ones[:, 0:1].to_broadcast([P, P]), compare_op=ALU.is_ge, fill=0.0, base=0,
                                    pattern=[[1, P]], channel_multiplier=-1).then_inc(consts, 1)
            nc.gpsimd.iota(slot_no[:, :], pattern=[[1, SLOTS]], base=0, channel_multiplier=0,
                           allow_small_or_imprecise_dtypes=True).then_inc(consts, 1)
            nc.gpsimd.iota(rank16[:, :], pattern=[[-1, EXPERTS]], base=EXPERTS, channel_multiplier=0,
                           allow_small_or_imprecise_dtypes=True).then_inc(consts, 1)
            if USED < SLOTS:
                pool.wait_ge(consts, 6)
                nc.gpsimd.memset(slot_no[:, USED:SLOTS], -1.0e6).then_inc(consts, 1)
            nc.gpsimd.memset(w_gate, 0.0).then_inc(gate_zero, 1)
            nc.gpsimd.memset(b_gate[:, :], 0.0).then_inc(gate_zero, 1)
            nc.gpsimd.memset(rows3[:, :], 0.0).then_inc(rows_part, 1)
            nc.gpsimd.memset(row_pick[:, :], 0.0).then_inc(rows_part, 1)
            pool.wait_ge(consts, NCONST)
            nc.gpsimd.tensor_scalar(alpha_i[:, :], ident[:, :], ALPHA, None, ALU.mult).then_inc(rows_part, 1)
            pool.wait_ge(rows_part, 3)
            for n in range(3):
                nc.gpsimd.tensor_copy(row_pick[32 * n:32 * n + 9, :], ident[0:9, 0:9]).then_inc(rows_part, 1)
            pool.wait_ge(rows_in, 16 * 3)
            for n in range(3):
                part = rows3[32 * n:32 * n + 9, :]
                nc.gpsimd.tensor_copy(part, rows[n]).then_inc(rows_part, 1)
                pool.wait_ge(rows_part, 7 + 2 * n)
                if n < 2:
                    nc.gpsimd.tensor_tensor(rows[n + 1], rows[n], part, ALU.subtract).then_inc(rows_part, 1)
                    pool.wait_ge(rows_part, 8 + 2 * n)
            pool.sem_inc(rows_ready, 1)
            for hd in range(M_HEADS):
                pool.wait_ge(w_exp, hd + 1)
                for blk in range(2):
                    d = wts[:, hd, 256 * blk:256 * blk + P]
                    nc.gpsimd.tensor_tensor(d, d, tri[:, :], ALU.mult).then_inc(w_masked, 1)
            for n in range(8):
                pool.wait_ge(inv_ready, n + 1)
                o = 20 * (n % 4)
                p3 = prob[n % 2].rearrange("p (s k) -> p s k", s=4)
                nc.gpsimd.tensor_tensor(p3, p3, st[:, o + 16:o + 20].rearrange("p (s o) -> p s o", o=1).to_broadcast([P, 4, P]),
                                        ALU.mult).then_inc(pn_ready, 1)

        @block.tensor
        def _(pe):
            mm = nc.tensor.matmul

            def wait_big(n, q, i=0):
                _, sems, fill = big_at(n)
                pe.wait_ge(sems[q], i * 16 + 16 * fill)

            def turn(src, n, t, j, bank0):
                for kk in range(4):
                    k = 4 * j + kk
                    last = nc.tensor.transpose(pb[bank0 + 2 * t + j][:, kk * P:(kk + 1) * P],
                                               src[:, t, k * P:(k + 1) * P], ident[:, :])
                last.then_inc(turned, 1)

            def stay_awake(bank, n):
                for _ in range(n):
                    mm(pb[bank][:, :], ident[:, :], ident[:, 0:1].to_broadcast([P, HALF]), start=True, stop=True)

            def turn_h(n, ln_no, t, bank0):
                for j in range(2):
                    pe.wait_ge(ln_ready, 2 * (NT * ln_no + t) + j + 1)
                    turn(h, n, t, j, bank0)

            def wait_hT(n, t):
                pe.wait_ge(hT_act, 3 * n + t + 2)
                if t:
                    pe.wait_ge(hT_dve, n + 1)

            def project(n, t, c, bank, done, between={}):
                w = big_at(n)[0]
                for k in range(KC):
                    if k in between:
                        between[k]()
                    if t == 0 and c == 0 and k % 2 == 0:
                        wait_big(n, k // 2)
                    last = mm(pb[bank][:, :], hT[:, k, t * P:(t + 1) * P], w[:, k, c * HALF:(c + 1) * HALF],
                              start=k == 0, stop=k == KC - 1)
                last.then_inc(done, 1)

            def bcast_row(bank, row, c):
                return mm(pb[bank][:, :], row_pick[:, row:row + 1].to_broadcast([64 + 9, P]),
                          rows3[:, c * HALF:(c + 1) * HALF], start=True, stop=True)

            def ln_bcast(l, which, g0, b0):
                r = 2 * l + which
                for c in range(2):
                    bcast_row(g0 + c, r, c)
                    last = bcast_row(b0 + c, 4 + r, c)
                last.then_inc(ln_rows, 1)

            for first in (x_got, gu_done, heT_done, y_done, ov[0]["w_used"], ov[1]["w_used"]):
                pe.sem_inc(first, START)

            pe.wait_ge(consts, NCONST)
            for t in range(NT):
                pe.wait_ge(x_in[t], 16)
                for j in range(2):
                    turn(h, 0, t, j, 4)
            wait_hT(0, 1)
            for g in range(8):
                if g % 2 == 0:
                    wait_big(0, g // 2)
                for k in range(KC):
                    last = mm(pb[g // 2][:, (g % 2) * SEQ:(g % 2 + 1) * SEQ], big[0][:, k, g * P:(g + 1) * P],
                              hT[:, k, :], start=k == 0, stop=k == KC - 1)
                last.then_inc(qk_done, 1)
            pe.wait_ge(gates_w_in, 64)
            for k in range(KC):
                last = mm(pb[4][0:GW, 0:SEQ], w_gate[:, k, :], hT[:, k, :], start=k == 0, stop=k == KC - 1)
            last.then_inc(gates_done, 1)
            for t, c, bank in ((0, 0, 5), (0, 1, 6), (1, 0, 7), (1, 1, 4)):
                if bank == 4:
                    pe.wait_ge(gates_read, 1)
                project(1, t, c, bank, v_done)
            pe.wait_ge(lanes_ready, 1)
            pe.wait_ge(v_sb, 4)
            for n, ln_no in enumerate((3, 5)):
                for t in range(NT):
                    c = (2 * n + t) * M_HEADS
                    last = nc.tensor.transpose(pb[4][:, c:c + M_HEADS], lane[ln_no][:, t * P:(t + 1) * P],
                                               ident[0:M_HEADS, 0:M_HEADS])
            last.then_inc(small_T, 1)
            for hd in range(M_HEADS):
                mm(pb[5 + hd // 2][:, (hd % 2) * SEQ:(hd % 2 + 1) * SEQ],
                   ident[0:M_HEADS, hd:hd + 1].to_broadcast([M_HEADS, P]), lane[4], start=True, stop=True
                   ).then_inc(m_bcast, 1)
            pe.wait_ge(qk_sb, 8)
            for hd in range(M_HEADS):
                mm(pb[hd][:, 0:SEQ], qkT[:, 4 + hd, 0:P], qkT[:, hd, :], start=True, stop=True)
                mm(pb[hd][:, SEQ:SEQ + P], qkT[:, 4 + hd, P:SEQ], qkT[:, hd, P:SEQ], start=True, stop=True
                   ).then_inc(s_done, 1)
            project(2, 0, 0, 7, o_done)
            pe.wait_ge(small_sb, 1)
            project(2, 0, 1, 4, o_done)
            pe.wait_ge(o_sb, 1)
            pe.wait_ge(p_ready, M_HEADS)
            for t in range(NT):
                for hd in range(M_HEADS):
                    c = t * M_HEADS + hd
                    for s in range(t + 1):
                        lo = (s + t) * P
                        last = mm(pb[7][:, c:c + 1], wts[:, hd, lo:lo + P], ones[:, 0:1], start=s == 0, stop=s == t)
            last.then_inc(den_done, 1)
            for hd in range(M_HEADS):
                for t in range(NT):
                    for s in range(t + 1):
                        lo = (s + t) * P
                        last = mm(pb[hd][:, t * M_V:(t + 1) * M_V], wts[:, hd, lo:lo + P],
                                  val[:, s, hd * M_V:(hd + 1) * M_V], start=s == 0, stop=s == t)
                last.then_inc(num_done, 1)
            pe.wait_ge(params_in, 16 * 6)
            pe.wait_ge(rows_ready, 1)
            pe.wait_ge(o_sb, 2)
            pe.wait_ge(den_inv, 1)
            for c, bank in ((0, 7), (1, 4)):
                last = bcast_row(bank, 8, c)
            last.then_inc(mh_bcast, 1)
            pe.wait_ge(w_arg, 2 * M_HEADS)
            project(2, 1, 0, 5, o_done)
            pe.wait_ge(num_sb, NT * M_HEADS)
            pe.wait_ge(gated, 1)
            for j in range(2):
                turn(val, 1, 0, j, 0)
            project(2, 1, 1, 6, o_done)
            wait_hT(1, 0)
            for c in range(2):
                project(3, 0, c, c, mix_done)
            pe.wait_ge(gated, 2)
            for j in range(2):
                turn(val, 1, 1, j, 0)
            ln_bcast(0, 0, 4, 6)
            wait_hT(1, 1)
            project(3, 1, 0, 2, mix_done)
            turn_h(2, 0, 0, 0)
            project(3, 1, 1, 3, mix_done)

            PAIRS_E = EXPERTS // 2

            def moe(l):
                for t in range(NT):
                    if t:
                        stay_awake(1, 3)
                        turn_h(2 + 2 * l, 2 * l, t, 0)
                    wait_hT(2 + 2 * l, t)
                    for k in range(KC):
                        last = mm(pb[2 * t][0:EXPERTS, 0:P], w_rt[:, k, :], hT[:, k, t * P:(t + 1) * P],
                                  start=k == 0, stop=k == KC - 1)
                    last.then_inc(lgT_done, 1)
                    if t:
                        for tt in range(NT):
                            pe.wait_ge(lgT_sb, NT * l + tt + 1)
                            last = nc.tensor.transpose(pb[1][:, tt * EXPERTS:(tt + 1) * EXPERTS],
                                                       lgT[:, tt * P:(tt + 1) * P], ident[0:EXPERTS, 0:EXPERTS])
                last.then_inc(logits, 1)
                for _ in range(2):
                    for t in range(NT):
                        for c in range(2):
                            mm(pb[4 + 2 * t + c][:, :], alpha_i[:, :], h[:, t, c * HALF:(c + 1) * HALF],
                               start=True, stop=False, skip_group_check=True)
                pe.wait_ge(chosen, l + 1)
                mm(pb[1][:, 0:16], tri[:, :], oh[:, 0, :], start=True, stop=True)
                mm(pb[1][:, 16:32], ones[:, 0:1].to_broadcast([P, P]), oh[:, 0, :], start=True, stop=False)
                mm(pb[1][:, 16:32], tri[:, :], oh[:, 1, :], start=False, stop=True)
                mm(pb[1][:, 32:48], ones[:, 0:1].to_broadcast([P, P]), oh[:, 0, :], start=True, stop=False)
                mm(pb[1][:, 32:48], ones[:, 0:1].to_broadcast([P, P]), oh[:, 1, :], start=False, stop=True).then_inc(placed, 1)

                def gather(m, P0, ks, bank=1):
                    for k in ks:
                        if k == 0:
                            pe.wait_ge(pick_ready, P0 + (m + 1))
                        if k % 4 == 0 and bank == 1:
                            pe.wait_ge(x_sb, (P0 + m) * 2 + (k // 4 - START))
                        for t in range(NT):
                            last = mm(pb[bank][:, (k % 4) * P:(k % 4 + 1) * P], h[:, t, k * P:(k + 1) * P],
                                      pick[m % 2][:, t, :, :].rearrange("p e s -> p (e s)"),
                                      start=t == 0, stop=t == NT - 1)
                        if k % 4 == 3:
                            last.then_inc(x_got, 1)

                def gate_up(u, i, E0, P0, parts=False):
                    n = G_EXP[l] + u
                    w = big_at(n)[0]
                    pe.wait_ge(he_ready, E0 + u)
                    for k in range(KC):
                        if k % 2 == 0:
                            wait_big(n, k // 2, i)
                        if u % 2 == 0 and k % 4 == 0:
                            pe.wait_ge(x_sb, (P0 + u // 2) * 2 + (k // 4 + 1 - START))
                        for c in range(2):
                            last = mm(pb[0][c * 64:(c + 1) * 64, :].rearrange("p (a n) -> p a n", a=2),
                                      xe[u // 2 % 2][:, k, (u % 2) * SLOTS:(u % 2 + 1) * SLOTS],
                                      w[:, k, :].rearrange("p (a c n) -> p c a n", a=2, c=2)[:, c],
                                      start=k == 0, stop=k == KC - 1)
                        if parts and k in (1, 3, 5):
                            last.then_inc(first_gu, 1)
                    last.then_inc(gu_done, 1)

                def inner_T(u, E0, P0):
                    pe.wait_ge(he_ready, E0 + (u + 1))
                    pe.wait_ge(heT_sb, E0 + u)
                    if u % 2:
                        pe.wait_ge(pickg_ready, P0 + (u // 2 + 1))
                    else:
                        pe.wait_ge(back_sb, P0 + u // 2)
                    for j in range(2):
                        last = nc.tensor.transpose(pb[3][:, j * P:(j + 1) * P], act_g[u % 2][:, j * P:(j + 1) * P],
                                                   ident[:, :])
                    if u % 2:
                        for t in range(NT):
                            last = nc.tensor.transpose(pb[3][:, (2 + t) * P:(3 + t) * P],
                                                       pickg[:, t, :, :].rearrange("p e s -> p (e s)"), ident[:, :])
                    last.then_inc(heT_done, 1)

                def down(u, i, E0):
                    pe.wait_ge(heT_sb, E0 + (u + 1))
                    n = D_EXP[l] + u
                    w, sems, fill = small_at(n)
                    pe.wait_ge(y_sb, (E0 + u) * 2 - START)
                    for j in range(2):
                        for hf in range(2):
                            kk = 2 * hf + j
                            if j == 0:
                                pe.wait_ge(sems[hf], i * 32 + 16 * fill)
                            for c in range(2):
                                last = mm(pb[2][c * 64:(c + 1) * 64, :],
                                          heT[:, j * P + hf * 64:j * P + (hf + 1) * 64],
                                          w[:, kk, c * HALF:(c + 1) * HALF],
                                          start=(j, hf) == (0, 0), stop=(j, hf) == (1, 1))
                    last.then_inc(y_done, 1)

                def scatter(m, E0, P0, last_one):
                    pe.wait_ge(y_sb, (E0 + 2 * m) * 2 + (4 - START))
                    pe.wait_ge(back_sb, P0 + (m + 1))
                    for t in range(NT):
                        for c in range(2):
                            ins = mm(pb[4 + 2 * t + c][:, :], back[:, t * P:(t + 1) * P],
                                     ye[:, c * HALF:(c + 1) * HALF], start=False, stop=last_one,
                                     skip_group_check=True)
                            if last_one:
                                ins.then_inc(mix_done, 1)

                def one_turn(i, first, final):
                    E0 = EXPERTS * l + i * U + START
                    P0 = PAIRS_E * l + i * 2 + START
                    for m in range(2):
                        a, b = 2 * m, 2 * m + 1
                        over = final and m == 1
                        gate_up(b, i, E0, P0, parts=first and m == 0)
                        inner_T(a, E0, P0)
                        if not (first and m == 0):
                            scatter(m - 1, E0, P0, False)
                        down(a, i, E0)
                        if over:
                            bcast_row(1, 2 * l + 1, 0)
                        else:
                            gather(m + 1, P0, range(4, KC))
                            gate_up(b + 1, i, E0, P0)
                        inner_T(b, E0, P0)
                        if over:
                            bcast_row(0, 2 * l + 1, 1)
                        elif not (final and m == 0):
                            gather(m + 2, P0, range(4))
                        down(b, i, E0)
                        if over:
                            pe.wait_ge(back_sb, P0 + (m + 1))
                            bcast_row(3, 4 + 2 * l + 1, 0)
                            scatter(m, E0, P0, True)

                stay_awake(3, 1)
                P1, E1 = PAIRS_E * l + START, EXPERTS * l + START
                gather(0, P1, range(4))
                gather(0, P1, range(4, KC), bank=3)
                gate_up(0, 0, E1, P1, parts=True)
                gather(1, P1, range(4))
                one_turn(0, True, False)
                with pe.Fori(1, TURNS - 1) as i:
                    one_turn(i, False, False)
                one_turn(TURNS - 1, False, True)
                overflow(l)
                bcast_row(2, 4 + 2 * l + 1, 1).then_inc(ln_rows, 1)

            def overflow(l):
                s = ov[l]
                rounds = pe.value_load(extra[0:1, 0:1], min_val=0, max_val=3)
                with pe.If(rounds > 0):
                    pe.wait_ge(s["dve"], 1)
                    with pe.Fori(0, rounds) as j:
                        with pe.Fori(0, EXPERTS) as e:
                            n = j * EXPERTS + e
                            pe.wait_ge(s["pick"], n + 1)
                            for half in range(2):
                                if half:
                                    pe.wait_ge(s["xs"], n * 2 + 1)
                                for k in range(4 * half, 4 * half + 4):
                                    for t in range(NT):
                                        last = mm(pb[1][:, (k % 4) * P:(k % 4 + 1) * P], h[:, t, k * P:(k + 1) * P],
                                                  pick[0][:, t, :, :].rearrange("p e s -> p (e s)"),
                                                  start=t == 0, stop=t == NT - 1)
                                last.then_inc(s["x"], 1)
                            pe.wait_ge(s["xs"], n * 2 + 2)
                            for k in range(KC):
                                pe.wait_ge(s["w_in"], (n * (KC + FC) + (k + 1)) * 16)
                                for c in range(2):
                                    last = mm(pb[0][c * 64:(c + 1) * 64, :].rearrange("p (a n) -> p a n", a=2),
                                              xe[0][:, k, 0:SLOTS],
                                              spill_w.rearrange("p (a c n) -> p c a n", a=2, c=2)[:, c],
                                              start=k == 0, stop=k == KC - 1)
                                last.then_inc(s["w_used"], 1)
                            pe.wait_ge(s["he"], n + 1)
                            for jj in range(2):
                                nc.tensor.transpose(pb[3][:, jj * P:(jj + 1) * P], act_g[0][:, jj * P:(jj + 1) * P],
                                                    ident[:, :])
                            for t in range(NT):
                                last = nc.tensor.transpose(pb[3][:, (2 + t) * P:(3 + t) * P],
                                                           pickg[:, t, :, :].rearrange("p e s -> p (e s)"), ident[:, :])
                            last.then_inc(s["t"], 1)
                            pe.wait_ge(s["ts"], n + 1)
                            for kk in range(FC):
                                pe.wait_ge(s["w_in"], (n * (KC + FC) + (KC + kk + 1)) * 16)
                                hf, jj = kk // 2, kk % 2
                                for c in range(2):
                                    last = mm(pb[2][c * 64:(c + 1) * 64, :],
                                              heT[:, jj * P + hf * 64:jj * P + (hf + 1) * 64],
                                              spill_w[:, c * HALF:(c + 1) * HALF], start=kk == 0, stop=kk == FC - 1)
                                last.then_inc(s["w_used"], 1)
                            pe.wait_ge(s["ys"], n + 1)
                            for t in range(NT):
                                for c in range(2):
                                    last = mm(pb[4 + 2 * t + c][:, :], back[0:SLOTS, t * P:(t + 1) * P],
                                              ye[0:SLOTS, c * HALF:(c + 1) * HALF], start=True, stop=True)
                            last.then_inc(s["z"], 1)
                            pe.wait_ge(s["zs"], n * 4 + (4 + START))
                    bcast_row(1, 2 * l + 1, 0)
                    bcast_row(0, 2 * l + 1, 1)
                    bcast_row(3, 4 + 2 * l + 1, 0)

            moe(0)

            pe.wait_ge(res_in, 1)
            stay_awake(4, 4)
            turn_h(3, 1, 0, 4)
            kvw, kvs, kvf = small_at(D_KV)
            kvw = kvw[:, :, :].rearrange("p a (b n) -> p (a b) n", b=2)
            for t in range(NT):
                wait_hT(3, t)
                for k in range(KC):
                    if t == 0 and k % 4 == 0:
                        pe.wait_ge(kvs[k // 4], 16 * kvf)
                    if t == 0 and k == 4:
                        turn_h(3, 1, 1, 4)
                    last = mm(pb[4 + t][:, :], hT[:, k, t * P:(t + 1) * P], kvw[:, k, :], start=k == 0, stop=k == KC - 1)
                last.then_inc(kv_done, 1)
            for c in range(2):
                project(G_MIX[1], 0, c, 2 + c, q_done)
            pe.wait_ge(k_rot, NT)
            for g in range(A_KV):
                for t in range(NT):
                    c = (g % 2) * SEQ + t * P
                    last = nc.tensor.transpose(pb[4 + g // 2][:, c:c + P],
                                               kdup[:, t, g, :, :].rearrange("p d n -> p (d n)"), ident[:, :])
                if g % 2:
                    last.then_inc(kT_done, 1)

            def turn_q(t):
                for jj in range(2):
                    pe.wait_ge(q_rotd, 2 * t + jj + 1)
                    if t:
                        pe.wait_ge(qT_sb, 4)
                    for n in range(4):
                        j = 4 * jj + n
                        last = nc.tensor.transpose(pb[6 + jj][:, n * P:(n + 1) * P], q_rot[t][:, j * P:(j + 1) * P],
                                                   ident[:, :])
                    last.then_inc(qT_done, 1)

            def score(t):
                pe.wait_ge(qT_sb, 4 * t + 4)
                for (tt, par, jj) in SC_ORDER:
                    if tt != t:
                        continue
                    b = SCB[t][par][jj]
                    for gg in range(2):
                        for ci in range(2):
                            g, c = 2 * jj + gg, 2 * t + ci
                            lo = max(0, c - 1) * CHUNK
                            hi = (c + 1) * CHUNK
                            end = (2 * gg + ci + 1) * P
                            last = mm(pb[b][:, end - (hi - lo):end],
                                      qT[par * 64:(par + 1) * 64, g, c, :, :].rearrange("p r q -> p (r q)"),
                                      kT[par * 64:(par + 1) * 64, g, lo:hi], start=True, stop=True)
                    last.then_inc(sc_done, 1)

            def turn_probs(n0):
                for n in (n0, n0 + 1):
                    t, par, jj = SC_ORDER[n]
                    pe.wait_ge(pn_ready, n + 1)
                    for s in range(4):
                        last = nc.tensor.transpose(pb[SCB[t][par][jj]][:, s * P:(s + 1) * P],
                                                   prob[n % 2][:, s * P:(s + 1) * P], ident[:, :])
                    last.then_inc(pT_done, 1)

            def attend(n0):
                pe.wait_ge(pT_sb, n0 + 2)
                for gg in range(2):
                    for ci in range(2):
                        for n in (n0, n0 + 1):
                            t, par, jj = SC_ORDER[n]
                            o = pb[SCB[t][0][jj]][par * 64:(par + 1) * 64, :].rearrange("p (s q) -> p s q", s=4)
                            vw = v_tok if ci else v_shift
                            g, slot = 2 * jj + gg, 2 * gg + ci
                            last = mm(o[:, 2 * gg:2 * gg + 2, ci * 64:(ci + 1) * 64], vw[:, t, g * DH:(g + 1) * DH],
                                      probT[n % 2][:, slot * P:(slot + 1) * P].rearrange("p (r q) -> p r q", r=2),
                                      start=True, stop=True)
                last.then_inc(pv_done, 1)

            def first_scores():
                turn_q(0)
                pe.wait_ge(kT_sb, 2)
                score(0)

            def second_scores():
                turn_q(1)
                score(1)

            pe.wait_ge(q_rotd, 1)
            project(G_MIX[1], 1, 0, 2, q_done, {4: first_scores})
            project(G_MIX[1], 1, 1, 3, q_done, {2: lambda: turn_probs(0), 4: lambda: attend(0),
                                                6: lambda: turn_probs(2)})
            attend(2)
            wo = G_MIX[1] + 1
            pe.wait_ge(outT_sb, 2)
            project(wo, 0, 0, 0, mix_done, {4: second_scores})
            project(wo, 0, 1, 1, mix_done, {2: lambda: turn_probs(4), 4: lambda: attend(4),
                                            6: lambda: turn_probs(6)})
            attend(6)
            ln_bcast(1, 0, 4, 6)
            pe.wait_ge(outT_sb, 4)
            project(wo, 1, 0, 2, mix_done)
            turn_h(4, 2, 0, 0)
            project(wo, 1, 1, 3, mix_done)
            moe(1)

        @block.scalar
        def _(act):
            A = nc.scalar.activation
            n_ach = [0]

            def link(ins):
                n_ach[0] += 1
                ins.then_inc(ach, 1)
                act.wait_ge(ach, n_ach[0])

            for first in (x_sb, silu_done):
                act.sem_inc(first, START)

            act.wait_ge(gate_zero, 2)
            for g in range(2):
                w4 = w_in_a[0, :, 3072 + g * M_HEADS:3072 + (g + 1) * M_HEADS]
                act.dma_start(w_gate[:, :, 32 * g:32 * g + M_HEADS], w4.rearrange("(k p) n -> p k n", p=P)).then_inc(gates_w_in, 16)
                act.dma_start(b_gate[32 * g:32 * g + M_HEADS, :],
                              b_gates_a[0, g * M_HEADS:(g + 1) * M_HEADS].rearrange("(h o) -> h o", o=1)).then_inc(gates_w_in, 16)
            def take_hT(n, t, bank0):
                for j in range(t, 2):
                    act.wait_ge(turned, 4 * n + 2 * t + j + 1)
                    A(hT[:, 4 * j:4 * j + 4, t * P:(t + 1) * P],
                      pb[bank0 + 2 * t + j][:, :].rearrange("p (k n) -> p k n", k=4), ACT.Copy).then_inc(hT_act, 1)

            def ln_std_part(n, t):
                act.wait_ge(ln_std_in, NT * n + t + 1)
                A(ln[:, t, 15:16], ln[:, t, 14:15], ACT.Sqrt).then_inc(ln_std, 1)

            for t in range(NT):
                take_hT(0, t, 4)
            act.dma_start(rows[0][0:4], ln_g.rearrange("l w n -> (l w) n")).then_inc(rows_in, 16)
            act.dma_start(rows[0][4:8], ln_b.rearrange("l w n -> (l w) n")).then_inc(rows_in, 16)
            act.dma_start(rows[0][8:9], mh_norm_a).then_inc(rows_in, 16)
            act.dma_start(w_rt[:, :, :], w_router.rearrange("(k p) n -> p k n", p=P)).then_inc(params_in, 16)
            act.dma_start(b_rt[:, :], b_router.rearrange("(a n) -> a n", a=1).to_broadcast([P, EXPERTS])).then_inc(params_in, 16)
            for r in range(2):
                act.dma_start(sink[64 * r:64 * r + 64, :].rearrange("p (g a) -> p g a", a=2),
                              sinks_b.rearrange("o (g r a) -> r o g a", r=2, a=2)[r].to_broadcast([64, A_KV, 2])
                              ).then_inc(params_in, 16)
            for a in range(2):
                act.dma_start(cs[:, :, a * 32:(a + 1) * 32], rope[a].rearrange("(t p) n -> p t n", p=P)).then_inc(params_in, 16)
            for g in range(8):
                act.wait_ge(qk_done, 2 * (g // 2) + 2)
                A(qkT[:, g, :], pb[g // 2][:, (g % 2) * SEQ:(g % 2 + 1) * SEQ], ACT.Copy,
                  scale=1.0 if g < 4 else float(M_QK) ** -0.5).then_inc(qk_sb, 1)
            act.wait_ge(gates_done, 1)
            act.wait_ge(d2a, 1)
            A(tanh_rows, pb[4][0:GW, 0:SEQ], ACT.Tanh, bias=b_gate[:, 0:1], scale=1.0 / CAP).then_inc(gates_read, 1)
            act.wait_ge(gates_read, 1)
            link(A(lane[2], tanh_rows[32:GW, :], ACT.Exp, scale=-CAP))
            A(lane[2], lane[2], ACT.Ln, bias=ones[0:M_HEADS, 0:1]).then_inc(a2d, 1)
            act.wait_ge(rows_ready, 1)
            for n, bank in enumerate((5, 6, 7, 4)):
                act.wait_ge(v_done, n + 1)
                A(val[:, n // 2, (n % 2) * HALF:(n % 2 + 1) * HALF], pb[bank][:, :], ACT.Copy).then_inc(v_sb, 1)
            act.wait_ge(d2a, 2)
            A(st[:, 8:16], st[:, 8:16], ACT.Exp).then_inc(a2d, 1)
            for hd in range(M_HEADS):
                act.wait_ge(w_arg, 2 * hd + 2)
                A(wts[:, hd, :], wts[:, hd, :], ACT.Exp).then_inc(w_exp, 1)

            def o_gate(n, bank):
                act.wait_ge(o_done, n + 1)
                A(gate_o[:, n // 2, (n % 2) * HALF:(n % 2 + 1) * HALF], pb[bank][:, :], ACT.Sigmoid).then_inc(o_sb, 1)
            act.wait_ge(s_done, M_HEADS)
            o_gate(0, 7)
            o_gate(1, 4)
            act.wait_ge(den_inv, 1)
            for hd in range(M_HEADS):
                act.wait_ge(num_done, hd + 1)
                for t in range(NT):
                    c = t * M_HEADS + hd
                    A(wts[:, hd, t * P:t * P + M_V], pb[hd][:, t * M_V:(t + 1) * M_V], ACT.Square,
                      scale=st[:, 16 + c:17 + c], accum_out=st[:, 24 + c:25 + c]).then_inc(sq_done, 1)
                    act.wait_ge(sq_done, hd * 2 + t + 1)
            act.wait_ge(rms_in, 1)
            A(st[:, 32:40], st[:, 32:40], ACT.Sqrt).then_inc(rms_std, 1)
            act.wait_ge(std_ready, 1)
            for t in range(NT):
                for hd in range(M_HEADS):
                    c = 40 + t * M_HEADS + hd
                    A(val[:, t, hd * M_V:(hd + 1) * M_V], pb[hd][:, t * M_V:(t + 1) * M_V], ACT.Copy,
                      scale=st[:, c:c + 1]).then_inc(num_sb, 1)
            o_gate(2, 5)
            take_hT(1, 0, 0)
            o_gate(3, 6)
            take_hT(1, 1, 0)
            ln_std_part(0, 0)
            take_hT(2, 0, 0)
            ln_std_part(0, 1)

            def moe(l):
                A(extra_f[:, 3:4], ones[:, 0:1], ACT.Exp)
                for t in range(NT):
                    if t:
                        take_hT(2 + 2 * l, t, 0)
                    act.wait_ge(lgT_done, NT * l + t + 1)
                    A(lgT[:, t * P:(t + 1) * P], pb[2 * t][0:EXPERTS, 0:P], ACT.Copy).then_inc(lgT_sb, 1)
                act.wait_ge(rt_exp_in, l + 1)
                A(r_logit, r_logit, ACT.Exp).then_inc(rt_exp, 1)

                def take_x(m, P0, half, bank=1):
                    act.wait_ge(x_got, (P0 + m) * 2 + (half + 1 - START))
                    A(xe[m % 2][:, 4 * half:4 * half + 4, :].rearrange("p k s -> p (k s)"), pb[bank][:, :], ACT.Copy
                      ).then_inc(x_sb, 1)

                def take_y(u, E0):
                    p = (u % 2) * 64
                    act.wait_ge(y_done, E0 + (u + 1))
                    A(ye[p:p + 64, HALF:2 * HALF], pb[2][64:128, :], ACT.Copy).then_inc(y_sb, 1)

                def silu(u, E0):
                    act.wait_ge(gu_done, E0 + (u + 1))
                    A(act_g[u % 2], pb[0][:, 0:256], ACT.Silu).then_inc(silu_done, 1)

                def one_turn(i, final):
                    E0 = EXPERTS * l + i * U + START
                    P0 = EXPERTS // 2 * l + i * 2 + START
                    for m in range(2):
                        over = final and m == 1
                        silu(2 * m + 1, E0)
                        take_y(2 * m, E0)
                        if not over:
                            take_x(m + 1, P0, 1)
                            silu(2 * m + 2, E0)
                            if not final:
                                take_x(m + 2, P0, 0)
                        take_y(2 * m + 1, E0)

                P1, E1 = EXPERTS // 2 * l + START, EXPERTS * l + START
                for half in range(2):
                    take_x(0, P1, half, bank=1 + 2 * half)
                silu(0, E1)
                take_x(1, P1, 0)
                with act.Fori(0, TURNS - 1) as i:
                    one_turn(i, False)
                one_turn(TURNS - 1, True)
                for t in range(NT):
                    for c in range(2):
                        act.wait_ge(mix_done, 4 * (2 * l + 1) + 2 * t + c + 1)
                        A(res[:, t, c * HALF:(c + 1) * HALF], pb[4 + 2 * t + c][:, :], ACT.Copy).then_inc(res_in, 1)
                s = ov[l]
                rounds = act.value_load(extra[0:1, 0:1], min_val=0, max_val=3)
                with act.If(rounds > 0):
                    with act.Fori(0, rounds) as j:
                        with act.Fori(0, EXPERTS) as e:
                            n = j * EXPERTS + e
                            for half in range(2):
                                act.wait_ge(s["x"], n * 2 + (half + 1))
                                A(xe[0][:, 4 * half:4 * half + 4, :].rearrange("p k s -> p (k s)"), pb[1][:, :], ACT.Copy
                                  ).then_inc(s["xs"], 1)
                            act.wait_ge(s["w_used"], n * (KC + FC) + (KC + START))
                            A(act_g[0], pb[0][:, 0:256], ACT.Silu).then_inc(s["silu"], 1)
                for t in range(NT):
                    ln_std_part(2 * l + 1, t)

            moe(0)

            for t in range(NT):
                take_hT(3, t, 4)
            act.wait_ge(shift_zero, 1)
            for t in range(NT):
                act.wait_ge(kv_done, t + 1)
                A(v_tok[:, t, :], pb[4 + t][:, KV_W:2 * KV_W], ACT.Copy)
                if t == 0:
                    A(v_shift[0:64, 1, :], pb[4][64:128, KV_W:2 * KV_W], ACT.Copy)
                A(v_shift[64:128, t, :], pb[4 + t][0:64, KV_W:2 * KV_W], ACT.Copy).then_inc(v_split, 1)
            for b in range(2):
                act.wait_ge(kT_done, b + 1)
                A(kT[:, 2 * b:2 * b + 2, :].rearrange("p g n -> p (g n)"), pb[4 + b][:, :], ACT.Copy).then_inc(kT_sb, 1)

            def take_qT(t):
                for jj in range(2):
                    act.wait_ge(qT_done, 2 * t + jj + 1)
                    for ci in range(2):
                        A(qT[:, 2 * jj:2 * jj + 2, 2 * t + ci, :, :],
                          pb[6 + jj][:, :].rearrange("p (g r c q) -> p g r c q", g=2, r=2, c=2)[:, :, :, ci, :],
                          ACT.Copy).then_inc(qT_sb, 1)

            def exps(n):
                t, par, jj = SC_ORDER[n]
                b = SCB[t][par][jj]
                act.wait_ge(mx_ready, n + 1)
                if n >= 2:
                    act.wait_ge(pT_done, n - 1)
                o = 20 * (n % 4)
                for s in range(4):
                    A(prob[n % 2][:, s * P:(s + 1) * P], pb[b][:, s * P:(s + 1) * P], ACT.Exp,
                      bias=st[:, o + 4 + s:o + 5 + s], scale=float(DH) ** -0.5, accum_out=st[:, o + 12 + s:o + 13 + s]
                      ).then_inc(e_done, 1)
                A(st[:, o + 8:o + 12], st[:, o + 8:o + 12], ACT.Exp).then_inc(e_done, 1)

            take_qT(0)
            for n in range(4):
                exps(n)
            take_qT(1)
            for n in range(4, 8):
                exps(n)
            ln_std_part(2, 0)
            take_hT(4, 0, 0)
            ln_std_part(2, 1)
            moe(1)

        @block.vector
        def _(dve):
            V = nc.vector
            n_dch = [0]

            def link(ins):
                n_dch[0] += 1
                ins.then_inc(dch, 1)
                dve.wait_ge(dch, n_dch[0])

            def take_hT(n, t, bank0):
                if t == 0:
                    return
                dve.wait_ge(turned, 4 * n + 2 * t + 1)
                V.tensor_copy(hT[:, 0:4, t * P:(t + 1) * P], pb[bank0 + 2 * t][:, :].rearrange("p (k n) -> p k n", k=4)
                              ).then_inc(hT_dve, 1)

            def ln_sum(n, t, src, bank0):
                for c in range(2):
                    dve.wait_ge(mix_done, 4 * n + 2 * t + c + 1)
                    cc = slice(c * HALF, (c + 1) * HALF)
                    link(V.scalar_tensor_tensor(out=src[:, t, cc], in0=h[:, t, cc], scalar=ALPHA,
                                                in1=pb[bank0 + 2 * t + c][:, :], op0=ALU.mult, op1=ALU.add))
                    link(V.bn_stats(ln[:, t, 6 * c:6 * c + 6], src[:, t, cc]))

            def ln_tile(n, t, src, g_banks, b_banks):
                link(V.bn_aggr(ln[:, t, 12:14], ln[:, t, 0:12]))
                V.tensor_scalar(ln[:, t, 14:15], ln[:, t, 13:14], LN_EPS, None, ALU.add).then_inc(ln_std_in, 1)
                dve.wait_ge(ln_rows, n + 1)
                for c in range(2):
                    cc = slice(c * HALF, (c + 1) * HALF)
                    V.scalar_tensor_tensor(out=src[:, t, cc], in0=src[:, t, cc], scalar=ln[:, t, 12:13],
                                           in1=pb[g_banks[c]][:, :], op0=ALU.subtract, op1=ALU.mult)
                dve.wait_ge(ln_std, NT * n + t + 1)
                link(V.reciprocal(ln[:, t, 16:17], ln[:, t, 15:16]))
                for c in range(2):
                    cc = slice(c * HALF, (c + 1) * HALF)
                    V.scalar_tensor_tensor(out=h[:, t, cc], in0=src[:, t, cc], scalar=ln[:, t, 16:17],
                                           in1=pb[b_banks[c]][:, :], op0=ALU.mult, op1=ALU.add).then_inc(ln_ready, 1)

            for first in (pick_ready, pickg_ready, he_ready, heT_sb, back_sb, y_sb, ov[0]["zs"], ov[1]["zs"]):
                dve.sem_inc(first, START)

            for t in range(NT):
                take_hT(0, t, 4)
            dve.wait_ge(gates_w_in, 64)
            V.tensor_scalar(b_gate[:, :], b_gate[:, :], 1.0 / CAP, None, ALU.mult).then_inc(d2a, 1)
            dve.wait_ge(a2d, 1)
            link(V.tensor_tensor_scan(out=lane[1], data0=ones[0:M_HEADS, 0:1].to_broadcast([M_HEADS, SEQ]),
                                      data1=lane[2], initial=0.0, op0=ALU.mult, op1=ALU.add))
            link(V.scalar_tensor_tensor(out=lane[3], in0=lane[0], scalar=CAP, in1=lane[1], op0=ALU.mult, op1=ALU.add))
            link(V.tensor_tensor_scan(out=lane[2], data0=lane[3], data1=lane[3], initial=0.0, op0=ALU.max, op1=ALU.max))
            V.tensor_scalar(lane[4], lane[2], -1.0, None, ALU.mult)
            V.tensor_tensor(lane[5], lane[1], lane[2], ALU.subtract).then_inc(lanes_ready, 1)
            dve.wait_ge(small_T, 1)
            link(V.tensor_copy(st[:, 0:8], pb[4][:, 0:8]))
            V.tensor_scalar(st[:, 8:16], pb[4][:, 8:16], 88.0, None, ALU.min).then_inc(d2a, 1)
            dve.wait_ge(d2a, 2)
            dve.sem_inc(small_sb, 1)
            dve.wait_ge(m_bcast, M_HEADS)
            for hd in range(M_HEADS):
                mb = pb[5 + hd // 2][:, (hd % 2) * SEQ:(hd % 2 + 1) * SEQ]
                V.tensor_scalar(wts[:, hd, 0:SEQ], mb, st[:, hd:hd + 1], 0.0, ALU.add, ALU.min).then_inc(w_arg, 1)
                V.tensor_scalar(wts[:, hd, SEQ:SEQ + P], mb[:, P:SEQ], st[:, 4 + hd:5 + hd], 0.0, ALU.add, ALU.min
                                ).then_inc(w_arg, 1)
            for hd in range(M_HEADS):
                dve.wait_ge(s_done, hd + 1)
                dve.wait_ge(w_masked, 2 * hd + 2)
                V.tensor_tensor(wts[:, hd, :], wts[:, hd, :], pb[hd][:, 0:SEQ + P], ALU.mult).then_inc(p_ready, 1)
            dve.wait_ge(den_done, 1)
            dve.wait_ge(a2d, 2)
            link(V.tensor_copy(st[:, 32:40], pb[7][:, 0:8]))
            link(V.scalar_tensor_tensor(out=st[:, 40:48], in0=st[:, 32:40], scalar=-1.0, in1=st[:, 32:40],
                                        op0=ALU.mult, op1=ALU.max))
            link(V.tensor_tensor(st[:, 40:48], st[:, 40:48], st[:, 8:16], ALU.max))
            V.reciprocal(st[:, 16:24], st[:, 40:48]).then_inc(den_inv, 1)
            dve.wait_ge(sq_done, 8)
            V.tensor_scalar(st[:, 32:40], st[:, 24:32], 1.0 / M_V, MH_EPS, ALU.mult, ALU.add).then_inc(rms_in, 1)
            dve.wait_ge(rms_std, 1)
            link(V.reciprocal(st[:, 40:48], st[:, 32:40]))
            V.tensor_tensor(st[:, 40:48], st[:, 40:48], st[:, 16:24], ALU.mult).then_inc(std_ready, 1)
            dve.wait_ge(mh_bcast, 1)
            for t in range(NT):
                for c, bank in ((0, 7), (1, 4)):
                    cc = slice(c * HALF, (c + 1) * HALF)
                    dve.wait_ge(o_sb, 2 * t + c + 1)
                    dve.wait_ge(num_sb, M_HEADS * (t + 1))
                    link(V.tensor_tensor(gate_o[:, t, cc], gate_o[:, t, cc], pb[bank][:, :], ALU.mult))
                    ins = V.tensor_tensor(val[:, t, cc], val[:, t, cc], gate_o[:, t, cc], ALU.mult)
                ins.then_inc(gated, 1)
                take_hT(1, t, 0)
            for t in range(NT):
                ln_sum(0, t, h, 0)
                ln_tile(0, t, h, (4, 5), (6, 7))
                take_hT(2, t, 0)

            def route(l):
                def b3(ap, n):
                    return ap.rearrange("p (t o) -> p t o", o=1).to_broadcast([P, NT, n])
                lg = r_logit.rearrange("p (t e) -> p t e", t=NT)
                dve.wait_ge(logits, l + 1)
                dve.wait_ge(params_in, 16 * 6)
                link(V.reduce_max(r_s[:, 0:2], pb[1][:, 0:32].rearrange("p (t e) -> p t e", t=NT), AX_X))
                V.tensor_tensor(lg, pb[1][:, 0:32].rearrange("p (t e) -> p t e", t=NT), b3(r_s[:, 0:2], 16),
                                ALU.subtract).then_inc(rt_exp_in, 1)
                dve.wait_ge(rt_exp, l + 1)
                link(V.reduce_sum(r_s[:, 2:4], lg, AX_X))
                link(V.reciprocal(r_s[:, 4:6], r_s[:, 2:4]))
                link(V.tensor_tensor(r_prob, lg, b3(r_s[:, 4:6], 16), ALU.mult))
                link(V.tensor_tensor(r_sel, r_prob, b_rt[:, :].rearrange("p (o e) -> p o e", o=1).to_broadcast([P, NT, 16]), ALU.add))
                s4 = st[:, 64:96].rearrange("p (q a b) -> p q a b", a=2, b=2)
                hi = r_logit[:, 0:16].rearrange("p (q a) -> p q a", a=2)
                lo = r_logit[:, 16:32].rearrange("p (q a) -> p q a", a=2)
                V.tensor_tensor(hi, s4[:, :, :, 0], s4[:, :, :, 1], ALU.max)
                link(V.tensor_tensor(lo, s4[:, :, :, 0], s4[:, :, :, 1], ALU.min))
                V.tensor_tensor(r_s[:, 0:8], hi[:, :, 0], hi[:, :, 1], ALU.max)
                V.tensor_tensor(r_s[:, 8:16], hi[:, :, 0], hi[:, :, 1], ALU.min)
                link(V.tensor_tensor(r_s[:, 16:24], lo[:, :, 0], lo[:, :, 1], ALU.max))
                link(V.tensor_tensor(r_s[:, 8:16], r_s[:, 8:16], r_s[:, 16:24], ALU.max))
                link(V.tensor_tensor(r_s[:, 0:8], r_s[:, 0:8], r_s[:, 8:16], ALU.add))
                gs = r_s[:, 0:8].rearrange("p (t g) -> p t g", t=NT)

                def first_best(vals, n, rank, key, m, res_):
                    link(V.reduce_max(m, vals, AX_X))
                    link(V.tensor_tensor(key, vals, b3(m, n), ALU.is_equal))
                    link(V.tensor_tensor(key, key, rank[:, :].rearrange("p (o e) -> p o e", o=1).to_broadcast([P, NT, n]), ALU.mult))
                    link(V.reduce_max(m, key, AX_X))
                    link(V.tensor_tensor(res_, key, b3(m, n), ALU.is_equal))
                gm = r_s[:, 8:16].rearrange("p (t g) -> p t g", t=NT)
                first_best(gs, 4, rank4, r_s[:, 16:24].rearrange("p (t g) -> p t g", t=NT), r_s[:, 24:26], gm)
                link(V.tensor_scalar(r_s[:, 16:24], r_s[:, 8:16], 1.0, -LOW, ALU.subtract, ALU.mult))
                q4 = lambda ap: ap.rearrange("p (q a) -> p q a", a=4)
                b4 = lambda ap: ap.rearrange("p (q o) -> p q o", o=1).to_broadcast([P, 8, 4])
                link(V.tensor_tensor(q4(r_logit), q4(st[:, 64:96]), b4(r_s[:, 8:16]), ALU.mult))
                link(V.tensor_tensor(q4(r_logit), q4(r_logit), b4(r_s[:, 16:24]), ALU.add))
                first_best(lg, 16, rank16, r_a, r_s[:, 24:26], oh1)
                link(V.scalar_tensor_tensor(out=r_logit, in0=ro[:, 0, :], scalar=3.0 * LOW, in1=r_logit, op0=ALU.mult, op1=ALU.add))
                first_best(lg, 16, rank16, r_a, r_s[:, 24:26], oh2)
                V.tensor_tensor(oh, oh1, oh2, ALU.add).then_inc(chosen, 1)
                dve.wait_ge(chosen, l + 1)
                link(V.tensor_tensor(r_a, oh, r_prob, ALU.mult))
                link(V.reduce_sum(r_s[:, 0:2], r_a, AX_X))
                link(V.reciprocal(r_s[:, 2:4], r_s[:, 0:2]))
                link(V.tensor_tensor(gate[:, :, :].rearrange("p e t -> p t e"), r_a, b3(r_s[:, 2:4], 16), ALU.mult))
                dve.wait_ge(placed, l + 1)
                pt = pos[:, :, :].rearrange("p e t -> p t e")
                link(V.tensor_tensor(r_a, pb[1][:, 0:32].rearrange("p (t e) -> p t e", t=NT), oh, ALU.mult))
                V.reduce_max(extra_f[:, 0:1], pb[1][:, 32:48], AX_X)
                link(V.tensor_scalar(pt, r_a, 1.0, None, ALU.subtract))

            def count_rounds(l):
                link(V.tensor_scalar(extra_f[:, 1:2], extra_f[:, 0:1], float(USED), None, ALU.is_gt))
                for r in range(2, SEQ // USED if USED == 64 else 4):
                    link(V.tensor_scalar(extra_f[:, 2:3], extra_f[:, 0:1], float(r * USED), None, ALU.is_gt))
                    link(V.tensor_tensor(extra_f[:, 1:2], extra_f[:, 1:2], extra_f[:, 2:3], ALU.add))
                V.tensor_copy(extra[:, :], extra_f[:, 1:2]).then_inc(lists, 1)

            def make_pick(dst, e):
                pt = pos[:, bass.ds(e, 2), :].rearrange("p e t -> p t e").rearrange("p t (e o) -> p t e o", o=1)
                return V.tensor_tensor(dst, slot_no[:, :].rearrange("p (t e s) -> p t e s", t=1, e=1).to_broadcast([P, NT, 2, SLOTS]),
                                       pt.to_broadcast([P, NT, 2, SLOTS]), ALU.is_equal)

            def make_pickg(src, e):
                gt = gate[:, bass.ds(e, 2), :].rearrange("p e t -> p t e").rearrange("p t (e o) -> p t e o", o=1)
                return V.tensor_tensor(pickg, src, gt.to_broadcast([P, NT, 2, SLOTS]), ALU.mult)

            def experts(l):
                def one_turn(i, final):
                    E0 = EXPERTS * l + i * U + START
                    P0 = EXPERTS // 2 * l + i * 2 + START

                    for m in range(2):
                        a, b = 2 * m, 2 * m + 1
                        dve.wait_ge(pick_ready, P0 + (m + 1))
                        make_pickg(pick[m % 2], i * U + 2 * m).then_inc(pickg_ready, 1)
                        if not final:
                            dve.wait_ge(x_got, (P0 + m) * 2 + (2 - START))
                            dve.wait_ge(pickg_ready, P0 + (m + 1))
                            make_pick(pick[m % 2], i * U + (2 * m + 4)).then_inc(pick_ready, 1)
                        times_up(b, E0)
                        take_T(a, E0)
                        take_y(a, E0)
                        if not (final and m == 1):
                            times_up(b + 1, E0)
                        take_T(b, E0)
                        take_y(b, E0)

                def times_up(u, E0):
                    dve.wait_ge(silu_done, E0 + (u + 1))
                    V.tensor_tensor(act_g[u % 2], act_g[u % 2], pb[0][:, 256:512], ALU.mult).then_inc(he_ready, 1)

                def take_T(u, E0):
                    dve.wait_ge(heT_done, E0 + (u + 1))
                    V.tensor_copy(heT, pb[3][:, 0:2 * P]).then_inc(heT_sb, 1)
                    if u % 2:
                        V.tensor_copy(back, pb[3][:, 2 * P:4 * P]).then_inc(back_sb, 1)

                def take_y(u, E0):
                    p = (u % 2) * 64
                    dve.wait_ge(y_done, E0 + (u + 1))
                    V.tensor_copy(ye[p:p + 64, 0:HALF], pb[2][0:64, :]).then_inc(y_sb, 1)

                for m in range(2):
                    make_pick(pick[m], 2 * m).then_inc(pick_ready, 1)
                count_rounds(l)
                dve.wait_ge(lists, l + 1)
                rounds = dve.value_load(extra[0:1, 0:1], min_val=0, max_val=3)
                times_up(0, EXPERTS * l + START)
                with dve.Fori(0, TURNS - 1) as i:
                    one_turn(i, False)
                one_turn(TURNS - 1, True)
                return rounds

            def make_pick1(e):
                return V.tensor_tensor(pick[0], slot_no[:, :].rearrange("p (t e s) -> p t e s", t=1, e=1).to_broadcast([P, NT, 2, SLOTS]),
                                       pos[:, bass.ds(e, 1), :].rearrange("p e t -> p t e").rearrange("p t (e o) -> p t e o", o=1)
                                       .to_broadcast([P, NT, 2, SLOTS]), ALU.is_equal)

            def make_pickg1(e):
                return V.tensor_tensor(pickg, pick[0], gate[:, bass.ds(e, 1), :].rearrange("p e t -> p t e")
                                       .rearrange("p t (e o) -> p t e o", o=1).to_broadcast([P, NT, 2, SLOTS]), ALU.mult)

            def overflow(l, rounds):
                s = ov[l]
                with dve.If(rounds > 0):
                    with dve.Fori(0, rounds) as j:
                        V.tensor_scalar(pos[:, :, :], pos[:, :, :], float(USED), None, ALU.subtract).then_inc(s["dve"], 1)
                        with dve.Fori(0, EXPERTS) as e:
                            n = j * EXPERTS + e

                            dve.wait_ge(s["dve"], n + j + 1)
                            make_pick1(e).then_inc(s["dve"], 1)
                            dve.wait_ge(s["dve"], n + j + 2)
                            make_pickg1(e).then_inc(s["pick"], 1)
                            dve.wait_ge(s["silu"], n + 1)
                            V.tensor_tensor(act_g[0], act_g[0], pb[0][:, 256:512], ALU.mult).then_inc(s["he"], 1)
                            dve.wait_ge(s["t"], n + 1)
                            V.tensor_copy(heT, pb[3][:, 0:2 * P])
                            V.tensor_copy(back, pb[3][:, 2 * P:4 * P]).then_inc(s["ts"], 1)
                            dve.wait_ge(s["w_used"], n * (KC + FC) + (KC + FC + START))
                            V.tensor_copy(ye[0:64, 0:HALF], pb[2][0:64, :])
                            V.tensor_copy(ye[0:64, HALF:2 * HALF], pb[2][64:128, :]).then_inc(s["ys"], 1)
                            dve.wait_ge(s["z"], n + 1)
                            dve.wait_ge(s["zs"], n * 4 + START)
                            for t in range(NT):
                                for c in range(2):
                                    cc = slice(c * HALF, (c + 1) * HALF)
                                    V.tensor_tensor(res[:, t, cc], res[:, t, cc], pb[4 + 2 * t + c][:, :], ALU.add
                                                    ).then_inc(s["zs"], 1)
                    dve.wait_ge(s["zs"], rounds * (EXPERTS * 4) + START)
                    for t in range(NT):
                        for c in range(2):
                            last = V.bn_stats(ln[:, t, 6 * c:6 * c + 6], res[:, t, c * HALF:(c + 1) * HALF])
                    last.then_inc(s["dve"], 1)
                    dve.wait_ge(s["dve"], rounds * (EXPERTS + 1) + 1)
                    V.tensor_copy(extra_f[:, 3:4], extra_f[:, 1:2])

            def moe(l):
                route(l)
                rounds = experts(l)
                for t in range(NT):
                    for c in range(2):
                        dve.wait_ge(res_in, 4 * l + 2 * t + c + 1)
                        link(V.bn_stats(ln[:, t, 6 * c:6 * c + 6], res[:, t, c * HALF:(c + 1) * HALF]))
                overflow(l, rounds)
                for t in range(NT):
                    ln_tile(2 * l + 1, t, res, (1, 0), (3, 2))

            moe(0)

            for t in range(NT):
                take_hT(3, t, 4)

            def rotate(dst1, dst2, src, t, nh):
                c = cs[:, t, 0:32].rearrange("p (o n) -> p o n", o=1).to_broadcast([P, nh, 32])
                s = cs[:, t, 32:64].rearrange("p (o n) -> p o n", o=1).to_broadcast([P, nh, 32])
                x1, x2 = src[:, :, 0:32], src[:, :, 32:64]
                V.tensor_tensor(dst1, x1, c, ALU.mult)
                link(V.tensor_tensor(dst2, x2, c, ALU.mult))
                V.tensor_tensor(x1, x1, s, ALU.mult)
                link(V.tensor_tensor(x2, x2, s, ALU.mult))
                V.tensor_tensor(dst1, dst1, x2, ALU.subtract)
                return V.tensor_tensor(dst2, dst2, x1, ALU.add)

            V.memset(v_shift[:, :, :], 0.0).then_inc(shift_zero, 1)
            for t in range(NT):
                dve.wait_ge(v_split, t + 1)
                link(rotate(kdup[:, t, :, 0, 0:32], kdup[:, t, :, 0, 32:64],
                            pb[4 + t][:, 0:KV_W].rearrange("p (g n) -> p g n", g=A_KV), t, A_KV))
                V.tensor_copy(kdup[:, t, :, 1, :], kdup[:, t, :, 0, :]).then_inc(k_rot, 1)

            def rotate_q(t, c):
                dve.wait_ge(q_done, 2 * t + c + 1)
                qd = q_rot[t][:, c * HALF:(c + 1) * HALF].rearrange("p (h n) -> p h n", n=DH)
                rotate(qd[:, :, 0:32], qd[:, :, 32:64], pb[2 + c][:, :].rearrange("p (h n) -> p h n", n=DH), t, 8
                       ).then_inc(q_rotd, 1)
            inv = float(DH) ** -0.5

            def soft_in(n):
                t, par, jj = SC_ORDER[n]
                b = SCB[t][par][jj]
                o = 20 * (n % 4)
                sk = sink[:, :].rearrange("p (g a) -> p g a", a=2)[:, 2 * jj:2 * jj + 2, par:par + 1].to_broadcast([P, 2, 2])
                gc = lambda i: st[:, o + i:o + i + 4].rearrange("p (g c) -> p g c", g=2)
                dve.wait_ge(sc_done, n + 1)
                pr = pb[b][:, :].rearrange("p (s k) -> p s k", s=4)
                if t == 0:
                    link(V.memset(pb[b][:, :].rearrange("p (g c k) -> p g c k", g=2, c=2)[:, :, 0, 0:64], LOW))
                link(V.reduce_max(st[:, o:o + 4], pr, AX_X))
                link(V.scalar_tensor_tensor(out=gc(0), in0=gc(0), scalar=inv, in1=sk, op0=ALU.mult, op1=ALU.max))
                V.tensor_scalar(st[:, o + 4:o + 8], st[:, o:o + 4], -1.0, None, ALU.mult)
                V.tensor_tensor(gc(8), sk, gc(0), ALU.subtract).then_inc(mx_ready, 1)

            def soft_out(n):
                o = 20 * (n % 4)
                dve.wait_ge(e_done, 5 * (n + 1))
                link(V.tensor_tensor(st[:, o:o + 4], st[:, o + 8:o + 12], st[:, o + 12:o + 16], ALU.add))
                V.reciprocal(st[:, o + 16:o + 20], st[:, o:o + 4]).then_inc(inv_ready, 1)

            def soft_T(n):
                t, par, jj = SC_ORDER[n]
                dve.wait_ge(pT_done, n + 1)
                V.tensor_copy(probT[n % 2], pb[SCB[t][par][jj]][:, :]).then_inc(pT_sb, 1)

            def take_out(n):
                t, _, jj = SC_ORDER[n]
                dve.wait_ge(pv_done, (n + 1) // 2)
                V.tensor_copy(hT[:, 4 * jj:4 * jj + 4, t * P:(t + 1) * P],
                              pb[SCB[t][0][jj]][:, :].rearrange("p (j n) -> p j n", j=4)).then_inc(outT_sb, 1)

            for c in range(2):
                rotate_q(0, c)
            for n0 in (0, 4):
                for n in range(n0, n0 + 4):
                    soft_in(n)
                for nn in (n0, n0 + 2):
                    soft_out(nn)
                    soft_out(nn + 1)
                    soft_T(nn)
                    soft_T(nn + 1)
                    if n0 == 0 and nn == 0:
                        rotate_q(1, 0)
                    take_out(nn + 1)
                    if n0 == 0 and nn == 2:
                        rotate_q(1, 1)
            for t in range(NT):
                ln_sum(2, t, h, 0)
                ln_tile(2, t, h, (4, 5), (6, 7))
                take_hT(4, t, 0)
            moe(1)


_INS = ['x', 'w_in_a', 'b_gates_a', 'mh_norm_a', 'w_out_a', 'w_kv_shared', 'w_q_b', 'sinks_b', 'w_out_b',
        'w_router', 'b_router', 'w_gu', 'w_down', 'ln_g', 'ln_b']


def kernel(**inputs):
    import numpy as _np
    import concourse.bacc as _bacc
    from concourse import mybir as _mybir
    from concourse.bass_utils import run_bass_kernel_spmd as _run

    nc = _bacc.Bacc("TRN2", target_bir_lowering=False, num_devices=1)
    arrays, args = {}, []
    for name in _INS:
        a = _np.ascontiguousarray(inputs[name])
        arrays[f"in_{name}"] = a
        args.append(nc.dram_tensor(f"in_{name}", a.shape, _mybir.dt.from_np(a.dtype), kind="ExternalInput").ap())
    freq = _np.float32(10000.0) ** (-_np.arange(0, DH, 2, dtype=_np.float32) / _np.float32(DH))
    ang = _np.arange(SEQ, dtype=_np.float32)[:, None] * freq[None, :]
    table = _np.stack([_np.cos(ang), _np.sin(ang)]).astype(_np.float32)
    arrays["rope"] = table
    args.append(nc.dram_tensor("rope", table.shape, F32, kind="ExternalInput").ap())
    args.append(nc.dram_tensor("out_0", (1, SEQ, D), F32, kind="ExternalOutput").ap())
    build(nc, *args)
    r = _run(nc, [arrays], core_ids=[0])
    return r.results[0]["out_0"]
```
